# Optimizing a Trainium2 kernel written in Bass

```python
import jax, jax.numpy as jnp
from jax import lax
import numpy as np

D_MODEL = 1024
BATCH = 1
SEQ = 256
DEPTH = 1
DEC_BATCH = 8
DEC_SEQ = 1
PAST_LEN = 2048
PAGE_SIZE = 128

D_MIX = D_MODEL
D_GMLP = D_MIX // 2
D_LRU = D_MIX - D_GMLP
GMLP_GROUPS = 4
GMLP_GROUP_DIM = D_GMLP // GMLP_GROUPS
CHUNK = 128
LRU_HEADS = 8
LRU_HEAD_DIM = D_LRU // LRU_HEADS
CONV_W = 4
LRU_C = 8.0
N_EXPERTS = 32
TOP_K = 4
D_FF_EXPERT = D_MODEL
SWIGLU_LIMIT = 7.0
SWIGLU_ALPHA = 1.702
PLE_DIM = 256
EPS = 1e-6
D_IN = 2 * D_GMLP + 2 * D_LRU

kernel_name = "hymba_gmlp_rglru_moe_decode_step"

F32 = jnp.float32

def rmsnorm(x, g):
    xf = x.astype(F32)
    y = xf * lax.rsqrt(jnp.mean(xf * xf, axis=-1, keepdims=True) + EPS)
    return (y * g.astype(F32)).astype(x.dtype)

def group_rmsnorm(x, g, n_groups):
    shp = x.shape
    xf = x.astype(F32).reshape(shp[:-1] + (n_groups, shp[-1] // n_groups))
    y = xf * lax.rsqrt(jnp.mean(xf * xf, axis=-1, keepdims=True) + EPS)
    return (y.reshape(shp) * g.astype(F32)).astype(x.dtype)

def gmlp_mixer(u, v, w_s, b_s, g_v):
    B, T, _ = v.shape
    cl = min(T, CHUNK)
    nc = T // cl
    v = group_rmsnorm(v, g_v, GMLP_GROUPS)
    mask = jnp.tril(jnp.ones((cl, cl), dtype=bool))
    w = jnp.where(mask, w_s[:, :cl, :cl], 0).astype(v.dtype)
    vc = v.reshape(B, nc, cl, GMLP_GROUPS, GMLP_GROUP_DIM)
    s = jnp.einsum('gts,bnsgd->bntgd', w, vc) + b_s[:, :cl].T[:, :, None].astype(v.dtype)
    y = u * s.reshape(B, T, D_GMLP)
    return y, v[:, T - cl:]

def causal_conv(x, buf, w, b):
    T = x.shape[1]
    xp = jnp.concatenate([buf.astype(x.dtype), x], axis=1)
    y = b.astype(x.dtype)
    for k in range(CONV_W):
        y = y + xp[:, k:k + T] * w[k]
    return y, xp[:, -(CONV_W - 1):]

def rglru(x, h0, w_a, b_a, w_x, b_x, lam, reset_first):
    B, T, C = x.shape
    xf = x.astype(F32)
    xh = xf.reshape(B, T, LRU_HEADS, LRU_HEAD_DIM)
    r = jax.nn.sigmoid(jnp.einsum('bthi,hij->bthj', xh, w_a.astype(F32)) + b_a.astype(F32)).reshape(B, T, C)
    i = jax.nn.sigmoid(jnp.einsum('bthi,hij->bthj', xh, w_x.astype(F32)) + b_x.astype(F32)).reshape(B, T, C)
    log_a = -LRU_C * r * jax.nn.softplus(-lam.astype(F32))
    a = jnp.exp(log_a)
    mult = jnp.sqrt(-jnp.expm1(2.0 * log_a))
    if reset_first:
        mult = mult.at[:, 0].set(1.0)
    bx = mult * i * xf

    def step(h, ab):
        a_t, b_t = ab
        h = a_t * h + b_t
        return h, h

    hT, hs = lax.scan(step, h0.astype(F32), (jnp.swapaxes(a, 0, 1), jnp.swapaxes(bx, 0, 1)))
    return jnp.swapaxes(hs, 0, 1).astype(x.dtype), hT.astype(h0.dtype)

def moe(x, w_r, b_r, w1, b1, w2, b2):
    B, T, D = x.shape
    xt = x.reshape(B * T, D)
    logits = xt.astype(F32) @ w_r.astype(F32) + b_r.astype(F32)
    top_v, top_i = lax.top_k(logits, TOP_K)
    gw = jax.nn.softmax(top_v, axis=-1)
    combine = jnp.sum(jax.nn.one_hot(top_i, N_EXPERTS, dtype=F32) * gw[..., None], axis=1).astype(x.dtype)
    out = jnp.zeros_like(xt)
    for e in range(N_EXPERTS):
        hdn = xt @ w1[e] + b1[e]
        gate = jnp.minimum(hdn[:, :D_FF_EXPERT], SWIGLU_LIMIT)
        up = jnp.clip(hdn[:, D_FF_EXPERT:], -SWIGLU_LIMIT, SWIGLU_LIMIT)
        act = (up + 1.0) * gate * jax.nn.sigmoid(SWIGLU_ALPHA * gate)
        out = out + combine[:, e:e + 1] * (act @ w2[e] + b2[e])
    return out.reshape(B, T, D)

def trunk(x, p, conv_bufs, lru_states, reset_first,
          g_mix, w_in, g_v, w_s, b_s, conv_w, conv_b, w_a, b_a, w_x, b_x, lam,
          g_oa, g_ob, w_out, g_ffn, w_r, b_r, w1, b1, w2, b2, g_ple, w_pg, b_pg, w_pp, g_final):
    h = x
    new_v, new_conv, new_lru = [], [], []
    for l in range(DEPTH):
        n = rmsnorm(h, g_mix[l])
        z = n @ w_in[l]
        u_a, v_a, x_b, g_b = jnp.split(z, [D_GMLP, 2 * D_GMLP, 2 * D_GMLP + D_LRU], axis=-1)
        y_a, v_rows = gmlp_mixer(jax.nn.gelu(u_a), jax.nn.gelu(v_a), w_s[l], b_s[l], g_v[l])
        xc, buf = causal_conv(x_b, conv_bufs[l], conv_w[l], conv_b[l])
        hs, hT = rglru(xc, lru_states[l], w_a[l], b_a[l], w_x[l], b_x[l], lam[l], reset_first)
        y_b = hs * jax.nn.gelu(g_b)
        y = jnp.concatenate([group_rmsnorm(y_a, g_oa[l], GMLP_GROUPS),
                             group_rmsnorm(y_b, g_ob[l], LRU_HEADS)], axis=-1)
        h = h + y @ w_out[l]
        h = h + moe(rmsnorm(h, g_ffn[l]), w_r[l], b_r[l], w1[l], b1[l], w2[l], b2[l])
        gate = jax.nn.sigmoid(rmsnorm(h, g_ple[l]) @ w_pg[l] + b_pg[l])
        h = h + gate * (p[l] @ w_pp[l])
        new_v.append(v_rows)
        new_conv.append(buf)
        new_lru.append(hT)
    return rmsnorm(h, g_final), jnp.stack(new_v), jnp.stack(new_conv), jnp.stack(new_lru)

def setup_inputs(seed: int = 0) -> dict:
    key = jax.random.key(seed)
    ks = iter(jax.random.split(key, 40))
    nrm = lambda shape, s=1.0: jax.random.normal(next(ks), shape, F32) * s
    gain = lambda shape: 1.0 + nrm(shape, 0.05)
    u = jax.random.uniform(next(ks), (DEPTH, D_LRU), F32, 0.9, 0.999)
    s_root = u ** (1.0 / LRU_C)
    lam = jnp.log(s_root) - jnp.log1p(-s_root)
    return {
        "x_prompt": nrm((BATCH, SEQ, D_MODEL)),
        "x_sample": nrm((DEC_BATCH, DEC_SEQ, D_MODEL)),
        "state_conv": nrm((DEPTH, DEC_BATCH, CONV_W - 1, D_LRU)),
        "state_lru": nrm((DEPTH, DEC_BATCH, D_LRU), 0.5),
        "p_prompt": nrm((DEPTH, BATCH, SEQ, PLE_DIM)),
        "p_sample": nrm((DEPTH, DEC_BATCH, DEC_SEQ, PLE_DIM)),
        "g_mix": gain((DEPTH, D_MODEL)),
        "w_in": nrm((DEPTH, D_MODEL, D_IN), D_MODEL ** -0.5),
        "g_v": gain((DEPTH, D_GMLP)),
        "w_s": nrm((DEPTH, GMLP_GROUPS, CHUNK, CHUNK), 0.5 * CHUNK ** -0.5),
        "b_s": 1.0 + nrm((DEPTH, GMLP_GROUPS, CHUNK), 0.1),
        "conv_w": nrm((DEPTH, CONV_W, D_LRU), CONV_W ** -0.5),
        "conv_b": nrm((DEPTH, D_LRU), 0.01),
        "w_a": nrm((DEPTH, LRU_HEADS, LRU_HEAD_DIM, LRU_HEAD_DIM), LRU_HEAD_DIM ** -0.5),
        "b_a": nrm((DEPTH, LRU_HEADS, LRU_HEAD_DIM), 0.01),
        "w_x": nrm((DEPTH, LRU_HEADS, LRU_HEAD_DIM, LRU_HEAD_DIM), LRU_HEAD_DIM ** -0.5),
        "b_x": nrm((DEPTH, LRU_HEADS, LRU_HEAD_DIM), 0.01),
        "lam": lam,
        "g_oa": gain((DEPTH, D_GMLP)),
        "g_ob": gain((DEPTH, D_LRU)),
        "w_out": nrm((DEPTH, D_MIX, D_MODEL), D_MIX ** -0.5),
        "g_ffn": gain((DEPTH, D_MODEL)),
        "w_r": nrm((DEPTH, D_MODEL, N_EXPERTS), D_MODEL ** -0.5),
        "b_r": nrm((DEPTH, N_EXPERTS), 0.01),
        "w1": nrm((DEPTH, N_EXPERTS, D_MODEL, 2 * D_FF_EXPERT), D_MODEL ** -0.5),
        "b1": nrm((DEPTH, N_EXPERTS, 2 * D_FF_EXPERT), 0.01),
        "w2": nrm((DEPTH, N_EXPERTS, D_FF_EXPERT, D_MODEL), D_FF_EXPERT ** -0.5),
        "b2": nrm((DEPTH, N_EXPERTS, D_MODEL), 0.01),
        "g_ple": gain((DEPTH, D_MODEL)),
        "w_pg": nrm((DEPTH, D_MODEL, D_MODEL), D_MODEL ** -0.5),
        "b_pg": nrm((DEPTH, D_MODEL), 0.01),
        "w_pp": nrm((DEPTH, PLE_DIM, D_MODEL), PLE_DIM ** -0.5),
        "g_final": gain((D_MODEL,)),
    }

def reference(x_prompt, x_sample, state_conv, state_lru, p_prompt, p_sample,
              g_mix, w_in, g_v, w_s, b_s, conv_w, conv_b, w_a, b_a, w_x, b_x, lam,
              g_oa, g_ob, w_out, g_ffn, w_r, b_r, w1, b1, w2, b2, g_ple, w_pg, b_pg, w_pp, g_final):
    weights = (g_mix, w_in, g_v, w_s, b_s, conv_w, conv_b, w_a, b_a, w_x, b_x, lam,
               g_oa, g_ob, w_out, g_ffn, w_r, b_r, w1, b1, w2, b2, g_ple, w_pg, b_pg, w_pp, g_final)
    bp = x_prompt.shape[0]
    conv0 = jnp.zeros((DEPTH, bp, CONV_W - 1, D_LRU), x_prompt.dtype)
    lru0 = jnp.zeros((DEPTH, bp, D_LRU), state_lru.dtype)
    y_prompt, v_prompt, conv_prompt, lru_prompt = trunk(x_prompt, p_prompt, conv0, lru0, True, *weights)
    y_sample, v_sample, conv_sample, lru_sample = trunk(x_sample, p_sample, state_conv, state_lru, False, *weights)
    return (y_prompt, y_sample, v_prompt, conv_prompt, lru_prompt, v_sample, conv_sample, lru_sample)


_drawn_inputs = setup_inputs


def setup_inputs(seed=0):
    import zlib

    import numpy as np

    out = dict(_drawn_inputs(seed))
    spreads = {}
    factors = {'b_a': 21.362,
     'b_x': 5.457,
     'b_r': 2.996,
     'b1': 8.0,
     'b2': 8.0,
     'g_ple': 8.0,
     'b_pg': 64.0}
    for name, (base, spread) in spreads.items():
        noise = np.random.default_rng([zlib.crc32(name.encode()), seed]).standard_normal(out[name].shape)
        drawn = base * np.exp(spread * noise) if base else spread * noise
        out[name] = __import__('jax').numpy.asarray(drawn.astype(out[name].dtype))
    for name, factor in factors.items():
        out[name] = (out[name] * factor).astype(out[name].dtype)
    return out
```

```python
from contextlib import ExitStack

import concourse.bass as bass
from concourse import mybir

ALU = mybir.AluOpType
ACT = mybir.ActivationFunctionType
AX = mybir.AxisListType
F32 = mybir.dt.float32
BF16 = mybir.dt.bfloat16
I32 = mybir.dt.int32

P = 128

VECTOR_ROWS = {"g_mix": (0, 8), "g_ffn": (8, 8), "g_ple": (16, 8), "conv_w": (24, 16), "conv_b": (40, 4),
               "lam": (44, 4), "b_a": (48, 4), "b_x": (52, 4), "g_oa": (56, 4), "g_ob": (60, 4)}
N_VECTOR_ROWS = 64


def decode_step(nc, a, out):
    SEQ, D = a["x_prompt"].shape[1:]
    NS = a["x_sample"].shape[0]
    DL = a["state_lru"].shape[2]
    NE, FF2 = a["w1"].shape[1], a["w1"].shape[3]
    FF = FF2 // 2
    PLE = a["w_pp"].shape[1]
    TAPS = a["conv_w"].shape[1]
    HEADS, HD = a["w_a"].shape[1], a["w_a"].shape[2]
    GROUPS = a["w_s"].shape[1]
    EPS = 1e-6
    LRU_C = 8.0
    LIMIT, ALPHA = 7.0, 1.702
    TOP_K = 4
    T = SEQ + NS
    TILES = [(t, P) for t in range(SEQ // P)] + [(SEQ // P, NS)]
    NT = len(TILES)
    KD = D // P
    NB = DL // P
    HALF = 512
    assert D == 2 * HALF and FF == D and SEQ == 2 * P and GROUPS == NB and HD * 2 == P

    CAP = 64
    MAX_ROUNDS = -(-T // CAP)
    STEPS = NE * MAX_ROUNDS
    W1_SLOTS, W2_SLOTS = KD, FF // P // 2
    SLOTS = W1_SLOTS + W2_SLOTS
    PARTS = 3

    with ExitStack() as ctx:
        def sb(name, shape, dt=F32, stack=ctx):
            return stack.enter_context(nc.sbuf_tensor(name, shape, dt))

        def sem(name):
            return ctx.enter_context(nc.semaphore(name))

        bank = [ctx.enter_context(nc.psum_tensor(f"bank{i}", [P, HALF], F32)) for i in range(8)]

        ring = sb("ring", [P, SLOTS, FF2])
        h = sb("h", [P, NT, D])
        hn = sb("hn", [P, NT, D])
        nT = sb("nT", [P, KD, T])
        b1_parts = sb("b1_parts", [P, FF2], BF16)
        ident = sb("ident", [P, P])
        ones = sb("ones", [P, P])
        head_ones = sb("head_ones", [P, P])
        ones_b = sb("ones_b", [P, P], BF16)
        before_b = sb("before_b", [P, P], BF16)
        slot_no = sb("slot_no", [P, 2 * CAP])
        expert_pick = sb("expert_pick", [P, STEPS + 1], BF16)
        vecT = sb("vecT", [P, N_VECTOR_ROWS])
        pos = sb("pos", [P, NT, STEPS + 1])
        share = sb("share", [P, NT, STEPS + 1])
        eps_col = sb("eps_col", [P, 1])
        sumsq = sb("sumsq", [P, NT])
        rms = sb("rms", [P, NT])
        rstd = sb("rstd", [P, NT])
        n_steps = sb("n_steps", [P, 2], I32)

        early = ExitStack()
        xpad = sb("xpad", [P, NB, 3 + SEQ + 4 * NS], stack=early)
        conv = sb("conv", [P, NB, SEQ + 4 * NS], stack=early)
        early.close()
        b1_mid = conv[0:NE, :, :].rearrange("p b t -> p (b t)").bitcast(BF16)[:, 0:FF2]
        mix = ExitStack()
        logT = sb("logT", [NE, T], stack=mix)
        NL = NE + TOP_K
        lg = sb("lg", [P, NT, NL], stack=mix)
        top = sb("top", [P, NT, 8], stack=mix)
        left = sb("left", [P, NT, NL], stack=mix)
        picked = sb("picked", [P, NT, NE], stack=mix)
        picked_b = sb("picked_b", [P, NT, NE], BF16, stack=mix)
        ex = sb("ex", [P, NT, NE], stack=mix)
        negmax = sb("negmax", [P, NT], stack=mix)
        exsum = sb("exsum", [P, NT], stack=mix)
        cw = sb("cw", [P, NT, NE], stack=mix)
        cwT = sb("cwT", [NE, T], stack=mix)
        slot1 = sb("slot1", [P, NT, NE], stack=mix)
        rounds = sb("rounds", [P, 8], stack=mix)
        sb("rest_of_early", [P, 1110], stack=mix)
        xc = sb("xc", [P, NB, T], stack=mix)
        yb = sb("yb", [P, NB, T], stack=mix)
        ya = sb("ya", [P, NB, T], stack=mix)
        ug = sb("ug", [P, NB, T], stack=mix)
        rg = sb("rg", [P, NB, T], stack=mix)
        ig = sb("ig", [P, NB, T], stack=mix)
        decay = sb("decay", [P, NB, T], stack=mix)
        th = sb("th", [P, NB, T], stack=mix)
        vt = sb("vt", [P, NT, DL], stack=mix)
        vss = sb("vss", [P, NT, GROUPS], stack=mix)
        ws = sb("ws", [P, GROUPS, P], stack=mix)
        wsT = sb("wsT", [P, GROUPS, P], stack=mix)
        w00 = sb("w00", [P, GROUPS], stack=mix)
        w00_diag = sb("w00_diag", [P, GROUPS, NS], stack=mix)
        bs_rows = sb("bs_rows", [GROUPS, T], stack=mix)
        past = sb("past", [32, DL], stack=mix)
        pastT = sb("pastT", [P, NB, 32], stack=mix)
        wab = sb("wab", [P, NB, P], stack=mix)
        wxb = sb("wxb", [P, NB, P], stack=mix)
        gv = sb("gv", [P, DL], stack=mix)
        news = sb("news", [P, NB, 36], stack=mix)
        vrows = sb("vrows", [N_VECTOR_ROWS, P], stack=mix)
        lamt = sb("lamt", [P, 8, NB], stack=mix)
        wr = sb("wr", [P, KD, NE], stack=mix)
        b2 = sb("b2", [NE, D], stack=mix)
        br = sb("br", [NE, 1], stack=mix)
        mix.close()

        moe = ExitStack()
        x_parts = sb("x_parts", [P, PARTS, 2, D], BF16, stack=moe)
        xs_parts = sb("xs_parts", [P, D], BF16, stack=moe)
        xs_mid = sb("xs_mid", [NS, D], BF16, stack=moe)
        pick = sb("pick", [P, NT, CAP], BF16, stack=moe)
        wpick = sb("wpick", [P, NT, 2 * CAP], stack=moe)
        wpickT = sb("wpickT", [P, T], stack=moe)
        b1_pick = sb("b1_pick", [P, CAP], BF16, stack=moe)
        xgT = sb("xgT", [P, KD, CAP], stack=moe)
        gmin = sb("gmin", [P, HALF], stack=moe)
        uclip = sb("uclip", [P, HALF], stack=moe)
        sig = sb("sig", [P, HALF], stack=moe)
        gu = sb("gu", [P, HALF], stack=moe)
        act_sb = sb("act_sb", [P, HALF], stack=moe)
        actT = sb("actT", [P, HALF], stack=moe)
        y = sb("y", [P, HALF], stack=moe)
        moe.close()

        tail = ExitStack()
        pw = sb("pw", [P, NT, D], stack=tail)
        p_rows = sb("p_rows", [P, NT, PLE], stack=tail)
        pT = sb("pT", [P, PLE // P, T], stack=tail)
        gate = sb("gate", [P, NT, D], stack=tail)
        bpg = sb("bpg", [P, D], stack=tail)
        gfin = sb("gfin", [P, D], stack=tail)
        tail.close()
        vsq = rg[:].rearrange("p b t -> p (b t)")[:, 0:DL]
        news_rows = ws[0:36, :, :].rearrange("p g t -> p (g t)")
        b1_rows = hn[0:NE, :, :].rearrange("p t d -> p (t d)")[:, 0:FF2]

        w_in = [ring[:, 2 * g:2 * g + 2, :].rearrange("p s n -> p (s n)").rearrange("p (k n) -> p k n", k=KD)
                for g in range(4)]
        w_out = ring[:, W1_SLOTS:SLOTS, :].rearrange("p s n -> p (s n)").rearrange("p (k n) -> p k n", k=KD)
        w_pg = ring[:, 0:4, :].rearrange("p s n -> p (s n)").rearrange("p (k n) -> p k n", k=KD)
        w_pp = ring[:, 4, :].rearrange("p (k n) -> p k n", k=PLE // P)

        x_in = sem("x_in")
        vec_in = sem("vec_in")
        past_in = sem("past_in")
        ws_in = sem("ws_in")
        bs_in = sem("bs_in")
        gates_in = sem("gates_in")
        gv_in = sem("gv_in")
        b1_in = sem("b1_in")
        router_in = sem("router_in")
        win_in = [sem(f"win_in{g}") for g in range(4)]
        wout_in = sem("wout_in")
        slot_in = [sem(f"slot_in{j}") for j in range(SLOTS)]
        p_in = sem("p_in")
        wpg_in = sem("wpg_in")
        wpp_in = sem("wpp_in")
        rows_in = sem("rows_in")
        stored = sem("stored")
        consts = sem("consts")
        zeroed = sem("zeroed")
        pool_done = sem("pool_done")
        dve_done = sem("dve_done")
        act_done = sem("act_done")
        turned = sem("turned")
        vecT_ready = sem("vecT_ready")
        pastT_ready = sem("pastT_ready")
        wsT_ready = sem("wsT_ready")
        sumsq_ready = sem("sumsq_ready")
        rms_ready = sem("rms_ready")
        hn_ready = sem("hn_ready")
        hn_turned = sem("hn_turned")
        nT_dve = sem("nT_dve")
        nT_act = sem("nT_act")
        z_made = sem("z_made")
        z_taken = sem("z_taken")
        xc_ready = sem("xc_ready")
        gates_made = sem("gates_made")
        gates_taken = sem("gates_taken")
        lru_act = sem("lru_act")
        lam_abs_ready = sem("lam_abs_ready")
        lam_exp_ready = sem("lam_exp_ready")
        decay_ready = sem("decay_ready")
        mult2_ready = sem("mult2_ready")
        mult_ready = sem("mult_ready")
        ybsq_ready = sem("ybsq_ready")
        ybss_made = sem("ybss_made")
        ybrms_ready = sem("ybrms_ready")
        yb_ready = sem("yb_ready")
        news_ready = sem("news_ready")
        news_turned = sem("news_turned")
        news_taken = sem("news_taken")
        v_turned = sem("v_turned")
        vsq_ready = sem("vsq_ready")
        vss_ready = sem("vss_ready")
        vrms_ready = sem("vrms_ready")
        vt_ready = sem("vt_ready")
        bs_ready = sem("bs_ready")
        s_made = sem("s_made")
        yasq_ready = sem("yasq_ready")
        yass_made = sem("yass_made")
        yarms_ready = sem("yarms_ready")
        ya_ready = sem("ya_ready")
        mixed_made = sem("mixed_made")
        h_mixed = sem("h_mixed")
        slots_free = sem("slots_free")
        logits_made = sem("logits_made")
        logT_ready = sem("logT_ready")
        lg_turned = sem("lg_turned")
        negmax_ready = sem("negmax_ready")
        ex_ready = sem("ex_ready")
        picked_ready = sem("picked_ready")
        places_made = sem("places_made")
        cw_ready = sem("cw_ready")
        cw_turned = sem("cw_turned")
        cwT_ready = sem("cwT_ready")
        b2_made = sem("b2_made")
        steps_ready = sem("steps_ready")
        parts_h = sem("parts_h")
        parts_r = sem("parts_r")
        parts_ready = sem("parts_ready")
        xs_low_ready = sem("xs_low_ready")
        moe_zeroed = sem("moe_zeroed")
        pick_ready = sem("pick_ready")
        wpick_ready = sem("wpick_ready")
        gathered = sem("gathered")
        xgT_ready = sem("xgT_ready")
        b1_pick_ready = sem("b1_pick_ready")
        gate_made = sem("gate_made")
        gmin_ready = sem("gmin_ready")
        uclip_ready = sem("uclip_ready")
        sig_ready = sem("sig_ready")
        gu_ready = sem("gu_ready")
        act_ready = sem("act_ready")
        act_turned = sem("act_turned")
        actT_ready = sem("actT_ready")
        wpick_turned = sem("wpick_turned")
        wpickT_ready = sem("wpickT_ready")
        y_ready = sem("y_ready")
        spread = sem("spread")
        h_added = sem("h_added")
        p_turned = sem("p_turned")
        pT_ready = sem("pT_ready")
        pw_made = sem("pw_made")
        pw_ready = sem("pw_ready")
        plegate_made = sem("plegate_made")
        plebias_ready = sem("plebias_ready")
        plegate_ready = sem("plegate_ready")
        h_final = sem("h_final")
        y_final = sem("y_final")

        def vcol(name, k):
            return vecT[:, VECTOR_ROWS[name][0] + k:VECTOR_ROWS[name][0] + k + 1]

        def halves(n):
            return slice(n * HALF, (n + 1) * HALF)

        block = ctx.enter_context(nc.Block())

        @block.sync
        def _(sp):
            sp.dma_start(h[:, 0:2, :], a["x_prompt"][0].rearrange("(t p) d -> p t d", p=P)).then_inc(x_in, 16)
            sp.dma_start(h[0:NS, 2, :], a["x_sample"].rearrange("b s d -> (b s) d")).then_inc(x_in, 16)
            for g, c in enumerate((2, 3, 1, 0)):
                sp.dma_start(w_in[g], a["w_in"][0].rearrange("(k p) n -> p k n", p=P)[:, :, c * DL:(c + 1) * DL]
                             ).then_inc(win_in[g], 16)
            sp.dma_start(w_out, a["w_out"][0].rearrange("(k p) n -> p k n", p=P)).then_inc(wout_in, 16)

            def load_slot(j, e):
                if j < W1_SLOTS:
                    src = a["w1"][0][bass.ds(e, 1)][:, j * P:(j + 1) * P, :].rearrange("e p n -> p (e n)")
                    sp.dma_start(ring[:, j, :], src).then_inc(slot_in[j], 16)
                else:
                    m = j - W1_SLOTS
                    src = a["w2"][0][bass.ds(e, 1)][:, 2 * m * P:(2 * m + 2) * P, :].rearrange(
                        "e (q p) n -> p (e q) n", p=P)
                    sp.dma_start(ring[:, j, :].rearrange("p (q n) -> p q n", q=2), src).then_inc(slot_in[j], 16)

            for j in range(SLOTS):
                if j < W1_SLOTS:
                    sp.wait_ge(z_made, NB * (j // 2 + 1))
                else:
                    sp.wait_ge(mixed_made, NT)
                load_slot(j, 0)
            with sp.Fori(0, NE - 1) as e:
                for j in range(SLOTS):
                    sp.wait_ge(slots_free, e * SLOTS + j + 1)
                    load_slot(j, e + 1)
            sp.wait_ge(steps_ready, 1)
            more = sp.value_load(n_steps[0:1, 1:2], min_val=0, max_val=STEPS - NE)
            with sp.If(more > 0):
                with sp.Fori(0, more) as i:
                    for j in range(SLOTS):
                        sp.wait_ge(slots_free, (i + (NE - 1)) * SLOTS + j + 1)
                        load_slot(j, i % NE)
            sp.wait_ge(slots_free, (more + (NE - 1)) * SLOTS + 4)
            sp.dma_start(w_pg, a["w_pg"][0].rearrange("(k p) n -> p k n", p=P)).then_inc(wpg_in, 16)
            sp.wait_ge(slots_free, (more + (NE - 1)) * SLOTS + 5)
            sp.dma_start(w_pp, a["w_pp"][0].rearrange("(k p) n -> p k n", p=P)).then_inc(wpp_in, 16)
            for t, rows in TILES:
                sp.wait_ge(y_final, t + 1)
                dst = (out["y_prompt"][0][t * P:(t + 1) * P, :] if t < 2
                       else out["y_sample"].rearrange("b s d -> (b s) d"))
                sp.dma_start(dst, hn[0:rows, t, :]).then_inc(stored, 16)
            sp.wait_ge(stored, 16 * 9)

        @block.gpsimd
        def _(pool):
            def link(ins):
                pool_count[0] += 1
                ins.then_inc(pool_done, 1)
                pool.wait_ge(pool_done, pool_count[0])
            pool_count = [0]
            link(pool.memset(ident[:], 0.0))
            pool.affine_select(out=ident[:], in_=ident[:], compare_op=ALU.not_equal, fill=1.0, base=0,
                               pattern=[[-1, P]], channel_multiplier=1).then_inc(consts, 1)
            link(pool.memset(before_b[:], 1.0))
            pool.affine_select(out=before_b[:], in_=before_b[:], compare_op=ALU.is_gt, fill=0.0, base=0,
                               pattern=[[1, P]], channel_multiplier=-1).then_inc(consts, 1)
            pool.iota(slot_no[:], pattern=[[0, 2], [1, CAP]], base=0, channel_multiplier=0,
                      allow_small_or_imprecise_dtypes=True).then_inc(consts, 1)
            pool.wait_ge(ws_in, 16)
            for g in range(GROUPS):
                pool.affine_select(out=ws[:, g, :], in_=ws[:, g, :], compare_op=ALU.is_ge, fill=0.0, base=0,
                                   pattern=[[-1, P]], channel_multiplier=1).then_inc(consts, 1)
            for t, rows in TILES:
                pool.wait_ge(parts_h, 2 * t + 1)
                hi = x_parts[0:rows, 0, t, :] if t < 2 else xs_parts[0:rows, :]
                pool.tensor_tensor(hn[0:rows, t, :], hn[0:rows, t, :], hi, ALU.subtract).then_inc(parts_r, 1)
                if t < 2:
                    pool.wait_ge(parts_h, 2 * t + 2)
                    pool.wait_ge(parts_r, t + 1)
                    pool.tensor_tensor(x_parts[:, 2, t, :], hn[:, t, :], x_parts[:, 1, t, :], ALU.subtract
                                       ).then_inc(parts_ready, 1)

        @block.scalar
        def _(act):
            count = [0]

            def link(ins):
                count[0] += 1
                ins.then_inc(act_done, 1)
                act.wait_ge(act_done, count[0])

            def load(dst, src, s, single_elements=False):
                act.dma_start(dst, src, allow_slow_non_contiguous=single_elements).then_inc(s, 16)

            for name, (r0, n) in VECTOR_ROWS.items():
                src = a[name][0]
                if name in ("b_a", "b_x"):
                    src = src.rearrange("(r q) j -> r (q j)", q=2)
                elif name == "conv_w":
                    src = src.rearrange("k (r j) -> (k r) j", j=P)
                else:
                    src = src.rearrange("(r j) -> r j", j=P)
                load(vrows[r0:r0 + n, :], src, vec_in)
            load(past[0:3 * NS, :], a["state_conv"][0].rearrange("b k d -> (b k) d"), past_in)
            load(past[3 * NS:3 * NS + NS, :], a["state_lru"][0], past_in)
            act.wait_ge(zeroed, 4)
            for dst, name in ((wab, "w_a"), (wxb, "w_x")):
                src = a[name][0].rearrange("(b q) i j -> q i b j", q=2)
                for q in range(2):
                    load(dst[HD * q:HD * (q + 1), :, HD * q:HD * (q + 1)], src[q], gates_in)
            load(ws[:], a["w_s"][0].rearrange("g t s -> t g s"), ws_in)
            load(gv[:], a["g_v"][0].partition_broadcast(P), gv_in)
            load(bs_rows[:, 0:P], a["b_s"][0], bs_in)
            load(bs_rows[:, P:2 * P], a["b_s"][0], bs_in)
            load(w00[0:NS, :], a["w_s"][0][:, 0, 0].partition_broadcast(NS), bs_in, True)
            load(wr[:], a["w_r"][0].rearrange("(k p) e -> p k e", p=P), router_in)
            load(br[:], a["b_r"].rearrange("o e -> e o"), router_in, True)
            load(b2[:], a["b2"][0], router_in)

            junk = ug[:].rearrange("p b t -> p (b t)")[:, 0:D]

            def row_rms(stage, junk_rows):
                for t, rows in TILES:
                    if stage == 1:
                        act.wait_ge(h_mixed, t + 1)
                    link(act.activation(junk_rows[0:rows, :], h[0:rows, t, :], ACT.Square,
                                        accum_out=sumsq[0:rows, t:t + 1]))
                act.activation(rms[:], sumsq[:], ACT.Sqrt, bias=eps_col[:], scale=1.0 / D).then_inc(rms_ready, 1)

            def take_nT(stage, gain):
                for k in range(1, KD, 2):
                    act.wait_ge(hn_turned, stage * KD + k + 1)
                    act.activation(nT[:, k, :], bank[4 + k % 4][:, 0:T], ACT.Identity,
                                   scale=vcol(gain, k)).then_inc(nT_act, 1)

            act.wait_ge(x_in, 32)
            act.wait_ge(zeroed, 2)
            row_rms(0, junk)
            act.wait_ge(vecT_ready, 1)
            take_nT(0, "g_mix")
            act.wait_ge(lam_abs_ready, 1)
            act.activation(lamt[:, 2, :], lamt[:, 1, :], ACT.Exp, scale=-1.0).then_inc(lam_exp_ready, 1)
            act.wait_ge(hn_turned, KD)
            load(b1_rows, a["b1"][0], b1_in)
            act.wait_ge(turned, 3)
            act.activation(wsT[:].rearrange("p g t -> p (g t)"), bank[2][:], ACT.Copy).then_inc(wsT_ready, 1)

            def take_z(first, count_, body):
                for b in range(first, first + count_):
                    act.wait_ge(z_made, b + 1)
                    body(b % NB, bank[b % 4])

            def to_xpad(blk, z):
                act.activation(xpad[:, blk, 3:3 + SEQ], z[:, 0:SEQ], ACT.Copy).then_inc(z_taken, 1)
                act.activation(xpad[:, blk, 3 + SEQ:].rearrange("p (s k) -> p s k", k=4)[:, :, 3], z[:, SEQ:T],
                               ACT.Copy).then_inc(z_taken, 1)

            def gelu_to(dst):
                def body(blk, z):
                    act.activation(dst[:, blk, :], z[:, 0:T], ACT.Gelu_apprx_tanh).then_inc(z_taken, 2)
                return body

            act.wait_ge(zeroed, 5)
            take_z(0, NB, to_xpad)
            take_z(NB, NB, gelu_to(yb))
            for dst, bias, first in ((rg, "b_a", 0), (ig, "b_x", NB)):
                for blk in range(NB):
                    act.wait_ge(gates_made, first + blk + 1)
                    act.activation(dst[:, blk, :], bank[4 + blk][:, 0:T], ACT.Sigmoid, bias=vcol(bias, blk)
                                   ).then_inc(gates_taken, 1)
            act.wait_ge(decay_ready, 1)
            act.wait_ge(gates_taken, 2 * NB)
            for blk in range(NB):
                act.activation(th[:, blk, :], rg[:, blk, :], ACT.Tanh, scale=lamt[:, 6, blk:blk + 1]
                               ).then_inc(lru_act, 1)
            for blk in range(NB):
                act.activation(decay[:, blk, :], rg[:, blk, :], ACT.Exp, scale=lamt[:, 7, blk:blk + 1]
                               ).then_inc(lru_act, 1)
            act.wait_ge(mult2_ready, 1)
            act.activation(th[:], th[:], ACT.Sqrt).then_inc(mult_ready, 1)
            take_z(2 * NB, NB, gelu_to(ya))
            take_z(3 * NB, NB, gelu_to(ug))

            act.wait_ge(news_turned, 1)
            act.activation(news_rows[:], bank[7][0:36, :], ACT.Copy).then_inc(news_taken, 1)
            act.wait_ge(news_taken, 1)
            lru0 = 3 + 3 * NS
            load(out["conv_prompt"].rearrange("l b k d -> (l b k) d"), news_rows[0:3, :], stored)
            load(out["conv_sample"].rearrange("l b k d -> (l b k) d"), news_rows[3:lru0, :], stored)
            load(out["lru_prompt"].rearrange("l b d -> (l b) d"), news_rows[lru0:lru0 + 1, :], stored)
            load(out["lru_sample"].rearrange("l b d -> (l b) d"), news_rows[lru0 + 1:lru0 + 1 + NS, :], stored)
            act.wait_ge(ybsq_ready, 1)
            for t, rows in TILES:
                act.wait_ge(v_turned, t + 1)
                if t:
                    act.wait_ge(vss_ready, t)
                act.activation(vsq[0:rows, :], bank[4 + t][0:rows, :], ACT.Square).then_inc(vsq_ready, 1)
            act.wait_ge(vss_ready, NT)
            act.activation(vss[:], vss[:], ACT.Sqrt, bias=eps_col[:], scale=1.0 / P).then_inc(vrms_ready, 1)
            for blk in range(NB):
                act.wait_ge(ybss_made, blk + 1)
                act.activation(th[:, blk, :], bank[4 + blk][:, 0:T], ACT.Sqrt, bias=eps_col[:], scale=1.0 / HD
                               ).then_inc(ybrms_ready, 1)
            for blk in range(NB):
                act.wait_ge(yass_made, blk + 1)
                act.activation(decay[:, blk, :], bank[blk][:, 0:T], ACT.Sqrt, bias=eps_col[:], scale=1.0 / P
                               ).then_inc(yarms_ready, 1)
            act.wait_ge(vt_ready, NT)
            load(out["v_prompt"].rearrange("l b t d -> (l b t) d"), vt[:, 1, :], stored)
            load(out["v_sample"].rearrange("l b t d -> (l b t) d"), vt[0:NS, 2, :], stored)

            row_rms(1, junk)
            take_nT(1, "g_ffn")
            act.wait_ge(logits_made, 1)
            act.wait_ge(router_in, 48)
            act.activation(logT[:], bank[0][0:NE, 0:T], ACT.Identity, bias=br[:]).then_inc(logT_ready, 1)
            act.wait_ge(negmax_ready, 1)
            for t in range(NT):
                act.activation(ex[:, t, :], lg[:, t, 0:NE], ACT.Exp, bias=negmax[:, t:t + 1]).then_inc(ex_ready, 1)
            act.wait_ge(cw_turned, 1)
            act.activation(cwT[:], bank[0][0:NE, 0:T], ACT.Copy).then_inc(cwT_ready, 1)
            act.wait_ge(stored, 16 * 6)
            act.wait_ge(b2_made, NT)
            act.wait_ge(steps_ready, 1)
            act.wait_ge(moe_zeroed, 1)
            for t, rows in TILES:
                hi = x_parts[0:rows, 0, t, :] if t < 2 else xs_parts[0:rows, :]
                mid = x_parts[0:rows, 1, t, :] if t < 2 else xs_parts[32:32 + rows, :]
                act.activation(hi, hn[0:rows, t, :], ACT.Copy).then_inc(parts_h, 1)
                act.wait_ge(parts_r, t + 1)
                if t < 2:
                    act.activation(mid, hn[0:rows, t, :], ACT.Copy).then_inc(parts_h, 1)
                else:
                    act.activation(xs_mid[:], hn[0:rows, t, :], ACT.Copy).then_inc(parts_h, 1)
                    act.wait_ge(parts_h, 2 * NT)
                    act.activation(mid, xs_mid[:], ACT.Copy).then_inc(parts_h, 1)

            n = act.value_load(n_steps[0:1, 0:1], min_val=NE, max_val=STEPS)
            with act.Fori(0, n) as i:
                act.wait_ge(gmin_ready, i + 1)
                act.activation(sig[:], gmin[:], ACT.Sigmoid, scale=ALPHA).then_inc(sig_ready, 1)
                act.wait_ge(act_turned, i + 1)
                act.activation(actT[:], bank[3][:], ACT.Copy).then_inc(actT_ready, 1)
                act.wait_ge(wpick_turned, i + 1)
                act.activation(wpickT[:], bank[0][:, 0:T], ACT.Copy).then_inc(wpickT_ready, 1)
                act.wait_ge(slots_free, (i + 1) * SLOTS)
                act.activation(y[:], bank[2][:], ACT.Copy).then_inc(y_ready, 1)

            act.wait_ge(spread, n * NT + NT)
            load(p_rows[:, 0:2, :], a["p_prompt"][0, 0].rearrange("(t p) d -> p t d", p=P), p_in)
            load(p_rows[0:NS, 2, :], a["p_sample"][0].rearrange("b s d -> (b s) d"), p_in)
            load(bpg[:], a["b_pg"][0].partition_broadcast(P), rows_in)
            load(gfin[:], a["g_final"].partition_broadcast(P), rows_in)
            act.wait_ge(h_added, (n + 1) * (2 * NT) + NT)
            for t, rows in TILES:
                link(act.activation(gate[0:rows, t, :], h[0:rows, t, :], ACT.Square,
                                    accum_out=sumsq[0:rows, t:t + 1]))
            act.activation(rms[:], sumsq[:], ACT.Sqrt, bias=eps_col[:], scale=1.0 / D).then_inc(rms_ready, 1)
            for k in range(PLE // P):
                act.wait_ge(p_turned, k + 1)
                act.activation(pT[:, k, :], bank[k][:, 0:T], ACT.Copy).then_inc(pT_ready, 1)
            for t in range(2):
                for m in range(2):
                    act.wait_ge(pw_made, t + 1)
                    act.activation(pw[:, t, halves(m)], bank[2 * t + m][:], ACT.Copy).then_inc(pw_ready, 1)
            for m in range(2):
                act.wait_ge(pw_made, NT)
                act.activation(pw[0:NS, 2, halves(m)], bank[0][32 * m:32 * m + NS, :], ACT.Copy).then_inc(pw_ready, 1)
            take_nT(2, "g_ple")
            for t, rows in TILES:
                act.wait_ge(plebias_ready, t + 1)
                act.activation(gate[0:rows, t, :], gate[0:rows, t, :], ACT.Sigmoid).then_inc(plegate_ready, 1)
            for t, rows in TILES:
                act.wait_ge(h_final, t + 1)
                link(act.activation(gate[0:rows, t, :], h[0:rows, t, :], ACT.Square,
                                    accum_out=sumsq[0:rows, t:t + 1]))
                act.activation(rms[0:rows, t:t + 1], sumsq[0:rows, t:t + 1], ACT.Sqrt, bias=eps_col[0:rows, :],
                               scale=1.0 / D).then_inc(rms_ready, 1)

        @block.vector
        def _(dve):
            count = [0]

            def link(ins):
                count[0] += 1
                ins.then_inc(dve_done, 1)
                dve.wait_ge(dve_done, count[0])

            dve.memset(eps_col[:], EPS).then_inc(zeroed, 1)
            dve.memset(sumsq[:], 1.0).then_inc(zeroed, 1)
            dve.memset(wab[:], 0.0).then_inc(zeroed, 1)
            dve.memset(wxb[:], 0.0).then_inc(zeroed, 1)
            dve.memset(xpad[:], 0.0).then_inc(zeroed, 1)
            dve.memset(vss[:], 1.0)
            link(dve.memset(head_ones[:], 0.0))
            dve.memset(ones[:], 1.0).then_inc(zeroed, 1)
            dve.memset(ones_b[:], 1.0)
            dve.memset(head_ones[0:HD, 0:HD], 1.0)
            link(dve.memset(head_ones[HD:P, HD:P], 1.0))

            dve.wait_ge(turned, 1)
            dve.tensor_copy(vecT[:], bank[0][:, 0:N_VECTOR_ROWS]).then_inc(vecT_ready, 1)

            def norm_rows(stage):
                dve.wait_ge(rms_ready, stage + 1)
                link(dve.reciprocal(rstd[:], rms[:]))
                for t, rows in TILES:
                    dve.tensor_scalar(hn[0:rows, t, :], h[0:rows, t, :], rstd[0:rows, t:t + 1], None, ALU.mult
                                      ).then_inc(hn_ready, 1)

            def take_nT(stage, gain):
                for k in range(0, KD, 2):
                    dve.wait_ge(hn_turned, stage * KD + k + 1)
                    dve.tensor_scalar(nT[:, k, :], bank[4 + k % 4][:, 0:T], vcol(gain, k), None, ALU.mult
                                      ).then_inc(nT_dve, 1)

            norm_rows(0)
            dve.wait_ge(vecT_ready, 1)
            take_nT(0, "g_mix")

            dve.wait_ge(turned, 2)
            dve.tensor_copy(pastT[:].rearrange("p b r -> p (b r)"), bank[1][:, 0:NB * 32]).then_inc(pastT_ready, 1)
            dve.wait_ge(pastT_ready, 1)
            sam = xpad[:, :, 3 + SEQ:].rearrange("p b (s k) -> p b s k", k=4)
            for blk in range(NB):
                link(dve.tensor_copy(sam[:, blk, :, 0:3],
                                     pastT[:, blk, 0:3 * NS].rearrange("p (s k) -> p s k", k=3)))

            L = [lamt[:, j, :] for j in range(8)]
            lam = vecT[:, VECTOR_ROWS["lam"][0]:VECTOR_ROWS["lam"][0] + NB]
            link(dve.tensor_scalar(L[0], lam, -1.0, None, ALU.mult))
            link(dve.tensor_tensor(L[1], lam, L[0], ALU.max))
            dve.tensor_scalar(L[0], L[0], 0.0, None, ALU.max).then_inc(lam_abs_ready, 1)
            dve.wait_ge(lam_exp_ready, 1)
            link(dve.tensor_scalar(L[3], L[2], 2.0, None, ALU.add))
            link(dve.reciprocal(L[3], L[3]))
            link(dve.tensor_tensor(L[2], L[2], L[3], ALU.mult))
            link(dve.tensor_tensor(L[3], L[2], L[2], ALU.mult))
            link(dve.memset(L[4], 1.0 / 17))
            for odd in range(15, 0, -2):
                link(dve.tensor_tensor(L[4], L[4], L[3], ALU.mult))
                link(dve.tensor_scalar(L[4], L[4], 1.0 / odd, None, ALU.add))
            link(dve.tensor_tensor(L[4], L[4], L[2], ALU.mult))
            link(dve.scalar_tensor_tensor(out=L[5], in0=L[4], scalar=2.0, in1=L[0], op0=ALU.mult, op1=ALU.add))
            link(dve.tensor_scalar(L[6], L[5], LRU_C, None, ALU.mult))
            dve.tensor_scalar(L[7], L[5], -LRU_C, None, ALU.mult).then_inc(decay_ready, 1)

            for blk in range(NB):
                dve.wait_ge(z_taken, 2 * (blk + 1))
                width = SEQ + 4 * NS
                link(dve.tensor_scalar(conv[:, blk, :], xpad[:, blk, 0:width], vcol("conv_w", blk),
                                       vcol("conv_b", blk), ALU.mult, ALU.add))
                for k in range(1, TAPS - 1):
                    link(dve.scalar_tensor_tensor(out=conv[:, blk, :], in0=xpad[:, blk, k:k + width],
                                                  scalar=vcol("conv_w", k * NB + blk), in1=conv[:, blk, :],
                                                  op0=ALU.mult, op1=ALU.add))
                k = TAPS - 1
                dve.scalar_tensor_tensor(out=xc[:, blk, 0:SEQ], in0=xpad[:, blk, k:k + SEQ],
                                         scalar=vcol("conv_w", k * NB + blk), in1=conv[:, blk, 0:SEQ],
                                         op0=ALU.mult, op1=ALU.add)
                dve.scalar_tensor_tensor(out=xc[:, blk, SEQ:T], in0=sam[:, blk, :, k],
                                         scalar=vcol("conv_w", k * NB + blk),
                                         in1=conv[:, blk, SEQ:width].rearrange("p (s k) -> p s k", k=4)[:, :, k],
                                         op0=ALU.mult, op1=ALU.add).then_inc(xc_ready, 1)

            dve.wait_ge(lru_act, NB)
            link(dve.tensor_scalar(conv[:, :, 0:T], th[:], 1.0, None, ALU.add))
            link(dve.reciprocal(conv[:, :, 0:T], conv[:, :, 0:T]))
            dve.scalar_tensor_tensor(out=th[:], in0=th[:], scalar=2.0, in1=conv[:, :, 0:T],
                                     op0=ALU.mult, op1=ALU.mult).then_inc(mult2_ready, 1)
            dve.wait_ge(gates_taken, 2 * NB)
            link(dve.tensor_tensor(ig[:], ig[:], xc[:], ALU.mult))
            dve.wait_ge(mult_ready, 1)
            link(dve.memset(th[:, :, 0:1], 1.0))
            link(dve.tensor_tensor(ig[:], ig[:], th[:], ALU.mult))
            dve.wait_ge(lru_act, 2 * NB)
            for blk in range(NB):
                dve.tensor_tensor_scan(rg[:, blk, 0:SEQ], decay[:, blk, 0:SEQ], ig[:, blk, 0:SEQ], 0.0,
                                       ALU.mult, ALU.add)
            link(dve.tensor_tensor(rg[:, :, SEQ:T], decay[:, :, SEQ:T], pastT[:, :, 3 * NS:4 * NS], ALU.mult))
            link(dve.tensor_tensor(rg[:, :, SEQ:T], rg[:, :, SEQ:T], ig[:, :, SEQ:T], ALU.add))
            dve.tensor_copy(news[:, :, 0:3], xpad[:, :, SEQ:SEQ + 3])
            for blk in range(NB):
                dve.tensor_copy(news[:, blk, 3:3 + 3 * NS].rearrange("p (s k) -> p s k", k=3), sam[:, blk, :, 1:4])
            dve.tensor_copy(news[:, :, 3 + 3 * NS:4 + 4 * NS], rg[:, :, SEQ - 1:T]).then_inc(news_ready, 1)
            dve.wait_ge(z_taken, 4 * NB)
            link(dve.tensor_tensor(yb[:], rg[:], yb[:], ALU.mult))
            dve.tensor_tensor(ig[:], yb[:], yb[:], ALU.mult).then_inc(ybsq_ready, 1)

            dve.wait_ge(b1_in, 16)
            link(dve.tensor_copy(b1_parts[0:NE, :], b1_rows))
            link(dve.tensor_tensor(b1_rows, b1_rows, b1_parts[0:NE, :], ALU.subtract))
            link(dve.tensor_copy(b1_mid[:], b1_rows))
            dve.tensor_copy(b1_parts[NE:2 * NE, :], b1_mid[:])
            link(dve.tensor_tensor(b1_parts[2 * NE:3 * NE, :], b1_rows, b1_mid[:], ALU.subtract))

            for t, rows in TILES:
                dve.wait_ge(vsq_ready, t + 1)
                dve.tensor_reduce(vss[0:rows, t, :], vsq[0:rows, :].rearrange("p (g d) -> p g d", g=GROUPS),
                                  AX.X, ALU.add).then_inc(vss_ready, 1)
            dve.wait_ge(vrms_ready, 1)
            dve.wait_ge(gv_in, 16)
            link(dve.reciprocal(vss[:], vss[:]))
            for t, rows in TILES:
                for g in range(GROUPS):
                    cols = slice(g * P, (g + 1) * P)
                    ins = dve.scalar_tensor_tensor(out=vt[0:rows, t, cols], in0=bank[4 + t][0:rows, cols],
                                                   scalar=vss[0:rows, t, g:g + 1], in1=gv[0:rows, cols],
                                                   op0=ALU.mult, op1=ALU.mult)
                ins.then_inc(vt_ready, 1)
            dve.wait_ge(bs_in, 48)
            dve.wait_ge(consts, 1)
            for g in range(GROUPS):
                dve.tensor_scalar(w00_diag[0:NS, g, :], ident[0:NS, 0:NS], w00[0:NS, g:g + 1], None, ALU.mult)
            dve.tensor_scalar(bs_rows[:, SEQ:T], ones[0:GROUPS, 0:NS], bs_rows[:, 0:1], None, ALU.mult
                              ).then_inc(bs_ready, 1)

            for blk in range(NB):
                dve.wait_ge(ybrms_ready, blk + 1)
                link(dve.reciprocal(th[:, blk, :], th[:, blk, :]))
                dve.scalar_tensor_tensor(out=yb[:, blk, :], in0=yb[:, blk, :], scalar=vcol("g_ob", blk),
                                         in1=th[:, blk, :], op0=ALU.mult, op1=ALU.mult).then_inc(yb_ready, 1)

            dve.wait_ge(z_taken, 8 * NB)
            for g in range(GROUPS):
                dve.wait_ge(s_made, g + 1)
                link(dve.tensor_tensor(ya[:, g, :], bank[g][:, 0:T], ug[:, g, :], ALU.mult))
                dve.tensor_tensor(xc[:, g, :], ya[:, g, :], ya[:, g, :], ALU.mult).then_inc(yasq_ready, 1)
            for g in range(GROUPS):
                dve.wait_ge(yarms_ready, g + 1)
                link(dve.reciprocal(decay[:, g, :], decay[:, g, :]))
                dve.scalar_tensor_tensor(out=ya[:, g, :], in0=ya[:, g, :], scalar=vcol("g_oa", g),
                                         in1=decay[:, g, :], op0=ALU.mult, op1=ALU.mult).then_inc(ya_ready, 1)

            for t in range(2):
                dve.wait_ge(mixed_made, t + 1)
                for m in range(2):
                    ins = dve.tensor_tensor(h[:, t, halves(m)], bank[4 + 2 * t + m][:], h[:, t, halves(m)], ALU.add)
                ins.then_inc(h_mixed, 1)
            dve.wait_ge(mixed_made, NT)
            for q in range(2):
                for m in range(2):
                    r0 = 32 * (2 * q + m)
                    ins = dve.tensor_tensor(h[0:NS, 2, halves(m)], bank[0][r0:r0 + NS, :], h[0:NS, 2, halves(m)],
                                            ALU.add)
                    if q == 0:
                        link(ins)
            ins.then_inc(h_mixed, 1)

            link(dve.memset(lg[:], 0.0))
            link(dve.memset(lg[:, :, NE:NL], 3.0e38))
            link(dve.memset(pos[:], -1.0))
            link(dve.memset(share[:], 0.0))
            norm_rows(1)
            take_nT(1, "g_ffn")
            dve.wait_ge(lg_turned, 1)
            dve.tensor_copy(lg[:, 0:2, 0:NE], bank[1][:, 0:2 * NE].rearrange("p (t e) -> p t e", t=2))
            link(dve.tensor_copy(lg[0:NS, 2, 0:NE], bank[1][0:NS, 2 * NE:3 * NE]))
            for t in range(NT):
                link(dve.max(top[:, t, :], lg[:, t, :]))
            dve.tensor_scalar(negmax[:], top[:, :, TOP_K], -1.0, None, ALU.mult).then_inc(negmax_ready, 1)
            for t in range(NT):
                link(dve.match_replace(left[:, t, :], top[:, t, :], lg[:, t, :], -3.0e38))
            link(dve.tensor_tensor(picked[:], left[:, :, 0:NE], lg[:, :, 0:NE], ALU.is_lt))
            dve.tensor_copy(picked_b[:], picked[:]).then_inc(picked_ready, 1)
            dve.wait_ge(ex_ready, NT)
            link(dve.tensor_tensor(cw[:], ex[:], picked[:], ALU.mult))
            link(dve.tensor_reduce(exsum[:], cw[:], AX.X, ALU.add))
            link(dve.reciprocal(exsum[:], exsum[:]))
            for t in range(NT):
                ins = dve.tensor_scalar(cw[:, t, :], cw[:, t, :], exsum[:, t:t + 1], None, ALU.mult)
            ins.then_inc(cw_ready, 1)

            dve.wait_ge(places_made, 1)
            dve.tensor_copy(slot1[:, 0:2, :], bank[2][:, 0:2 * NE].rearrange("p (t e) -> p t e", t=2))
            link(dve.tensor_copy(slot1[0:NS, 2, :], bank[2][0:NS, 2 * NE:3 * NE]))
            for rows, tt in ((P, slice(0, 2)), (NS, slice(2, 3))):
                link(dve.scalar_tensor_tensor(out=slot1[0:rows, tt, :], in0=slot1[0:rows, tt, :], scalar=1.0,
                                              in1=picked[0:rows, tt, :], op0=ALU.add, op1=ALU.mult))
            for r in range(MAX_ROUNDS):
                cols = slice(r * NE, (r + 1) * NE)
                shift = -1.0 - CAP * r
                dve.tensor_scalar(pos[:, 0:2, cols], slot1[:, 0:2, :], shift, None, ALU.add)
                for q in range(PARTS):
                    dve.tensor_scalar(pos[32 * q:32 * q + NS, 2, cols], slot1[0:NS, 2, :], shift, None, ALU.add)
                dve.tensor_copy(share[:, 0:2, cols], cw[:, 0:2, :])
                dve.tensor_copy(share[0:NS, 2, cols], cw[0:NS, 2, :])
                for q in range(PARTS):
                    dve.tensor_copy(expert_pick[NE * q:NE * (q + 1), cols], ident[0:NE, 0:NE])
            link(dve.memset(expert_pick[0:PARTS * NE, STEPS:STEPS + 1], 0.0))
            link(dve.tensor_reduce(rounds[:, 0:1], bank[3][:, 0:NE], AX.X, ALU.max))
            for r in range(1, MAX_ROUNDS):
                dve.memset(rounds[:, r:r + 1], float(CAP * r))
            link(dve.memset(rounds[:, 6:7], 0.0))
            link(dve.tensor_scalar(rounds[:, 1:MAX_ROUNDS], rounds[:, 1:MAX_ROUNDS], rounds[:, 0:1], None, ALU.is_lt))
            link(dve.tensor_reduce(rounds[:, 6:7], rounds[:, 1:MAX_ROUNDS], AX.X, ALU.add))
            dve.tensor_scalar(n_steps[:, 0:1], rounds[:, 6:7], float(NE), float(NE), ALU.mult, ALU.add)
            dve.tensor_scalar(n_steps[:, 1:2], rounds[:, 6:7], float(NE), None, ALU.mult).then_inc(steps_ready, 1)

            for t, rows in TILES:
                dve.wait_ge(b2_made, t + 1)
                for m in range(2):
                    src = bank[4 + 2 * t + m] if t < 2 else bank[m]
                    ins = dve.tensor_tensor(h[0:rows, t, halves(m)], src[0:rows, :], h[0:rows, t, halves(m)], ALU.add)
                ins.then_inc(h_added, 1)

            dve.wait_ge(stored, 16 * 6)
            dve.wait_ge(steps_ready, 1)
            dve.memset(xs_parts[:], 0.0).then_inc(moe_zeroed, 1)
            dve.memset(y[:], 0.0).then_inc(y_ready, 1)
            dve.memset(wpickT[:], 0.0).then_inc(wpickT_ready, 1)

            def make_pick(step):
                for t, rows in ((0, P), (1, P), (2, PARTS * 32)):
                    ins = dve.tensor_scalar(pick[0:rows, t, :], slot_no[0:rows, 0:CAP],
                                            pos[0:rows, t, bass.ds(step, 1)], None, ALU.is_equal)
                ins.then_inc(pick_ready, 1)

            def make_b1_pick(step):
                dve.tensor_scalar(b1_pick[0:PARTS * NE, :], ones_b[0:PARTS * NE, 0:CAP],
                                  expert_pick[0:PARTS * NE, bass.ds(step, 1)], None, ALU.mult
                                  ).then_inc(b1_pick_ready, 1)

            def make_xgT(step):
                dve.wait_ge(gathered, step + 1)
                dve.tensor_tensor(xgT[:], bank[3][:].rearrange("p (k s) -> p k s", k=KD),
                                  g_ffn_wide, ALU.mult).then_inc(xgT_ready, 1)

            g0 = VECTOR_ROWS["g_ffn"][0]
            g_ffn_wide = vecT[:, g0:g0 + KD].unsqueeze(2).to_broadcast([P, KD, CAP])
            make_pick(0)
            make_b1_pick(0)
            dve.wait_ge(parts_r, NT)
            dve.wait_ge(parts_h, 2 * NT)
            dve.tensor_tensor(xs_parts[64:64 + NS, :], hn[0:NS, 2, :], xs_mid[:], ALU.subtract
                              ).then_inc(xs_low_ready, 1)
            make_xgT(0)

            def add_tile(t, rows, first_bank, products, added):
                dve.wait_ge(spread, products)
                dve.wait_ge(h_added, added)
                for m in range(2):
                    src = bank[first_bank + m]
                    dve.tensor_tensor(h[0:rows, t, halves(m)], src[0:rows, :], h[0:rows, t, halves(m)], ALU.add
                                      ).then_inc(h_added, 1)

            n = dve.value_load(n_steps[0:1, 0:1], min_val=NE, max_val=STEPS)
            with dve.Fori(0, n) as i:
                dve.wait_ge(gathered, i + 1)
                make_pick(i + 1)
                dve.wait_ge(slots_free, i * SLOTS + 1)
                for t, rows in TILES:
                    ins = dve.tensor_scalar(wpick[0:rows, t, :], slot_no[0:rows, :],
                                            pos[0:rows, t, bass.ds(i, 1)], share[0:rows, t, bass.ds(i, 1)],
                                            ALU.is_equal, ALU.mult)
                ins.then_inc(wpick_ready, 1)
                dve.wait_ge(gate_made, i + 1)
                dve.tensor_scalar(gmin[:], bank[0][:], LIMIT, None, ALU.min).then_inc(gmin_ready, 1)
                dve.wait_ge(slots_free, i * SLOTS + W1_SLOTS)
                dve.tensor_scalar(uclip[:], bank[1][:], LIMIT, -LIMIT, ALU.min, ALU.max).then_inc(uclip_ready, 1)
                make_b1_pick(i + 1)
                add_tile(0, P, 4, i * NT + 1, i * 2 * NT + NT)
                dve.wait_ge(gmin_ready, i + 1)
                dve.wait_ge(uclip_ready, i + 1)
                dve.scalar_tensor_tensor(out=gu[:], in0=uclip[:], scalar=1.0, in1=gmin[:], op0=ALU.add,
                                         op1=ALU.mult).then_inc(gu_ready, 1)
                dve.wait_ge(sig_ready, i + 1)
                dve.wait_ge(gu_ready, i + 1)
                dve.tensor_tensor(act_sb[:], gu[:], sig[:], ALU.mult).then_inc(act_ready, 1)
                make_xgT(i + 1)
                add_tile(1, P, 6, i * NT + 2, i * 2 * NT + NT + 2)
                add_tile(2, NS, 4, i * NT + 3, i * 2 * NT + NT + 4)
            add_tile(0, P, 4, n * NT + 1, n * 2 * NT + NT)
            add_tile(1, P, 6, n * NT + 2, n * 2 * NT + NT + 2)
            add_tile(2, NS, 0, n * NT + 3, n * 2 * NT + NT + 4)

            norm_rows(2)
            take_nT(2, "g_ple")
            dve.wait_ge(rows_in, 32)
            for t, rows in TILES:
                dve.wait_ge(plegate_made, t + 1)
                for m in range(2):
                    if t < 2:
                        ins = dve.tensor_tensor(gate[:, t, halves(m)], bank[2 * t + m][:], bpg[:, halves(m)], ALU.add)
                    else:
                        link(dve.tensor_tensor(gate[0:NS, t, halves(m)], bank[4][32 * m:32 * m + NS, :],
                                               bpg[0:NS, halves(m)], ALU.add))
                        ins = dve.tensor_tensor(gate[0:NS, t, halves(m)], bank[4][64 + 32 * m:64 + 32 * m + NS, :],
                                                gate[0:NS, t, halves(m)], ALU.add)
                ins.then_inc(plebias_ready, 1)
            for t, rows in TILES:
                dve.wait_ge(plegate_ready, t + 1)
                dve.wait_ge(pw_ready, 6)
                link(dve.tensor_tensor(gate[0:rows, t, :], gate[0:rows, t, :], pw[0:rows, t, :], ALU.mult))
                dve.tensor_tensor(h[0:rows, t, :], gate[0:rows, t, :], h[0:rows, t, :], ALU.add).then_inc(h_final, 1)
            for t, rows in TILES:
                dve.wait_ge(rms_ready, 3 + t + 1)
                link(dve.reciprocal(rstd[0:rows, t:t + 1], rms[0:rows, t:t + 1]))
                dve.scalar_tensor_tensor(out=hn[0:rows, t, :], in0=h[0:rows, t, :], scalar=rstd[0:rows, t:t + 1],
                                         in1=gfin[0:rows, :], op0=ALU.mult, op1=ALU.mult).then_inc(y_final, 1)

        @block.tensor
        def _(pe):
            def turn_rows(stage):
                for k in range(KD):
                    if k >= 4:
                        pe.wait_ge(nT_act if k % 2 else nT_dve, stage * (KD // 2) + (k - 4) // 2 + 1)
                    for t, rows in TILES:
                        if k == 0:
                            pe.wait_ge(hn_ready, stage * NT + t + 1)
                        ins = pe.transpose(bank[4 + k % 4][:, t * P:t * P + rows], hn[0:rows, t, k * P:(k + 1) * P],
                                           ident[0:rows, 0:rows])
                    ins.then_inc(hn_turned, 1)

            def wait_nT(stage, k):
                pe.wait_ge(nT_act if k % 2 else nT_dve, stage * (KD // 2) + k // 2 + 1)

            pe.wait_ge(consts, 1)
            pe.wait_ge(vec_in, 16 * len(VECTOR_ROWS))
            pe.transpose(bank[0][:, 0:N_VECTOR_ROWS], vrows[:], ident[0:N_VECTOR_ROWS, 0:N_VECTOR_ROWS]
                         ).then_inc(turned, 1)
            turn_rows(0)
            pe.wait_ge(past_in, 32)
            for blk in range(NB):
                ins = pe.transpose(bank[1][:, blk * 32:(blk + 1) * 32], past[:, blk * P:(blk + 1) * P],
                                   ident[0:32, 0:32])
            ins.then_inc(turned, 1)
            pe.wait_ge(consts, 3 + GROUPS)
            for g in range(GROUPS):
                ins = pe.transpose(bank[2][:, g * P:(g + 1) * P], ws[:, g, :], ident[:])
            ins.then_inc(turned, 1)

            def project(b):
                g, blk = b // NB, b % NB
                if blk == 0:
                    pe.wait_ge(win_in[g], 16)
                if b >= 4:
                    pe.wait_ge(z_taken, 2 * (b - 3))
                elif b == 0:
                    pe.wait_ge(vecT_ready, 1)
                elif b == 1:
                    pe.wait_ge(pastT_ready, 1)
                elif b == 2:
                    pe.wait_ge(wsT_ready, 1)
                for k in range(KD):
                    wait_nT(0, k)
                    ins = pe.matmul(bank[b % 4][:, 0:T], w_in[g][:, k, blk * P:(blk + 1) * P], nT[:, k, :],
                                    start=(k == 0), stop=(k == KD - 1))
                ins.then_inc(z_made, 1)

            def gates(w, first):
                for blk in range(NB):
                    pe.wait_ge(xc_ready, blk + 1)
                    if first:
                        pe.wait_ge(gates_taken, blk + 1)
                    pe.matmul(bank[4 + blk][:, 0:T], w[:, blk, :], xc[:, blk, :], start=True, stop=True
                              ).then_inc(gates_made, 1)

            for b in range(2 * NB):
                project(b)
            pe.wait_ge(gates_in, 64)
            gates(wab, 0)
            project(2 * NB)
            project(2 * NB + 1)
            gates(wxb, NB)
            project(2 * NB + 2)
            project(2 * NB + 3)
            project(3 * NB)
            project(3 * NB + 1)
            pe.wait_ge(z_taken, 2 * 3 * NB)
            pe.wait_ge(gates_taken, 2 * NB)
            for t, rows in TILES:
                for g in range(GROUPS):
                    ins = pe.transpose(bank[4 + t][0:rows, g * P:(g + 1) * P], ya[:, g, t * P:t * P + rows], ident[:])
                ins.then_inc(v_turned, 1)
            project(3 * NB + 2)
            project(3 * NB + 3)
            pe.wait_ge(news_ready, 1)
            for blk in range(NB):
                ins = pe.transpose(bank[7][0:36, blk * P:(blk + 1) * P], news[:, blk, :], ident[:])
            ins.then_inc(news_turned, 1)
            pe.wait_ge(ybsq_ready, 1)
            for blk in range(NB):
                pe.wait_ge(vt_ready, min(blk + 1, NT))
                if blk == NB - 1:
                    pe.wait_ge(news_taken, 1)
                pe.matmul(bank[4 + blk][:, 0:T], head_ones[:], ig[:, blk, :], start=True, stop=True
                          ).then_inc(ybss_made, 1)
            pe.wait_ge(vt_ready, NT)
            pe.wait_ge(bs_ready, 1)
            pe.wait_ge(wsT_ready, 1)
            pe.wait_ge(z_taken, 8 * NB)
            for g in range(GROUPS):
                cols = slice(g * P, (g + 1) * P)
                s = bank[g]
                pe.matmul(s[:, 0:T], ident[0:GROUPS, g:g + 1].to_broadcast([GROUPS, P]), bs_rows[:], start=True,
                          stop=False, skip_group_check=True)
                for t in range(2):
                    pe.matmul(s[:, t * P:(t + 1) * P], vt[:, t, cols], wsT[:, g, :], start=False, stop=False,
                              skip_group_check=True)
                pe.matmul(s[:, SEQ:T], vt[0:NS, 2, cols], w00_diag[0:NS, g, :], start=False, stop=True,
                          skip_group_check=True).then_inc(s_made, 1)

            pe.wait_ge(wout_in, 16)

            def mixed(t, k, first, last):
                src = ya[:, k, :] if k < NB else yb[:, k - NB, :]
                for m in range(2):
                    ins = pe.matmul(bank[4 + 2 * t + m][:], src[:, t * P:(t + 1) * P], w_out[:, k, halves(m)],
                                    start=first, stop=last)
                return ins

            pe.wait_ge(ybrms_ready, NB)
            for blk in range(NB):
                pe.wait_ge(yb_ready, blk + 1)
                mixed(0, NB + blk, blk == 0, False)
            for g in range(GROUPS):
                pe.wait_ge(yasq_ready, g + 1)
                pe.matmul(bank[g][:, 0:T], ones[:], xc[:, g, :], start=True, stop=True).then_inc(yass_made, 1)
            for blk in range(NB):
                mixed(1, NB + blk, blk == 0, False)
            for t in range(2):
                for g in range(GROUPS):
                    pe.wait_ge(ya_ready, g + 1)
                    ins = mixed(t, g, False, g == GROUPS - 1)
                ins.then_inc(mixed_made, 1)

            def small_tile(dst, lhs, w, chunks):
                for c in range(chunks // 2):
                    for q in range(2):
                        for m in range(2):
                            k = q * (chunks // 2) + c
                            r0 = 32 * (2 * q + m)
                            ins = pe.matmul(dst[r0:r0 + NS, :], lhs(k), w[:, k, halves(m)], start=(c == 0),
                                            stop=(c == chunks // 2 - 1), skip_group_check=True)
                return ins

            pe.wait_ge(yarms_ready, NB)
            small_tile(bank[0], lambda k: (ya[:, k, :] if k < NB else yb[:, k - NB, :])[:, SEQ:T], w_out, KD
                       ).then_inc(mixed_made, 1)

            pe.wait_ge(h_mixed, NT)
            turn_rows(1)
            pe.wait_ge(router_in, 48)
            for k in range(KD):
                wait_nT(1, k)
                ins = pe.matmul(bank[0][0:NE, 0:T], wr[:, k, :], nT[:, k, :], start=(k == 0), stop=(k == KD - 1))
            ins.then_inc(logits_made, 1)
            pe.wait_ge(logT_ready, 1)
            for t, rows in TILES:
                ins = pe.transpose(bank[1][0:rows, t * NE:(t + 1) * NE], logT[:, t * P:t * P + rows], ident[0:NE, 0:NE])
            ins.then_inc(lg_turned, 1)
            pe.wait_ge(picked_ready, 1)
            pe.wait_ge(consts, 2)
            for t, rows in TILES:
                for s in range(t + 1):
                    rows_s = TILES[s][1]
                    lhs = before_b if s == t else ones_b
                    pe.matmul(bank[2][0:rows, t * NE:(t + 1) * NE], lhs[0:rows_s, 0:rows], picked_b[0:rows_s, s, :],
                              start=(s == 0), stop=(s == t), skip_group_check=True)
            for s, rows_s in TILES:
                ins = pe.matmul(bank[3][:, 0:NE], ones_b[0:rows_s, :], picked_b[0:rows_s, s, :], start=(s == 0),
                                stop=(s == NT - 1))
            ins.then_inc(places_made, 1)
            pe.wait_ge(cw_ready, 1)
            for t, rows in TILES:
                ins = pe.transpose(bank[0][0:NE, t * P:t * P + rows], cw[0:rows, t, :], ident[0:rows, 0:rows])
            ins.then_inc(cw_turned, 1)
            pe.wait_ge(cwT_ready, 1)
            for t, rows in TILES:
                for m in range(2):
                    dst = bank[4 + 2 * t + m] if t < 2 else bank[m]
                    ins = pe.matmul(dst[0:rows, :], cwT[:, t * P:t * P + rows], b2[:, halves(m)], start=True, stop=True)
                ins.then_inc(b2_made, 1)

            def gather(step, added=None):
                pe.wait_ge(pick_ready, step + 1)
                for k in range(KD):
                    cols = slice(k * P, (k + 1) * P)
                    dst = bank[3][:, k * CAP:(k + 1) * CAP]
                    for t in range(2):
                        for q in range(PARTS):
                            pe.matmul(dst, x_parts[:, q, t, cols], pick[:, t, :], start=(t == 0 and q == 0),
                                      stop=False, skip_group_check=True)
                    if k == KD - 1 and added is not None:
                        pe.wait_ge(h_added, added)
                    ins = pe.matmul(dst, xs_parts[0:32 * PARTS, cols], pick[0:32 * PARTS, 2, :], start=False,
                                    stop=True, skip_group_check=True)
                ins.then_inc(gathered, 1)

            def scatter(t, rows, first_bank):
                for m in range(2):
                    r = slice(CAP * m, CAP * (m + 1))
                    ins = pe.matmul(bank[first_bank + m][0:rows, :], wpickT[r, t * P:t * P + rows], y[r, :],
                                    start=True, stop=True)
                ins.then_inc(spread, 1)

            pe.wait_ge(parts_ready, 2)
            pe.wait_ge(parts_h, 2 * NT + 1)
            pe.wait_ge(xs_low_ready, 1)
            pe.wait_ge(steps_ready, 1)
            n = pe.value_load(n_steps[0:1, 0:1], min_val=NE, max_val=STEPS)
            gather(0)
            pe.wait_ge(h_added, NT)
            with pe.Fori(0, n) as i:
                pe.wait_ge(b1_pick_ready, i + 1)
                pe.wait_ge(wpickT_ready, i + 1)
                for part in range(2):
                    for m in range(2):
                        r = slice(CAP * m, CAP * (m + 1))
                        c = part * FF + m * HALF
                        pe.matmul(bank[part][r, :], b1_pick[0:PARTS * NE, :], b1_parts[0:PARTS * NE, c:c + HALF],
                                  start=True, stop=False, skip_group_check=True)
                pe.wait_ge(xgT_ready, i + 1)
                for k in range(W1_SLOTS):
                    pe.wait_ge(slot_in[k], (i + 1) * 16)
                    for part in range(2):
                        for m in range(2):
                            r = slice(CAP * m, CAP * (m + 1))
                            c = part * FF + m * HALF
                            ins = pe.matmul(bank[part][r, :], xgT[:, k, :], ring[:, k, c:c + HALF],
                                            start=False, stop=(k == W1_SLOTS - 1), skip_group_check=True)
                        if part == 0 and k == W1_SLOTS - 1:
                            ins.then_inc(gate_made, 1)
                    ins.then_inc(slots_free, 1)
                pe.wait_ge(y_ready, i + 1)
                pe.wait_ge(h_added, i * 2 * NT + NT)
                scatter(0, P, 4)
                scatter(1, P, 6)
                gather(i + 1, i * 2 * NT + NT + 2)
                scatter(2, NS, 4)
                pe.wait_ge(act_ready, i + 1)
                pe.wait_ge(xgT_ready, i + 2)
                for c in range(HALF // P):
                    ins = pe.transpose(bank[3][:, c * P:(c + 1) * P], act_sb[:, c * P:(c + 1) * P], ident[:])
                ins.then_inc(act_turned, 1)
                pe.wait_ge(wpick_ready, i + 1)
                pe.wait_ge(gmin_ready, i + 1)
                for t, rows in TILES:
                    ins = pe.transpose(bank[0][:, t * P:t * P + rows], wpick[0:rows, t, :], ident[0:rows, 0:rows])
                ins.then_inc(wpick_turned, 1)
                pe.wait_ge(actT_ready, i + 1)
                for j in range(W2_SLOTS):
                    pe.wait_ge(slot_in[W1_SLOTS + j], (i + 1) * 16)
                    for q in range(2):
                        f = 2 * j + q
                        half = (f % 4) * P + (f // 4) * CAP
                        for m in range(2):
                            c = q * D + m * HALF
                            ins = pe.matmul(bank[2][CAP * m:CAP * (m + 1), :], actT[:, half:half + CAP],
                                            ring[:, W1_SLOTS + j, c:c + HALF], start=(f == 0),
                                            stop=(f == FF // P - 1), skip_group_check=True)
                    ins.then_inc(slots_free, 1)
            pe.wait_ge(y_ready, n + 1)
            pe.wait_ge(wpickT_ready, n + 1)
            pe.wait_ge(h_added, n * 2 * NT + NT)
            scatter(0, P, 4)
            scatter(1, P, 6)
            scatter(2, NS, 0)

            pe.wait_ge(p_in, 32)
            pe.wait_ge(h_added, (n + 1) * 2 * NT + NT)
            for k in range(PLE // P):
                for t, rows in TILES:
                    ins = pe.transpose(bank[k][:, t * P:t * P + rows], p_rows[0:rows, t, k * P:(k + 1) * P],
                                       ident[0:rows, 0:rows])
                ins.then_inc(p_turned, 1)
            pe.wait_ge(pT_ready, PLE // P)
            pe.wait_ge(wpp_in, 16)
            for t in range(2):
                for k in range(PLE // P):
                    for m in range(2):
                        ins = pe.matmul(bank[2 * t + m][:], pT[:, k, t * P:(t + 1) * P], w_pp[:, k, halves(m)],
                                        start=(k == 0), stop=(k == PLE // P - 1))
                ins.then_inc(pw_made, 1)
            pe.wait_ge(pw_ready, 2)
            for k in range(PLE // P):
                for m in range(2):
                    ins = pe.matmul(bank[0][32 * m:32 * m + NS, :], pT[:, k, SEQ:T], w_pp[:, k, halves(m)],
                                    start=(k == 0), stop=(k == PLE // P - 1), skip_group_check=True)
            ins.then_inc(pw_made, 1)
            turn_rows(2)
            pe.wait_ge(wpg_in, 16)
            pe.wait_ge(pw_ready, 6)
            for t in range(2):
                for k in range(KD):
                    wait_nT(2, k)
                    for m in range(2):
                        ins = pe.matmul(bank[2 * t + m][:], nT[:, k, t * P:(t + 1) * P], w_pg[:, k, halves(m)],
                                        start=(k == 0), stop=(k == KD - 1))
                ins.then_inc(plegate_made, 1)
            small_tile(bank[4], lambda k: nT[:, k, SEQ:T], w_pg, KD).then_inc(plegate_made, 1)


_INS = ["x_prompt", "x_sample", "state_conv", "state_lru", "p_prompt", "p_sample", "g_mix", "w_in", "g_v", "w_s",
        "b_s", "conv_w", "conv_b", "w_a", "b_a", "w_x", "b_x", "lam", "g_oa", "g_ob", "w_out", "g_ffn", "w_r",
        "b_r", "w1", "b1", "w2", "b2", "g_ple", "w_pg", "b_pg", "w_pp", "g_final"]


def kernel(**inputs):
    import numpy as np
    import concourse.bacc as bacc
    from concourse.bass_utils import run_bass_kernel_spmd

    nc = bacc.Bacc("TRN2", target_bir_lowering=False, num_devices=1)
    arrays, ins, outs = {}, {}, {}
    for name in _INS:
        x = np.ascontiguousarray(inputs[name])
        arrays[f"in_{name}"] = x
        ins[name] = nc.dram_tensor(f"in_{name}", x.shape, mybir.dt.from_np(x.dtype), kind="ExternalInput").ap()
    depth, samples, past, lru = inputs["state_conv"].shape
    chunk = inputs["w_s"].shape[2]
    gmlp = inputs["g_v"].shape[1]
    prompts = inputs["x_prompt"].shape[0]
    shapes = {
        "y_prompt": inputs["x_prompt"].shape,
        "y_sample": inputs["x_sample"].shape,
        "v_prompt": (depth, prompts, chunk, gmlp),
        "conv_prompt": (depth, prompts, past, lru),
        "lru_prompt": (depth, prompts, lru),
        "v_sample": (depth, samples, 1, gmlp),
        "conv_sample": (depth, samples, past, lru),
        "lru_sample": (depth, samples, lru),
    }
    for name, shape in shapes.items():
        outs[name] = nc.dram_tensor(f"out_{name}", shape, F32, kind="ExternalOutput").ap()
    decode_step(nc, ins, outs)
    r = run_bass_kernel_spmd(nc, [arrays], core_ids=[0])
    return tuple(r.results[0][f"out_{name}"] for name in shapes)
```

```python
from contextlib import ExitStack

import concourse.bass as bass
from concourse import mybir

ALU = mybir.AluOpType
ACT = mybir.ActivationFunctionType
AX = mybir.AxisListType
F32 = mybir.dt.float32
BF16 = mybir.dt.bfloat16
I32 = mybir.dt.int32

P = 128

VECTOR_ROWS = {"g_mix": (0, 8), "g_ffn": (8, 8), "g_ple": (16, 8), "conv_w": (24, 16), "conv_b": (40, 4),
               "lam": (44, 4), "b_a": (48, 4), "b_x": (52, 4), "g_oa": (56, 4), "g_ob": (60, 4)}
N_VECTOR_ROWS = 64


def decode_step(nc, a, out):
    SEQ, D = a["x_prompt"].shape[1:]
    NS = a["x_sample"].shape[0]
    DL = a["state_lru"].shape[2]
    NE, FF2 = a["w1"].shape[1], a["w1"].shape[3]
    FF = FF2 // 2
    PLE = a["w_pp"].shape[1]
    TAPS = a["conv_w"].shape[1]
    HEADS, HD = a["w_a"].shape[1], a["w_a"].shape[2]
    GROUPS = a["w_s"].shape[1]
    EPS = 1e-6
    LRU_C = 8.0
    LIMIT, ALPHA = 7.0, 1.702
    TOP_K = 4
    T = SEQ + NS
    TILES = [(t, P) for t in range(SEQ // P)] + [(SEQ // P, NS)]
    NT = len(TILES)
    KD = D // P
    NB = DL // P
    HALF = 512
    assert D == 2 * HALF and FF == D and SEQ == 2 * P and GROUPS == NB and HD * 2 == P

    CAP = 64
    MAX_ROUNDS = -(-T // CAP)
    STEPS = NE * MAX_ROUNDS
    W1_SLOTS, W2_SLOTS = KD, FF // P // 2
    SLOTS = W1_SLOTS + W2_SLOTS
    MIX_ORDER, MIX_BANKS = (0, 2, 1), (0, 2, 4)
    GATE_ORDER, GATE_BANKS = (0, 2, 1), (6, 0, 2)
    TURN_BANKS = ((4, 5, 6, 7), (5, 6, 7, 0), (2, 3, 4, 5))
    PARTS = 3

    with ExitStack() as ctx:
        def sb(name, shape, dt=F32, stack=ctx):
            return stack.enter_context(nc.sbuf_tensor(name, shape, dt))

        def sem(name):
            return ctx.enter_context(nc.semaphore(name))

        bank = [ctx.enter_context(nc.psum_tensor(f"bank{i}", [P, HALF], F32)) for i in range(8)]

        ring = sb("ring", [P, SLOTS, FF2])
        h = sb("h", [P, NT, D])
        hn = sb("hn", [P, NT, D])
        nT = sb("nT", [P, KD, T])
        b1_parts = sb("b1_parts", [P, FF2], BF16)
        ident = sb("ident", [P, P])
        head_sum = sb("head_sum", [P, NB, 2 * NB])
        group_sum = sb("group_sum", [P, GROUPS, GROUPS])
        ones_b = sb("ones_b", [P, P], BF16)
        before_b = sb("before_b", [P, P], BF16)
        slot_no = sb("slot_no", [P, 2 * CAP])
        expert_pick = sb("expert_pick", [P, STEPS + 1], BF16)
        vecT = sb("vecT", [P, N_VECTOR_ROWS])
        pos = sb("pos", [P, NT, STEPS + 1])
        share = sb("share", [P, NT, STEPS + 1])
        eps_col = sb("eps_col", [P, 1])
        sumsq = sb("sumsq", [P, NT])
        squares = sb("squares", [P, 2])
        rms = sb("rms", [P, NT])
        rstd = sb("rstd", [P, NT])
        n_steps = sb("n_steps", [P, 2], I32)
        y = sb("y", [P, HALF])

        early = ExitStack()
        xpad = sb("xpad", [P, NB, 3 + SEQ + 4 * NS], stack=early)
        conv = sb("conv", [P, NB, SEQ + 4 * NS], stack=early)
        early.close()
        mix = ExitStack()
        NL = NE + TOP_K
        router_words = NT * (2 * NL + 5 * NE + NE // 2 + 8 + 2) + 8 + NT * PLE + 800 + 64
        lg = sb("lg", [P, NT, NL], stack=mix)
        top = sb("top", [P, NT, 8], stack=mix)
        left = sb("left", [P, NT, NL], stack=mix)
        picked = sb("picked", [P, NT, NE], stack=mix)
        picked_b = sb("picked_b", [P, NT, NE], BF16, stack=mix)
        ex = sb("ex", [P, NT, NE], stack=mix)
        negmax = sb("negmax", [P, NT], stack=mix)
        exsum = sb("exsum", [P, NT], stack=mix)
        cw = sb("cw", [P, NT, NE], stack=mix)
        lg_raw = sb("lg_raw", [P, NT, NE], stack=mix)
        slot1 = sb("slot1", [P, NT, NE], stack=mix)
        rounds = sb("rounds", [P, 8], stack=mix)
        p_rows = sb("p_rows", [P, NT, PLE], stack=mix)
        sb("rest_of_early", [P, 800], stack=mix)
        xc = sb("xc", [P, NB, T], stack=mix)
        yb = sb("yb", [P, NB, T], stack=mix)
        ya = sb("ya", [P, NB, T], stack=mix)
        ug = sb("ug", [P, NB, T], stack=mix)
        rg = sb("rg", [P, NB, T], stack=mix)
        ig = sb("ig", [P, NB, T], stack=mix)
        decay = sb("decay", [P, NB, T], stack=mix)
        th = sb("th", [P, NB, T], stack=mix)
        vt = sb("vt", [P, NT, DL], stack=mix)
        vss = sb("vss", [P, NT, GROUPS], stack=mix)
        ws = sb("ws", [P, GROUPS, P], stack=mix)
        wsT = sb("wsT", [P, GROUPS, P], stack=mix)
        w00 = sb("w00", [P, GROUPS], stack=mix)
        w00_diag = sb("w00_diag", [P, GROUPS, NS], stack=mix)
        bs_rows = sb("bs_rows", [GROUPS, T], stack=mix)
        sums = sb("sums", [2 * NB, T], stack=mix)
        past = sb("past", [32, DL], stack=mix)
        pastT = sb("pastT", [P, NB, 32], stack=mix)
        wab = sb("wab", [P, NB, P], stack=mix)
        wxb = sb("wxb", [P, NB, P], stack=mix)
        gv = sb("gv", [P, DL], stack=mix)
        news = sb("news", [P, NB, 36], stack=mix)
        vrows = sb("vrows", [N_VECTOR_ROWS, P], stack=mix)
        lamt = sb("lamt", [P, 8, NB], stack=mix)
        wr = sb("wr", [P, KD, NE], stack=mix)
        br_row = sb("br_row", [P, NE], stack=mix)
        mix.close()

        moe = ExitStack()
        sb("under_router", [P, router_words], stack=moe)
        x_parts = sb("x_parts", [P, PARTS, 2, D], BF16, stack=moe)
        xs_parts = sb("xs_parts", [P, D], BF16, stack=moe)
        xs_mid = sb("xs_mid", [NS, D], BF16, stack=moe)
        pick = sb("pick", [P, NT, CAP], BF16, stack=moe)
        wpick = sb("wpick", [P, NT, 2 * CAP], stack=moe)
        wpickT = sb("wpickT", [P, T], stack=moe)
        b1_pick = sb("b1_pick", [P, CAP], BF16, stack=moe)
        xgT = sb("xgT", [P, KD, CAP], stack=moe)
        split = ExitStack()
        rest = sb("rest", [P, 2, D], stack=split)
        pT = sb("pT", [P, PLE // P, T], stack=split)
        split.close()
        gmin = sb("gmin", [P, HALF], stack=moe)
        uclip = sb("uclip", [P, HALF], stack=moe)
        sig = sb("sig", [P, HALF], stack=moe)
        gu = sb("gu", [P, HALF], stack=moe)
        act_sb = sb("act_sb", [P, HALF], stack=moe)
        actT = sb("actT", [P, HALF], stack=moe)
        pw = sb("pw", [P, NT, D], stack=moe)
        bpg = sb("bpg", [P, D], stack=moe)
        gfin = sb("gfin", [P, D], stack=moe)
        moe.close()
        gate = hn
        y_out = x_parts[:].rearrange("p q t d -> p (q t d)").bitcast(F32).rearrange("p (t d) -> p t d", t=NT)
        b1_rows = hn[0:NE, 0:2, :].rearrange("p t d -> p (t d)")
        b1_mid = hn[0:NE, 2, :].bitcast(BF16)
        news_rows = ws[0:36, :, :].rearrange("p g t -> p (g t)")
        head_back = past[0:2 * NB, :]

        w_in = [ring[:, 2 * g:2 * g + 2, :].rearrange("p s n -> p (s n)").rearrange("p (k n) -> p k n", k=KD)
                for g in range(4)]
        w_out = ring[:, W1_SLOTS:SLOTS, :].rearrange("p s n -> p (s n)").rearrange("p (k n) -> p k n", k=KD)
        w_pg = ring[:, 0:4, :].rearrange("p s n -> p (s n)").rearrange("p (k n) -> p k n", k=KD)
        w_pp = ring[:, W1_SLOTS - 1, :].rearrange("p (k n) -> p k n", k=PLE // P)

        x_in = [sem(f"x_in{t}") for t in range(NT)]
        vec_in = sem("vec_in")
        past_in = sem("past_in")
        ws_in = sem("ws_in")
        bs_in = sem("bs_in")
        gates_in = sem("gates_in")
        gv_in = sem("gv_in")
        b1_in = sem("b1_in")
        b2_in = sem("b2_in")
        router_in = sem("router_in")
        win_in = [[sem("win_in0a"), sem("win_in0b")]] + [[sem(f"win_in{g}")] for g in range(1, 4)]
        wout_in = sem("wout_in")
        slot_in = [sem(f"slot_in{j}") for j in range(SLOTS)]
        p_in = sem("p_in")
        wpg_in = [sem(f"wpg_in{j}") for j in range(4)]
        wpp_in = sem("wpp_in")
        rows_in = sem("rows_in")
        stored = sem("stored")
        consts = sem("consts")
        zeroed = sem("zeroed")
        pool_done = sem("pool_done")
        dve_done = sem("dve_done")
        act_done = sem("act_done")
        turned = sem("turned")
        vecT_ready = sem("vecT_ready")
        pastT_ready = sem("pastT_ready")
        wsT_ready = sem("wsT_ready")
        square_mid = sem("square_mid")
        rms_ready = sem("rms_ready")
        hn_ready = sem("hn_ready")
        rows_turned = sem("rows_turned")
        nT_dve = sem("nT_dve")
        nT_act = sem("nT_act")
        z_made = sem("z_made")
        z_taken = sem("z_taken")
        xc_ready = sem("xc_ready")
        gates_made = sem("gates_made")
        gates_taken = sem("gates_taken")
        lru_act = sem("lru_act")
        lam_abs_ready = sem("lam_abs_ready")
        lam_exp_ready = sem("lam_exp_ready")
        decay_ready = sem("decay_ready")
        mult2_ready = sem("mult2_ready")
        mult_ready = sem("mult_ready")
        ybsq_ready = sem("ybsq_ready")
        ybss_made = sem("ybss_made")
        ybrms_ready = sem("ybrms_ready")
        ybrstd_ready = sem("ybrstd_ready")
        ybrstd_made = sem("ybrstd_made")
        yb_ready = sem("yb_ready")
        news_ready = sem("news_ready")
        news_turned = sem("news_turned")
        news_taken = sem("news_taken")
        v_turned = sem("v_turned")
        vsq_ready = sem("vsq_ready")
        vss_ready = sem("vss_ready")
        vrms_ready = sem("vrms_ready")
        vt_ready = sem("vt_ready")
        bs_ready = sem("bs_ready")
        s_made = sem("s_made")
        yasq_ready = sem("yasq_ready")
        yass_made = sem("yass_made")
        yarms_ready = sem("yarms_ready")
        yarstd_ready = sem("yarstd_ready")
        yarstd_made = sem("yarstd_made")
        ya_ready = sem("ya_ready")
        b1_ready = sem("b1_ready")
        mixed_made = sem("mixed_made")
        slots_free = sem("slots_free")
        logits_made = sem("logits_made")
        logits_taken = sem("logits_taken")
        negmax_ready = sem("negmax_ready")
        ex_ready = sem("ex_ready")
        picked_ready = sem("picked_ready")
        places_made = sem("places_made")
        steps_ready = sem("steps_ready")
        parts_h = sem("parts_h")
        parts_r = sem("parts_r")
        parts_ready = sem("parts_ready")
        xs_low_ready = sem("xs_low_ready")
        moe_zeroed = sem("moe_zeroed")
        pick_ready = sem("pick_ready")
        wpick_ready = sem("wpick_ready")
        gathered = sem("gathered")
        xgT_ready = sem("xgT_ready")
        b1_pick_ready = sem("b1_pick_ready")
        gate_made = sem("gate_made")
        gmin_ready = sem("gmin_ready")
        uclip_ready = sem("uclip_ready")
        sig_ready = sem("sig_ready")
        gu_ready = sem("gu_ready")
        act_ready = sem("act_ready")
        act_turned = sem("act_turned")
        actT_ready = sem("actT_ready")
        wpick_turned = sem("wpick_turned")
        wpickT_ready = sem("wpickT_ready")
        y_ready = sem("y_ready")
        spread = sem("spread")
        h_added = sem("h_added")
        p_turned = sem("p_turned")
        pT_ready = sem("pT_ready")
        pw_made = sem("pw_made")
        pw_ready = sem("pw_ready")
        plegate_made = sem("plegate_made")
        plebias_ready = sem("plebias_ready")
        plegate_ready = sem("plegate_ready")
        h_final = sem("h_final")
        squares_ready = sem("squares_ready")
        sumsq_ready = sem("sumsq_ready")
        y_final = sem("y_final")

        def vcol(name, k):
            return vecT[:, VECTOR_ROWS[name][0] + k:VECTOR_ROWS[name][0] + k + 1]

        def halves(n):
            return slice(n * HALF, (n + 1) * HALF)

        block = ctx.enter_context(nc.Block())

        @block.sync
        def _(sp):
            def load(dst, src, s, single_elements=False):
                sp.dma_start(dst, src, allow_slow_non_contiguous=single_elements).then_inc(s, 16)

            def load_w_in(g, k0, k1, s):
                c = (2, 1, 3, 0)[g]
                load(w_in[g][:, k0:k1, :],
                     a["w_in"][0].rearrange("(k p) n -> p k n", p=P)[:, k0:k1, c * DL:(c + 1) * DL], s)

            for t in range(2):
                load(h[:, t, :], a["x_prompt"][0][t * P:(t + 1) * P, :], x_in[t])
            load(h[0:NS, 2, :], a["x_sample"].rearrange("b s d -> (b s) d"), x_in[2])
            for name, (r0, n) in VECTOR_ROWS.items():
                src = a[name][0]
                if name in ("b_a", "b_x"):
                    src = src.rearrange("(r q) j -> r (q j)", q=2)
                elif name == "conv_w":
                    src = src.rearrange("k (r j) -> (k r) j", j=P)
                else:
                    src = src.rearrange("(r j) -> r j", j=P)
                load(vrows[r0:r0 + n, :], src, vec_in)
            load_w_in(0, 0, KD // 2, win_in[0][0])
            load(past[0:3 * NS, :], a["state_conv"][0].rearrange("b k d -> (b k) d"), past_in)
            load(past[3 * NS:3 * NS + NS, :], a["state_lru"][0], past_in)
            load_w_in(0, KD // 2, KD, win_in[0][1])
            sp.wait_ge(zeroed, 4)
            for dst, name in ((wab, "w_a"), (wxb, "w_x")):
                src = a[name][0].rearrange("(b q) i j -> q i b j", q=2)
                for q in range(2):
                    load(dst[HD * q:HD * (q + 1), :, HD * q:HD * (q + 1)], src[q], gates_in)
            load_w_in(1, 0, KD, win_in[1][0])
            load(ws[:], a["w_s"][0].rearrange("g t s -> t g s"), ws_in)
            load(gv[:], a["g_v"][0].partition_broadcast(P), gv_in)
            load_w_in(2, 0, KD, win_in[2][0])
            load(bs_rows[:, 0:P], a["b_s"][0], bs_in)
            load(bs_rows[:, P:2 * P], a["b_s"][0], bs_in)
            load(w00[0:NS, :], a["w_s"][0][:, 0, 0].partition_broadcast(NS), bs_in, True)
            load_w_in(3, 0, KD, win_in[3][0])
            sp.wait_ge(rows_turned, KD)
            load(b1_rows, a["b1"][0], b1_in)
            load(wr[:], a["w_r"][0].rearrange("(k p) e -> p k e", p=P), router_in)
            load(br_row[:], a["b_r"][0].partition_broadcast(P), router_in)
            sp.wait_ge(y_ready, 1)
            for m in range(2):
                load(y[CAP * m:CAP * m + NE, :], a["b2"][0][:, halves(m)], b2_in)
            load(w_out, a["w_out"][0].rearrange("(k p) n -> p k n", p=P), wout_in)

            def load_slot(j, e):
                if j < W1_SLOTS:
                    src = a["w1"][0][bass.ds(e, 1)][:, j * P:(j + 1) * P, :].rearrange("e p n -> p (e n)")
                    sp.dma_start(ring[:, j, :], src).then_inc(slot_in[j], 16)
                else:
                    m = j - W1_SLOTS
                    src = a["w2"][0][bass.ds(e, 1)][:, 2 * m * P:(2 * m + 2) * P, :].rearrange(
                        "e (q p) n -> p (e q) n", p=P)
                    sp.dma_start(ring[:, j, :].rearrange("p (q n) -> p q n", q=2), src).then_inc(slot_in[j], 16)

            for j in range(W1_SLOTS - 2):
                sp.wait_ge(z_made, NB * (j // 2 + 1))
                load_slot(j, 0)
            sp.wait_ge(vt_ready, NT)
            load(out["v_prompt"].rearrange("l b t d -> (l b t) d"), vt[:, 1, :], stored)
            load(out["v_sample"].rearrange("l b t d -> (l b t) d"), vt[0:NS, 2, :], stored)
            sp.wait_ge(news_taken, 1)
            lru0 = 3 + 3 * NS
            load(out["conv_prompt"].rearrange("l b k d -> (l b k) d"), news_rows[0:3, :], stored)
            load(out["conv_sample"].rearrange("l b k d -> (l b k) d"), news_rows[3:lru0, :], stored)
            load(out["lru_prompt"].rearrange("l b d -> (l b) d"), news_rows[lru0:lru0 + 1, :], stored)
            load(out["lru_sample"].rearrange("l b d -> (l b) d"), news_rows[lru0 + 1:lru0 + 1 + NS, :], stored)
            load(p_rows[:, 0:2, :], a["p_prompt"][0, 0].rearrange("(t p) d -> p t d", p=P), p_in)
            load(p_rows[0:NS, 2, :], a["p_sample"][0].rearrange("b s d -> (b s) d"), p_in)
            sp.wait_ge(z_made, 4 * NB)
            load(w_pp, a["w_pp"][0].rearrange("(k p) n -> p k n", p=P), wpp_in)
            load_slot(W1_SLOTS - 2, 0)
            sp.wait_ge(mixed_made, NT)
            for j in range(W1_SLOTS, SLOTS):
                load_slot(j, 0)
            sp.wait_ge(h_added, NT)
            sp.wait_ge(stored, 16 * 6)
            load(bpg[:], a["b_pg"][0].partition_broadcast(P), rows_in)
            load(gfin[:], a["g_final"].partition_broadcast(P), rows_in)
            sp.wait_ge(pw_made, NT)
            load_slot(W1_SLOTS - 1, 0)
            with sp.Fori(0, NE - 1) as e:
                for j in range(SLOTS):
                    sp.wait_ge(slots_free, e * SLOTS + j + 1)
                    load_slot(j, e + 1)
            sp.wait_ge(steps_ready, 1)
            more = sp.value_load(n_steps[0:1, 1:2], min_val=0, max_val=STEPS - NE)
            with sp.If(more > 0):
                with sp.Fori(0, more) as i:
                    for j in range(SLOTS):
                        sp.wait_ge(slots_free, (i + (NE - 1)) * SLOTS + j + 1)
                        load_slot(j, i % NE)
            for j in range(4):
                sp.wait_ge(slots_free, (more + (NE - 1)) * SLOTS + j + 1)
                load(w_pg[:, 2 * j:2 * j + 2, :],
                     a["w_pg"][0].rearrange("(k p) n -> p k n", p=P)[:, 2 * j:2 * j + 2, :], wpg_in[j])
            for i, t in enumerate(GATE_ORDER):
                rows = TILES[t][1]
                sp.wait_ge(y_final, i + 1)
                dst = (out["y_prompt"][0][t * P:(t + 1) * P, :] if t < 2
                       else out["y_sample"].rearrange("b s d -> (b s) d"))
                load(dst, y_out[0:rows, t, :], stored)
            sp.wait_ge(stored, 16 * 9)

        @block.gpsimd
        def _(pool):
            pool_count = [0]

            def link(ins):
                pool_count[0] += 1
                ins.then_inc(pool_done, 1)
                pool.wait_ge(pool_done, pool_count[0])
            link(pool.memset(ident[:], 0.0))
            pool.affine_select(out=ident[:], in_=ident[:], compare_op=ALU.not_equal, fill=1.0, base=0,
                               pattern=[[-1, P]], channel_multiplier=1).then_inc(consts, 1)
            link(pool.memset(before_b[:], 1.0))
            pool.affine_select(out=before_b[:], in_=before_b[:], compare_op=ALU.is_gt, fill=0.0, base=0,
                               pattern=[[1, P]], channel_multiplier=-1).then_inc(consts, 1)
            pool.iota(slot_no[:], pattern=[[0, 2], [1, CAP]], base=0, channel_multiplier=0,
                      allow_small_or_imprecise_dtypes=True).then_inc(consts, 1)
            pool.wait_ge(ws_in, 16)
            for g in range(GROUPS):
                pool.affine_select(out=ws[:, g, :], in_=ws[:, g, :], compare_op=ALU.is_ge, fill=0.0, base=0,
                                   pattern=[[-1, P]], channel_multiplier=1).then_inc(consts, 1)
            pool.wait_ge(b1_in, 16)
            link(pool.tensor_copy(b1_parts[0:NE, :], b1_rows))
            link(pool.tensor_tensor(b1_rows, b1_rows, b1_parts[0:NE, :], ALU.subtract))
            link(pool.tensor_copy(b1_mid, b1_rows))
            pool.tensor_copy(b1_parts[NE:2 * NE, :], b1_mid)
            pool.tensor_tensor(b1_parts[2 * NE:3 * NE, :], b1_rows, b1_mid, ALU.subtract).then_inc(b1_ready, 1)
            for t in range(2):
                pool.wait_ge(parts_h, t + 1)
                pool.tensor_tensor(rest[:, t, :], hn[:, t, :], x_parts[:, 0, t, :], ALU.subtract
                                   ).then_inc(parts_r, 1)
            for t in range(2):
                pool.wait_ge(parts_h, 3 + t + 1)
                pool.tensor_tensor(x_parts[:, 2, t, :], rest[:, t, :], x_parts[:, 1, t, :], ALU.subtract
                                   ).then_inc(parts_ready, 1)

        @block.scalar
        def _(act):
            count = [0]

            def link(ins):
                count[0] += 1
                ins.then_inc(act_done, 1)
                act.wait_ge(act_done, count[0])

            def square_rows(t, rows, junk):
                link(act.activation(junk[0:rows, :], h[0:rows, t, :], ACT.Square, accum_out=sumsq[0:rows, t:t + 1]))

            def root_means():
                act.activation(rms[:], sumsq[:], ACT.Sqrt, bias=eps_col[:], scale=1.0 / D).then_inc(rms_ready, 1)

            def take_nT(stage, gain, banks):
                for k in range(1, KD, 2):
                    act.wait_ge(rows_turned, stage * KD + k + 1)
                    act.activation(nT[:, k, :], bank[banks[k % 4]][:, 0:T], ACT.Identity,
                                   scale=vcol(gain, k)).then_inc(nT_act, 1)

            junk0 = ug[:].rearrange("p b t -> p (b t)")[:, 0:D]
            junk1 = th[:].rearrange("p b t -> p (b t)")[:, 0:D]
            act.wait_ge(zeroed, 2)
            for t, rows in (TILES[0], TILES[2]):
                act.wait_ge(x_in[t], 16)
                square_rows(t, rows, junk0)
            act.wait_ge(square_mid, 1)
            root_means()
            act.wait_ge(vecT_ready, 1)
            take_nT(0, "g_mix", TURN_BANKS[0])

            act.wait_ge(zeroed, 5)
            for blk in range(NB):
                z = bank[blk]
                act.wait_ge(z_made, blk + 1)
                act.activation(xpad[:, blk, 3:3 + SEQ], z[:, 0:SEQ], ACT.Copy).then_inc(z_taken, 1)
                act.activation(xpad[:, blk, 3 + SEQ:].rearrange("p (s k) -> p s k", k=4)[:, :, 3], z[:, SEQ:T],
                               ACT.Copy).then_inc(z_taken, 1)
            act.wait_ge(lam_abs_ready, 1)
            act.activation(lamt[:, 2, :], lamt[:, 1, :], ACT.Exp, scale=-1.0).then_inc(lam_exp_ready, 1)
            act.wait_ge(turned, 3)
            act.activation(wsT[:].rearrange("p g t -> p (g t)"), bank[7][:], ACT.Copy).then_inc(wsT_ready, 1)

            def take_gelu(dst, group, blocks):
                for blk in blocks:
                    act.wait_ge(z_made, group * NB + blk + 1)
                    act.activation(dst[:, blk, :], bank[blk][:, 0:T], ACT.Gelu_apprx_tanh).then_inc(z_taken, 2)

            def take_gate(dst, bias, first):
                for blk in range(NB):
                    act.wait_ge(gates_made, first + blk + 1)
                    act.activation(dst[:, blk, :], bank[4 + blk][:, 0:T], ACT.Sigmoid, bias=vcol(bias, blk)
                                   ).then_inc(gates_taken, 1)

            take_gelu(ya, 1, (0, 1))
            take_gate(rg, "b_a", 0)
            take_gelu(ya, 1, (2, 3))
            take_gate(ig, "b_x", NB)
            act.wait_ge(decay_ready, 1)
            act.wait_ge(gates_taken, 2 * NB)
            for blk in range(NB):
                act.activation(decay[:, blk, :], rg[:, blk, :], ACT.Exp, scale=lamt[:, 7, blk:blk + 1]
                               ).then_inc(lru_act, 1)
            for blk in range(NB):
                act.activation(th[:, blk, :], rg[:, blk, :], ACT.Tanh, scale=lamt[:, 6, blk:blk + 1]
                               ).then_inc(lru_act, 1)
            take_gelu(yb, 2, (0,))
            act.wait_ge(mult2_ready, 1)
            act.activation(th[:], th[:], ACT.Sqrt).then_inc(mult_ready, 1)
            for t, rows in TILES:
                act.wait_ge(v_turned, t + 1)
                act.activation(vt[0:rows, t, :], bank[4 + t][0:rows, :], ACT.Square).then_inc(vsq_ready, 1)
            take_gelu(yb, 2, (1, 2))
            act.wait_ge(vss_ready, NT)
            act.activation(vss[:], vss[:], ACT.Sqrt, bias=eps_col[:], scale=1.0 / P).then_inc(vrms_ready, 1)
            take_gelu(yb, 2, (3,))
            act.wait_ge(news_turned, 1)
            act.activation(news_rows[:], bank[7][0:36, :], ACT.Copy).then_inc(news_taken, 1)
            take_gelu(ug, 3, (0,))
            act.wait_ge(ybss_made, 1)
            act.activation(sums[:], bank[7][0:2 * NB, 0:T], ACT.Sqrt, bias=eps_col[0:2 * NB, :], scale=1.0 / HD
                           ).then_inc(ybrms_ready, 1)
            take_gelu(ug, 3, (1, 2, 3))
            act.wait_ge(yass_made, 1)
            act.activation(sums[0:GROUPS, :], bank[4][0:GROUPS, 0:T], ACT.Sqrt, bias=eps_col[0:GROUPS, :],
                           scale=1.0 / P).then_inc(yarms_ready, 1)

            act.wait_ge(yarstd_made, GROUPS)
            for i, t in enumerate(MIX_ORDER[:2]):
                act.wait_ge(h_added, i + 1)
                square_rows(t, TILES[t][1], junk1)
            take_nT(1, "g_ffn", TURN_BANKS[1])
            square_rows(MIX_ORDER[2], P, junk1)
            root_means()
            act.wait_ge(b1_ready, 1)

            def high_part(t, rows):
                act.wait_ge(hn_ready, NT + t + 1)
                act.activation(x_parts[0:rows, 0, t, :] if t < 2 else xs_parts[0:rows, :], hn[0:rows, t, :], ACT.Copy
                               ).then_inc(parts_h, 1)

            act.wait_ge(moe_zeroed, 1)
            high_part(0, P)
            high_part(1, P)
            act.wait_ge(negmax_ready, 1)
            for t in range(NT):
                act.activation(ex[:, t, :], lg[:, t, 0:NE], ACT.Exp, bias=negmax[:, t:t + 1]).then_inc(ex_ready, 1)
            high_part(2, NS)
            for t in range(2):
                act.wait_ge(parts_r, t + 1)
                act.activation(x_parts[:, 1, t, :], rest[:, t, :], ACT.Copy).then_inc(parts_h, 1)
            act.wait_ge(xs_low_ready, 1)
            act.activation(xs_mid[:], hn[0:NS, 2, :], ACT.Copy).then_inc(parts_h, 1)
            act.wait_ge(parts_h, 6)
            act.activation(xs_parts[32:32 + NS, :], xs_mid[:], ACT.Copy).then_inc(parts_h, 1)
            for k in range(PLE // P):
                act.wait_ge(p_turned, k + 1)
                act.activation(pT[:, k, :], bank[4 + k][:, 0:T], ACT.Copy).then_inc(pT_ready, 1)
            act.wait_ge(wpick_turned, 1)
            act.activation(wpickT[:], bank[0][:, 0:T], ACT.Copy).then_inc(wpickT_ready, 1)
            act.wait_ge(stored, 16 * 6)
            for t in range(2):
                for m in range(2):
                    act.wait_ge(pw_made, t + 1)
                    act.activation(pw[:, t, halves(m)], bank[4 + 2 * t + m][:], ACT.Copy).then_inc(pw_ready, 1)
            for m in range(2):
                act.wait_ge(pw_made, NT)
                act.activation(pw[0:NS, 2, halves(m)], bank[1][32 * m:32 * m + NS, :], ACT.Copy).then_inc(pw_ready, 1)

            act.wait_ge(steps_ready, 1)
            n = act.value_load(n_steps[0:1, 0:1], min_val=NE, max_val=STEPS)
            with act.Fori(0, n) as i:
                act.wait_ge(gmin_ready, i + 1)
                act.activation(sig[:], gmin[:], ACT.Sigmoid, scale=ALPHA).then_inc(sig_ready, 1)
                act.wait_ge(act_turned, i + 1)
                act.activation(actT[:], bank[3][:], ACT.Copy).then_inc(actT_ready, 1)
                act.wait_ge(wpick_turned, i + 2)
                act.activation(wpickT[:], bank[0][:, 0:T], ACT.Copy).then_inc(wpickT_ready, 1)
                act.wait_ge(slots_free, (i + 1) * SLOTS)
                act.activation(y[:], bank[2][:], ACT.Copy).then_inc(y_ready, 1)

            for t, rows in TILES:
                act.wait_ge(h_added, n * (2 * NT) + NT + 2 * t + 2)
                square_rows(t, rows, y_out[:, t, :])
            root_means()
            take_nT(2, "g_ple", TURN_BANKS[2])
            for i, t in enumerate(GATE_ORDER):
                rows = TILES[t][1]
                for m in range(2):
                    act.wait_ge(plebias_ready, 2 * i + m + 1)
                    act.activation(gate[0:rows, t, halves(m)], gate[0:rows, t, halves(m)], ACT.Sigmoid
                                   ).then_inc(plegate_ready, 1)
                for m in range(2):
                    act.wait_ge(h_final, 2 * i + m + 1)
                    act.activation(y_out[0:rows, t, halves(m)], h[0:rows, t, halves(m)], ACT.Square,
                                   accum_out=squares[0:rows, m:m + 1]).then_inc(squares_ready, 1)
                act.wait_ge(sumsq_ready, i + 1)
                act.activation(rms[0:rows, t:t + 1], sumsq[0:rows, t:t + 1], ACT.Sqrt, bias=eps_col[0:rows, :],
                               scale=1.0 / D).then_inc(rms_ready, 1)

        @block.vector
        def _(dve):
            count = [0]

            def link(ins):
                count[0] += 1
                ins.then_inc(dve_done, 1)
                dve.wait_ge(dve_done, count[0])

            dve.memset(eps_col[:], EPS).then_inc(zeroed, 1)
            dve.memset(sumsq[:], 1.0).then_inc(zeroed, 1)
            dve.memset(wab[:], 0.0).then_inc(zeroed, 1)
            dve.memset(wxb[:], 0.0).then_inc(zeroed, 1)
            dve.memset(xpad[:], 0.0).then_inc(zeroed, 1)
            dve.wait_ge(zeroed, 2)
            dve.wait_ge(x_in[1], 16)
            junk = rg[:].rearrange("p b t -> p (b t)")[:, 0:D]
            dve.scalar_tensor_tensor(out=junk, in0=h[:, 1, :], scalar=1.0, in1=h[:, 1, :], op0=ALU.mult,
                                     op1=ALU.mult, accum_out=sumsq[:, 1:2]).then_inc(square_mid, 1)
            dve.memset(vss[:], 1.0)
            dve.memset(ones_b[:], 1.0)
            dve.memset(y[:], 0.0).then_inc(y_ready, 1)
            link(dve.memset(head_sum[:], 0.0))
            link(dve.memset(group_sum[:], 0.0))
            for blk in range(NB):
                dve.memset(group_sum[:, blk, blk:blk + 1], 1.0)
                for q in range(2):
                    j = 2 * blk + q
                    dve.memset(head_sum[HD * q:HD * (q + 1), blk, j:j + 1], 1.0)
            dve.memset(pos[:], -1.0)
            link(dve.memset(share[:], 0.0)) 

            dve.wait_ge(turned, 1)
            dve.tensor_copy(vecT[:], bank[0][:, 0:N_VECTOR_ROWS]).then_inc(vecT_ready, 1)

            def norm_rows():
                for t, rows in TILES:
                    dve.tensor_scalar(hn[0:rows, t, :], h[0:rows, t, :], rstd[0:rows, t:t + 1], None, ALU.mult
                                      ).then_inc(hn_ready, 1)

            def take_nT(stage, gain, banks):
                for k in range(0, KD, 2):
                    dve.wait_ge(rows_turned, stage * KD + k + 1)
                    dve.tensor_scalar(nT[:, k, :], bank[banks[k % 4]][:, 0:T], vcol(gain, k), None, ALU.mult
                                      ).then_inc(nT_dve, 1)

            dve.wait_ge(rms_ready, 1)
            link(dve.reciprocal(rstd[:], rms[:]))
            norm_rows()
            dve.wait_ge(vecT_ready, 1)
            take_nT(0, "g_mix", TURN_BANKS[0])

            dve.wait_ge(turned, 2)
            dve.tensor_copy(pastT[:].rearrange("p b r -> p (b r)"), bank[1][:, 0:NB * 32]).then_inc(pastT_ready, 1)
            dve.wait_ge(pastT_ready, 1)
            sam = xpad[:, :, 3 + SEQ:].rearrange("p b (s k) -> p b s k", k=4)
            for blk in range(NB):
                link(dve.tensor_copy(sam[:, blk, :, 0:3],
                                     pastT[:, blk, 0:3 * NS].rearrange("p (s k) -> p s k", k=3)))

            L = [lamt[:, j, :] for j in range(8)]
            lam = vecT[:, VECTOR_ROWS["lam"][0]:VECTOR_ROWS["lam"][0] + NB]
            link(dve.tensor_scalar(L[0], lam, -1.0, None, ALU.mult))
            link(dve.tensor_tensor(L[1], lam, L[0], ALU.max))
            dve.tensor_scalar(L[0], L[0], 0.0, None, ALU.max).then_inc(lam_abs_ready, 1)
            for blk in range(NB):
                dve.wait_ge(z_taken, 2 * (blk + 1))
                width = SEQ + 4 * NS
                link(dve.tensor_scalar(conv[:, blk, :], xpad[:, blk, 0:width], vcol("conv_w", blk),
                                       vcol("conv_b", blk), ALU.mult, ALU.add))
                for k in range(1, TAPS - 1):
                    link(dve.scalar_tensor_tensor(out=conv[:, blk, :], in0=xpad[:, blk, k:k + width],
                                                  scalar=vcol("conv_w", k * NB + blk), in1=conv[:, blk, :],
                                                  op0=ALU.mult, op1=ALU.add))
                k = TAPS - 1
                dve.scalar_tensor_tensor(out=xc[:, blk, 0:SEQ], in0=xpad[:, blk, k:k + SEQ],
                                         scalar=vcol("conv_w", k * NB + blk), in1=conv[:, blk, 0:SEQ],
                                         op0=ALU.mult, op1=ALU.add)
                dve.scalar_tensor_tensor(out=xc[:, blk, SEQ:T], in0=sam[:, blk, :, k],
                                         scalar=vcol("conv_w", k * NB + blk),
                                         in1=conv[:, blk, SEQ:width].rearrange("p (s k) -> p s k", k=4)[:, :, k],
                                         op0=ALU.mult, op1=ALU.add).then_inc(xc_ready, 1)

            dve.wait_ge(lam_exp_ready, 1)
            link(dve.tensor_scalar(L[3], L[2], 2.0, None, ALU.add))
            link(dve.reciprocal(L[3], L[3]))
            link(dve.tensor_tensor(L[2], L[2], L[3], ALU.mult))
            link(dve.tensor_tensor(L[3], L[2], L[2], ALU.mult))
            link(dve.memset(L[4], 1.0 / 17))
            for odd in range(15, 0, -2):
                link(dve.tensor_tensor(L[4], L[4], L[3], ALU.mult))
                link(dve.tensor_scalar(L[4], L[4], 1.0 / odd, None, ALU.add))
            link(dve.tensor_tensor(L[4], L[4], L[2], ALU.mult))
            link(dve.scalar_tensor_tensor(out=L[5], in0=L[4], scalar=2.0, in1=L[0], op0=ALU.mult, op1=ALU.add))
            link(dve.tensor_scalar(L[6], L[5], LRU_C, None, ALU.mult))
            dve.tensor_scalar(L[7], L[5], -LRU_C, None, ALU.mult).then_inc(decay_ready, 1)
            dve.wait_ge(bs_in, 48)
            dve.wait_ge(consts, 1)
            for g in range(GROUPS):
                dve.tensor_scalar(w00_diag[0:NS, g, :], ident[0:NS, 0:NS], w00[0:NS, g:g + 1], None, ALU.mult)
            dve.tensor_copy(head_back.rearrange("p (j d) -> p j d", j=2 * NB),
                            ident[0:2 * NB, 0:2 * NB].unsqueeze(2).to_broadcast([2 * NB, 2 * NB, HD]))
            dve.tensor_scalar(bs_rows[:, SEQ:T], ones_b[0:GROUPS, 0:NS], bs_rows[:, 0:1], None, ALU.mult
                              ).then_inc(bs_ready, 1)
            for r in range(MAX_ROUNDS):
                for q in range(PARTS):
                    dve.tensor_copy(expert_pick[NE * q:NE * (q + 1), r * NE:(r + 1) * NE], ident[0:NE, 0:NE])
            link(dve.memset(expert_pick[0:PARTS * NE, STEPS:STEPS + 1], 0.0))

            dve.wait_ge(gates_taken, 2 * NB)
            dve.tensor_tensor(ig[:], ig[:], xc[:], ALU.mult)
            dve.wait_ge(lru_act, NB)
            a2 = conv[:, :, 0:T]
            link(dve.tensor_tensor(a2, decay[:], decay[:], ALU.mult))
            dve.wait_ge(lru_act, 2 * NB)
            dve.scalar_tensor_tensor(out=th[:], in0=a2, scalar=1.0, in1=th[:], op0=ALU.add,
                                     op1=ALU.mult).then_inc(mult2_ready, 1)
            dve.wait_ge(mult_ready, 1)
            link(dve.memset(th[:, :, 0:1], 1.0))
            link(dve.tensor_tensor(ig[:], ig[:], th[:], ALU.mult))
            for blk in range(NB):
                dve.tensor_tensor_scan(rg[:, blk, 0:SEQ], decay[:, blk, 0:SEQ], ig[:, blk, 0:SEQ], 0.0,
                                       ALU.mult, ALU.add)
            link(dve.tensor_tensor(rg[:, :, SEQ:T], decay[:, :, SEQ:T], pastT[:, :, 3 * NS:4 * NS], ALU.mult))
            link(dve.tensor_tensor(rg[:, :, SEQ:T], rg[:, :, SEQ:T], ig[:, :, SEQ:T], ALU.add))

            for t, rows in TILES:
                dve.wait_ge(vsq_ready, t + 1)
                dve.tensor_reduce(vss[0:rows, t, :], vt[0:rows, t, :].rearrange("p (g d) -> p g d", g=GROUPS),
                                  AX.X, ALU.add).then_inc(vss_ready, 1)
            dve.tensor_copy(news[:, :, 0:3], xpad[:, :, SEQ:SEQ + 3])
            for blk in range(NB):
                dve.tensor_copy(news[:, blk, 3:3 + 3 * NS].rearrange("p (s k) -> p s k", k=3), sam[:, blk, :, 1:4])
            dve.tensor_copy(news[:, :, 3 + 3 * NS:4 + 4 * NS], rg[:, :, SEQ - 1:T]).then_inc(news_ready, 1)
            dve.wait_ge(vrms_ready, 1)
            dve.wait_ge(gv_in, 16)
            link(dve.reciprocal(vss[:], vss[:]))
            for t, rows in TILES:
                for g in range(GROUPS):
                    cols = slice(g * P, (g + 1) * P)
                    ins = dve.scalar_tensor_tensor(out=vt[0:rows, t, cols], in0=bank[4 + t][0:rows, cols],
                                                   scalar=vss[0:rows, t, g:g + 1], in1=gv[0:rows, cols],
                                                   op0=ALU.mult, op1=ALU.mult)
                ins.then_inc(vt_ready, 1)

            dve.wait_ge(z_taken, 2 * 3 * NB)
            link(dve.tensor_tensor(yb[:], rg[:], yb[:], ALU.mult))
            dve.tensor_tensor(ig[:], yb[:], yb[:], ALU.mult).then_inc(ybsq_ready, 1)
            dve.wait_ge(ybrms_ready, 1)
            dve.reciprocal(sums[:], sums[:]).then_inc(ybrstd_ready, 1)
            for blk in range(NB):
                dve.wait_ge(ybrstd_made, blk + 1)
                dve.scalar_tensor_tensor(out=yb[:, blk, :], in0=yb[:, blk, :], scalar=vcol("g_ob", blk),
                                         in1=bank[4 + blk][:, 0:T], op0=ALU.mult, op1=ALU.mult).then_inc(yb_ready, 1)

            for g in range(GROUPS):
                dve.wait_ge(s_made, g + 1)
                dve.wait_ge(z_taken, 2 * (3 * NB + g + 1))
                link(dve.tensor_tensor(ya[:, g, :], bank[4 + g][:, 0:T], ug[:, g, :], ALU.mult))
                dve.tensor_tensor(xc[:, g, :], ya[:, g, :], ya[:, g, :], ALU.mult).then_inc(yasq_ready, 1)
            dve.memset(lg[:], 0.0)
            link(dve.memset(lg_raw[:], 0.0))
            link(dve.memset(lg[:, :, NE:NL], 3.0e38))
            dve.wait_ge(yarms_ready, 1)
            dve.reciprocal(sums[0:GROUPS, :], sums[0:GROUPS, :]).then_inc(yarstd_ready, 1)
            for g in range(GROUPS):
                dve.wait_ge(yarstd_made, g + 1)
                dve.scalar_tensor_tensor(out=ya[:, g, :], in0=ya[:, g, :], scalar=vcol("g_oa", g),
                                         in1=bank[4 + g][:, 0:T], op0=ALU.mult, op1=ALU.mult).then_inc(ya_ready, 1)

            for i, t in enumerate(MIX_ORDER):
                dve.wait_ge(mixed_made, i + 1)
                if t < 2:
                    for m in range(2):
                        ins = dve.tensor_tensor(h[:, t, halves(m)], bank[MIX_BANKS[t] + m][:], h[:, t, halves(m)],
                                                ALU.add)
                else:
                    for q in range(2):
                        for m in range(2):
                            r0 = 32 * (2 * q + m)
                            ins = dve.tensor_tensor(h[0:NS, 2, halves(m)], bank[MIX_BANKS[t]][r0:r0 + NS, :],
                                                    h[0:NS, 2, halves(m)], ALU.add)
                            if q == 0:
                                link(ins)
                ins.then_inc(h_added, 1)

            take_nT(1, "g_ffn", TURN_BANKS[1])
            dve.wait_ge(rms_ready, 2)
            link(dve.reciprocal(rstd[:], rms[:]))
            dve.wait_ge(b1_ready, 1)
            dve.wait_ge(logits_made, 1)
            dve.wait_ge(router_in, 32)
            for t, rows in TILES:
                ins = dve.scalar_tensor_tensor(out=lg[0:rows, t, 0:NE], in0=bank[1 + t][0:rows, 0:NE],
                                               scalar=rstd[0:rows, t:t + 1], in1=br_row[0:rows, :], op0=ALU.mult,
                                               op1=ALU.add)
            link(ins)
            for t in range(NT):
                link(dve.max(top[:, t, :], lg[:, t, :]))
            dve.tensor_scalar(negmax[:], top[:, :, TOP_K], -1.0, None, ALU.mult).then_inc(negmax_ready, 1)
            for t in range(NT):
                link(dve.match_replace(left[:, t, :], top[:, t, :], lg[:, t, :], -3.0e38))
            link(dve.tensor_tensor(picked[:], left[:, :, 0:NE], lg[:, :, 0:NE], ALU.is_lt))
            dve.tensor_copy(picked_b[:], picked[:]).then_inc(picked_ready, 1)
            dve.memset(xs_parts[:], 0.0).then_inc(moe_zeroed, 1)
            norm_rows()
            dve.memset(wpick[:], 0.0)
            dve.wait_ge(ex_ready, NT)
            link(dve.tensor_tensor(cw[:], ex[:], picked[:], ALU.mult))
            link(dve.tensor_reduce(exsum[:], cw[:], AX.X, ALU.add))
            link(dve.reciprocal(exsum[:], exsum[:]))
            for t in range(NT):
                ins = dve.tensor_scalar(cw[:, t, :], cw[:, t, :], exsum[:, t:t + 1], None, ALU.mult)
            link(ins)
            for m in range(2):
                ins = dve.tensor_copy(wpick[:, :, CAP * m:CAP * m + NE], cw[:])
            ins.then_inc(wpick_ready, 1)

            dve.wait_ge(places_made, 1)
            dve.tensor_copy(slot1[:, 0:2, :], bank[2][:, 0:2 * NE].rearrange("p (t e) -> p t e", t=2))
            link(dve.tensor_copy(slot1[0:NS, 2, :], bank[2][0:NS, 2 * NE:3 * NE]))
            for rows, tt in ((P, slice(0, 2)), (NS, slice(2, 3))):
                link(dve.scalar_tensor_tensor(out=slot1[0:rows, tt, :], in0=slot1[0:rows, tt, :], scalar=1.0,
                                              in1=picked[0:rows, tt, :], op0=ALU.add, op1=ALU.mult))

            def make_places(r):
                cols = slice(r * NE, (r + 1) * NE)
                shift = -1.0 - CAP * r
                for q in range(PARTS):
                    dve.tensor_scalar(pos[32 * q:32 * q + NS, 2, cols], slot1[0:NS, 2, :], shift, None, ALU.add)
                dve.tensor_copy(share[:, 0:2, cols], cw[:, 0:2, :])
                dve.tensor_copy(share[0:NS, 2, cols], cw[0:NS, 2, :])
                link(dve.tensor_scalar(pos[:, 0:2, cols], slot1[:, 0:2, :], shift, None, ALU.add))

            def make_pick(step):
                for t, rows in ((0, P), (1, P), (2, PARTS * 32)):
                    ins = dve.tensor_scalar(pick[0:rows, t, :], slot_no[0:rows, 0:CAP],
                                            pos[0:rows, t, bass.ds(step, 1)], None, ALU.is_equal)
                ins.then_inc(pick_ready, 1)

            def make_b1_pick(step):
                dve.tensor_scalar(b1_pick[0:PARTS * NE, :], ones_b[0:PARTS * NE, 0:CAP],
                                  expert_pick[0:PARTS * NE, bass.ds(step, 1)], None, ALU.mult
                                  ).then_inc(b1_pick_ready, 1)

            def make_xgT(step):
                dve.wait_ge(gathered, step + 1)
                dve.tensor_tensor(xgT[:], bank[3][:].rearrange("p (k s) -> p k s", k=KD),
                                  g_ffn_wide, ALU.mult).then_inc(xgT_ready, 1)

            g0 = VECTOR_ROWS["g_ffn"][0]
            g_ffn_wide = vecT[:, g0:g0 + KD].unsqueeze(2).to_broadcast([P, KD, CAP])
            make_places(0)
            dve.wait_ge(consts, 3)
            make_pick(0)
            make_b1_pick(0)
            dve.wait_ge(parts_h, 3)
            dve.tensor_tensor(hn[0:NS, 2, :], hn[0:NS, 2, :], xs_parts[0:NS, :], ALU.subtract
                              ).then_inc(xs_low_ready, 1)
            link(dve.tensor_reduce(rounds[:, 0:1], bank[3][:, 0:NE], AX.X, ALU.max))
            for r in range(1, MAX_ROUNDS):
                dve.memset(rounds[:, r:r + 1], float(CAP * r))
            link(dve.memset(rounds[:, 6:7], 0.0))
            link(dve.tensor_scalar(rounds[:, 1:MAX_ROUNDS], rounds[:, 1:MAX_ROUNDS], rounds[:, 0:1], None, ALU.is_lt))
            link(dve.tensor_reduce(rounds[:, 6:7], rounds[:, 1:MAX_ROUNDS], AX.X, ALU.add))
            dve.tensor_scalar(n_steps[:, 0:1], rounds[:, 6:7], float(NE), float(NE), ALU.mult, ALU.add)
            dve.tensor_scalar(n_steps[:, 1:2], rounds[:, 6:7], float(NE), None, ALU.mult).then_inc(steps_ready, 1)
            dve.wait_ge(parts_h, 6)
            dve.wait_ge(xs_low_ready, 1)
            dve.tensor_tensor(xs_parts[64:64 + NS, :], hn[0:NS, 2, :], xs_mid[:], ALU.subtract
                              ).then_inc(xs_low_ready, 1)
            for r in range(1, MAX_ROUNDS):
                make_places(r)
            make_xgT(0)

            def add_tile(t, rows, first_bank, products, added):
                dve.wait_ge(spread, products)
                dve.wait_ge(h_added, added)
                for m in range(2):
                    src = bank[first_bank + m]
                    dve.tensor_tensor(h[0:rows, t, halves(m)], src[0:rows, :], h[0:rows, t, halves(m)], ALU.add
                                      ).then_inc(h_added, 1)

            dve.wait_ge(steps_ready, 1)
            n = dve.value_load(n_steps[0:1, 0:1], min_val=NE, max_val=STEPS)
            with dve.Fori(0, n) as i:
                dve.wait_ge(gathered, i + 1)
                make_pick(i + 1)
                dve.wait_ge(slots_free, i * SLOTS + 1)
                for t, rows in TILES:
                    ins = dve.tensor_scalar(wpick[0:rows, t, :], slot_no[0:rows, :],
                                            pos[0:rows, t, bass.ds(i, 1)], share[0:rows, t, bass.ds(i, 1)],
                                            ALU.is_equal, ALU.mult)
                ins.then_inc(wpick_ready, 1)
                dve.wait_ge(gate_made, i + 1)
                dve.tensor_scalar(gmin[:], bank[0][:], LIMIT, None, ALU.min).then_inc(gmin_ready, 1)
                dve.wait_ge(slots_free, i * SLOTS + W1_SLOTS)
                dve.tensor_scalar(uclip[:], bank[1][:], LIMIT, -LIMIT, ALU.min, ALU.max).then_inc(uclip_ready, 1)
                make_b1_pick(i + 1)
                add_tile(0, P, 4, i * NT + 1, i * 2 * NT + NT)
                dve.wait_ge(gmin_ready, i + 1)
                dve.wait_ge(uclip_ready, i + 1)
                dve.scalar_tensor_tensor(out=gu[:], in0=uclip[:], scalar=1.0, in1=gmin[:], op0=ALU.add,
                                         op1=ALU.mult).then_inc(gu_ready, 1)
                dve.wait_ge(sig_ready, i + 1)
                dve.wait_ge(gu_ready, i + 1)
                dve.tensor_tensor(act_sb[:], gu[:], sig[:], ALU.mult).then_inc(act_ready, 1)
                make_xgT(i + 1)
                add_tile(1, P, 6, i * NT + 2, i * 2 * NT + NT + 2)
                add_tile(2, NS, 4, i * NT + 3, i * 2 * NT + NT + 4)
            add_tile(0, P, 4, n * NT + 1, n * 2 * NT + NT)
            add_tile(1, P, 6, n * NT + 2, n * 2 * NT + NT + 2)
            add_tile(2, NS, 0, n * NT + 3, n * 2 * NT + NT + 4)

            take_nT(2, "g_ple", TURN_BANKS[2])
            dve.wait_ge(rms_ready, 3)
            link(dve.reciprocal(rstd[:], rms[:]))
            dve.wait_ge(rows_in, 32)
            dve.wait_ge(pw_ready, 2 * NT)
            for i, t in enumerate(GATE_ORDER):
                rows = TILES[t][1]
                for m in range(2):
                    dve.wait_ge(plegate_made, 2 * i + m + 1)
                    src = bank[GATE_BANKS[t] + m][:] if t < 2 else bank[GATE_BANKS[t]][32 * m:32 * m + NS, :]
                    ins = dve.scalar_tensor_tensor(out=gate[0:rows, t, halves(m)], in0=src,
                                                   scalar=rstd[0:rows, t:t + 1], in1=bpg[0:rows, halves(m)],
                                                   op0=ALU.mult, op1=ALU.add)
                    if t == 2:
                        link(ins)
                        ins = dve.scalar_tensor_tensor(out=gate[0:NS, t, halves(m)],
                                                       in0=bank[GATE_BANKS[t]][64 + 32 * m:64 + 32 * m + NS, :],
                                                       scalar=rstd[0:NS, t:t + 1], in1=gate[0:NS, t, halves(m)],
                                                       op0=ALU.mult, op1=ALU.add)
                    ins.then_inc(plebias_ready, 1)
                for m in range(2):
                    dve.wait_ge(plegate_ready, 2 * i + m + 1)
                    link(dve.tensor_tensor(gate[0:rows, t, halves(m)], gate[0:rows, t, halves(m)],
                                           pw[0:rows, t, halves(m)], ALU.mult))
                    dve.tensor_tensor(h[0:rows, t, halves(m)], gate[0:rows, t, halves(m)], h[0:rows, t, halves(m)],
                                      ALU.add).then_inc(h_final, 1)
                dve.wait_ge(squares_ready, 2 * i + 2)
                dve.tensor_tensor(sumsq[0:rows, t:t + 1], squares[0:rows, 0:1], squares[0:rows, 1:2], ALU.add
                                  ).then_inc(sumsq_ready, 1)
                dve.wait_ge(rms_ready, 3 + i + 1)
                link(dve.reciprocal(rstd[0:rows, t:t + 1], rms[0:rows, t:t + 1]))
                dve.scalar_tensor_tensor(out=y_out[0:rows, t, :], in0=h[0:rows, t, :], scalar=rstd[0:rows, t:t + 1],
                                         in1=gfin[0:rows, :], op0=ALU.mult, op1=ALU.mult).then_inc(y_final, 1)

        @block.tensor
        def _(pe):
            def turn_tile(src, k, t, rows, banks):
                return pe.transpose(bank[banks[k % 4]][:, t * P:t * P + rows], src[0:rows, t, k * P:(k + 1) * P],
                                    ident[0:rows, 0:rows])

            def turn_chunk(src, stage, k, tiles):
                if k >= 4:
                    pe.wait_ge(nT_act if k % 2 else nT_dve, stage * (KD // 2) + (k - 4) // 2 + 1)
                for t in tiles:
                    ins = turn_tile(src, k, t, TILES[t][1], TURN_BANKS[stage])
                ins.then_inc(rows_turned, 1)

            def wait_nT(stage, k):
                pe.wait_ge(nT_act if k % 2 else nT_dve, stage * (KD // 2) + k // 2 + 1)

            pe.wait_ge(consts, 1)
            pe.wait_ge(vec_in, 16 * len(VECTOR_ROWS))
            pe.transpose(bank[0][:, 0:N_VECTOR_ROWS], vrows[:], ident[0:N_VECTOR_ROWS, 0:N_VECTOR_ROWS]
                         ).then_inc(turned, 1)
            pe.wait_ge(hn_ready, NT)
            for k in range(KD):
                turn_chunk(hn, 0, k, range(NT))
            pe.wait_ge(past_in, 32)
            for blk in range(NB):
                ins = pe.transpose(bank[1][:, blk * 32:(blk + 1) * 32], past[:, blk * P:(blk + 1) * P],
                                   ident[0:32, 0:32])
            ins.then_inc(turned, 1)

            def project(b):
                g, blk = b // NB, b % NB
                if b >= 4:
                    pe.wait_ge(z_taken, 2 * (b - 3))
                elif b == 0:
                    pe.wait_ge(vecT_ready, 1)
                elif b == 1:
                    pe.wait_ge(pastT_ready, 1)
                for k in range(KD):
                    if blk == 0 and k % (KD // 2) == 0 and k // (KD // 2) < len(win_in[g]):
                        pe.wait_ge(win_in[g][k // (KD // 2)], 16)
                    wait_nT(0, k)
                    ins = pe.matmul(bank[b % 4][:, 0:T], w_in[g][:, k, blk * P:(blk + 1) * P], nT[:, k, :],
                                    start=(k == 0), stop=(k == KD - 1))
                ins.then_inc(z_made, 1)

            def gates(w, first):
                for blk in range(NB):
                    pe.wait_ge(xc_ready, blk + 1)
                    if first:
                        pe.wait_ge(gates_taken, blk + 1)
                    elif blk == NB - 1:
                        pe.wait_ge(wsT_ready, 1)
                    pe.matmul(bank[4 + blk][:, 0:T], w[:, blk, :], xc[:, blk, :], start=True, stop=True
                              ).then_inc(gates_made, 1)

            for b in range(NB):
                project(b)
            pe.wait_ge(nT_act, KD // 2)
            pe.wait_ge(consts, 3 + GROUPS)
            for g in range(GROUPS):
                ins = pe.transpose(bank[7][:, g * P:(g + 1) * P], ws[:, g, :], ident[:])
            ins.then_inc(turned, 1)
            project(NB)
            project(NB + 1)
            pe.wait_ge(gates_in, 64)
            gates(wab, 0)
            project(NB + 2)
            project(NB + 3)
            gates(wxb, NB)
            project(2 * NB)
            pe.wait_ge(z_taken, 2 * 2 * NB)
            pe.wait_ge(gates_taken, 2 * NB)
            for t, rows in TILES:
                for g in range(GROUPS):
                    ins = pe.transpose(bank[4 + t][0:rows, g * P:(g + 1) * P], ya[:, g, t * P:t * P + rows], ident[:])
                ins.then_inc(v_turned, 1)
            project(2 * NB + 1)
            project(2 * NB + 2)
            project(2 * NB + 3)
            pe.wait_ge(news_ready, 1)
            for blk in range(NB):
                ins = pe.transpose(bank[7][0:36, blk * P:(blk + 1) * P], news[:, blk, :], ident[:])
            ins.then_inc(news_turned, 1)
            project(3 * NB)
            pe.wait_ge(ybsq_ready, 1)
            pe.wait_ge(news_taken, 1)
            for blk in range(NB):
                ins = pe.matmul(bank[7][0:2 * NB, 0:T], head_sum[:, blk, :], ig[:, blk, :], start=(blk == 0),
                                stop=(blk == NB - 1))
            ins.then_inc(ybss_made, 1)
            project(3 * NB + 1)
            pe.wait_ge(ybrstd_ready, 1)
            pe.wait_ge(vt_ready, NT)
            for blk in range(NB):
                pe.matmul(bank[4 + blk][:, 0:T],
                          head_back[:, blk * P:(blk + 1) * P], sums[:], start=True, stop=True).then_inc(ybrstd_made, 1)
            project(3 * NB + 2)
            pe.wait_ge(bs_ready, 1)
            for g in range(GROUPS):
                cols = slice(g * P, (g + 1) * P)
                s = bank[4 + g]
                pe.wait_ge(yb_ready, g + 1)
                pe.matmul(s[:, 0:T], ident[0:GROUPS, g:g + 1].to_broadcast([GROUPS, P]), bs_rows[:], start=True,
                          stop=False, skip_group_check=True)
                for t in range(2):
                    pe.matmul(s[:, t * P:(t + 1) * P], vt[:, t, cols], wsT[:, g, :], start=False, stop=False,
                              skip_group_check=True)
                pe.matmul(s[:, SEQ:T], vt[0:NS, 2, cols], w00_diag[0:NS, g, :], start=False, stop=True,
                          skip_group_check=True).then_inc(s_made, 1)
            project(3 * NB + 3)

            def mixed(t, k, first, last):
                src = ya[:, k, :] if k < NB else yb[:, k - NB, :]
                for m in range(2):
                    ins = pe.matmul(bank[MIX_BANKS[t] + m][:], src[:, t * P:(t + 1) * P], w_out[:, k, halves(m)],
                                    start=first, stop=last)
                return ins

            def small_tile(dst, lhs, w, chunks):
                for c in range(chunks // 2):
                    for q in range(2):
                        for m in range(2):
                            k = q * (chunks // 2) + c
                            r0 = 32 * (2 * q + m)
                            ins = pe.matmul(dst[r0:r0 + NS, :], lhs(k), w[:, k, halves(m)], start=(c == 0),
                                            stop=(c == chunks // 2 - 1), skip_group_check=True)
                return ins

            pe.wait_ge(wout_in, 16)
            pe.wait_ge(z_taken, 2 * (3 * NB + 2))
            mixed(0, NB, True, False)
            mixed(0, NB + 1, False, False)
            pe.wait_ge(yasq_ready, GROUPS)
            for g in range(GROUPS):
                ins = pe.matmul(bank[4][0:GROUPS, 0:T], group_sum[:, g, :], xc[:, g, :], start=(g == 0),
                                stop=(g == GROUPS - 1))
            ins.then_inc(yass_made, 1)
            mixed(0, NB + 2, False, False)
            mixed(0, NB + 3, False, False)
            pe.wait_ge(yarstd_ready, 1)
            for g in range(GROUPS):
                pe.matmul(bank[4 + g][:, 0:T], ident[0:GROUPS, g:g + 1].to_broadcast([GROUPS, P]),
                          sums[0:GROUPS, :], start=True, stop=True).then_inc(yarstd_made, 1)
            pe.wait_ge(z_taken, 8 * NB)
            for blk in range(NB):
                mixed(1, NB + blk, blk == 0, False)
            for g in range(GROUPS):
                pe.wait_ge(ya_ready, g + 1)
                ins = mixed(0, g, False, g == GROUPS - 1)
            ins.then_inc(mixed_made, 1)
            small_tile(bank[MIX_BANKS[2]], lambda k: (ya[:, k, :] if k < NB else yb[:, k - NB, :])[:, SEQ:T], w_out,
                       KD).then_inc(mixed_made, 1)
            for g in range(GROUPS):
                ins = mixed(1, g, False, g == GROUPS - 1)
            ins.then_inc(mixed_made, 1)

            pe.wait_ge(h_added, 2)
            for k in range(4):
                for t in MIX_ORDER[:2]:
                    turn_tile(h, k, t, TILES[t][1], TURN_BANKS[1])
            pe.wait_ge(h_added, NT)
            for k in range(KD):
                turn_chunk(h, 1, k, MIX_ORDER[2:] if k < 4 else MIX_ORDER)
            pe.wait_ge(router_in, 32)
            for k in range(KD):
                wait_nT(1, k)
                for t, rows in TILES:
                    ins = pe.matmul(bank[1 + t][0:rows, 0:NE], nT[:, k, t * P:t * P + rows], wr[:, k, :],
                                    start=(k == 0), stop=(k == KD - 1))
            ins.then_inc(logits_made, 1)
            pe.wait_ge(p_in, 32)
            for k in range(PLE // P):
                for t, rows in TILES:
                    ins = pe.transpose(bank[4 + k][:, t * P:t * P + rows], p_rows[0:rows, t, k * P:(k + 1) * P],
                                       ident[0:rows, 0:rows])
                ins.then_inc(p_turned, 1)
            pe.wait_ge(picked_ready, 1)
            pe.wait_ge(consts, 2)
            for t, rows in TILES:
                for s in range(t + 1):
                    rows_s = TILES[s][1]
                    lhs = before_b if s == t else ones_b
                    pe.matmul(bank[2][0:rows, t * NE:(t + 1) * NE], lhs[0:rows_s, 0:rows], picked_b[0:rows_s, s, :],
                              start=(s == 0), stop=(s == t), skip_group_check=True)
            for s, rows_s in TILES:
                ins = pe.matmul(bank[3][:, 0:NE], ones_b[0:rows_s, :], picked_b[0:rows_s, s, :], start=(s == 0),
                                stop=(s == NT - 1))
            ins.then_inc(places_made, 1)
            pe.wait_ge(wpick_ready, 1)
            for t, rows in TILES:
                ins = pe.transpose(bank[0][:, t * P:t * P + rows], wpick[0:rows, t, :], ident[0:rows, 0:rows])
            ins.then_inc(wpick_turned, 1)
            pe.wait_ge(pT_ready, PLE // P)
            pe.wait_ge(wpp_in, 16)
            for t in range(2):
                for k in range(PLE // P):
                    for m in range(2):
                        ins = pe.matmul(bank[4 + 2 * t + m][:], pT[:, k, t * P:(t + 1) * P], w_pp[:, k, halves(m)],
                                        start=(k == 0), stop=(k == PLE // P - 1))
                ins.then_inc(pw_made, 1)
            for k in range(PLE // P):
                for m in range(2):
                    ins = pe.matmul(bank[1][32 * m:32 * m + NS, :], pT[:, k, SEQ:T], w_pp[:, k, halves(m)],
                                    start=(k == 0), stop=(k == PLE // P - 1), skip_group_check=True)
            ins.then_inc(pw_made, 1)

            def gather(step, added=None):
                pe.wait_ge(pick_ready, step + 1)
                for k in range(KD):
                    cols = slice(k * P, (k + 1) * P)
                    dst = bank[3][:, k * CAP:(k + 1) * CAP]
                    for t in range(2):
                        for q in range(PARTS):
                            pe.matmul(dst, x_parts[:, q, t, cols], pick[:, t, :], start=(t == 0 and q == 0),
                                      stop=False, skip_group_check=True)
                    if k == KD - 1 and added is not None:
                        pe.wait_ge(h_added, added)
                    ins = pe.matmul(dst, xs_parts[0:32 * PARTS, cols], pick[0:32 * PARTS, 2, :], start=False,
                                    stop=True, skip_group_check=True)
                ins.then_inc(gathered, 1)

            def scatter(t, rows, first_bank):
                for m in range(2):
                    r = slice(CAP * m, CAP * (m + 1))
                    ins = pe.matmul(bank[first_bank + m][0:rows, :], wpickT[r, t * P:t * P + rows], y[r, :],
                                    start=True, stop=True)
                ins.then_inc(spread, 1)

            pe.wait_ge(parts_ready, 2)
            pe.wait_ge(parts_h, 7)
            pe.wait_ge(xs_low_ready, 2)
            pe.wait_ge(steps_ready, 1)
            gather(0)
            n = pe.value_load(n_steps[0:1, 0:1], min_val=NE, max_val=STEPS)
            pe.wait_ge(pw_ready, 2 * NT)
            pe.wait_ge(b2_in, 32)
            with pe.Fori(0, n) as i:
                pe.wait_ge(b1_pick_ready, i + 1)
                pe.wait_ge(wpickT_ready, i + 1)
                for part in range(2):
                    for m in range(2):
                        r = slice(CAP * m, CAP * (m + 1))
                        c = part * FF + m * HALF
                        pe.matmul(bank[part][r, :], b1_pick[0:PARTS * NE, :], b1_parts[0:PARTS * NE, c:c + HALF],
                                  start=True, stop=False, skip_group_check=True)
                pe.wait_ge(xgT_ready, i + 1)
                for k in range(W1_SLOTS):
                    pe.wait_ge(slot_in[k], (i + 1) * 16)
                    for part in range(2):
                        for m in range(2):
                            r = slice(CAP * m, CAP * (m + 1))
                            c = part * FF + m * HALF
                            ins = pe.matmul(bank[part][r, :], xgT[:, k, :], ring[:, k, c:c + HALF],
                                            start=False, stop=(k == W1_SLOTS - 1), skip_group_check=True)
                        if part == 0 and k == W1_SLOTS - 1:
                            ins.then_inc(gate_made, 1)
                    ins.then_inc(slots_free, 1)
                pe.wait_ge(y_ready, i + 1)
                pe.wait_ge(h_added, i * 2 * NT + NT)
                scatter(0, P, 4)
                scatter(1, P, 6)
                gather(i + 1, i * 2 * NT + NT + 2)
                scatter(2, NS, 4)
                pe.wait_ge(act_ready, i + 1)
                pe.wait_ge(xgT_ready, i + 2)
                for c in range(HALF // P):
                    ins = pe.transpose(bank[3][:, c * P:(c + 1) * P], act_sb[:, c * P:(c + 1) * P], ident[:])
                ins.then_inc(act_turned, 1)
                pe.wait_ge(wpick_ready, i + 2)
                pe.wait_ge(gmin_ready, i + 1)
                for t, rows in TILES:
                    ins = pe.transpose(bank[0][:, t * P:t * P + rows], wpick[0:rows, t, :], ident[0:rows, 0:rows])
                ins.then_inc(wpick_turned, 1)
                pe.wait_ge(actT_ready, i + 1)
                for j in range(W2_SLOTS):
                    pe.wait_ge(slot_in[W1_SLOTS + j], (i + 1) * 16)
                    for q in range(2):
                        f = 2 * j + q
                        half = (f % 4) * P + (f // 4) * CAP
                        for m in range(2):
                            c = q * D + m * HALF
                            ins = pe.matmul(bank[2][CAP * m:CAP * (m + 1), :], actT[:, half:half + CAP],
                                            ring[:, W1_SLOTS + j, c:c + HALF], start=(f == 0),
                                            stop=(f == FF // P - 1), skip_group_check=True)
                    ins.then_inc(slots_free, 1)
            pe.wait_ge(y_ready, n + 1)
            pe.wait_ge(wpickT_ready, n + 1)
            pe.wait_ge(h_added, n * 2 * NT + NT)
            scatter(0, P, 4)
            scatter(1, P, 6)
            scatter(2, NS, 0)

            pe.wait_ge(h_added, (n + 1) * 2 * NT + NT)
            for k in range(KD):
                turn_chunk(h, 2, k, range(NT))
            for k in range(KD):
                pe.wait_ge(wpg_in[k // 2], 16)
                wait_nT(2, k)
                for m in range(2):
                    ins = pe.matmul(bank[GATE_BANKS[0] + m][:], nT[:, k, 0:P], w_pg[:, k, halves(m)],
                                    start=(k == 0), stop=(k == KD - 1))
                    if k == KD - 1:
                        ins.then_inc(plegate_made, 1)
            small_tile(bank[GATE_BANKS[2]], lambda k: nT[:, k, SEQ:T], w_pg, KD).then_inc(plegate_made, 2)
            for m in range(2):
                for k in range(KD):
                    ins = pe.matmul(bank[GATE_BANKS[1] + m][:], nT[:, k, P:2 * P], w_pg[:, k, halves(m)],
                                    start=(k == 0), stop=(k == KD - 1))
                ins.then_inc(plegate_made, 1)


_INS = ["x_prompt", "x_sample", "state_conv", "state_lru", "p_prompt", "p_sample", "g_mix", "w_in", "g_v", "w_s",
        "b_s", "conv_w", "conv_b", "w_a", "b_a", "w_x", "b_x", "lam", "g_oa", "g_ob", "w_out", "g_ffn", "w_r",
        "b_r", "w1", "b1", "w2", "b2", "g_ple", "w_pg", "b_pg", "w_pp", "g_final"]


def kernel(**inputs):
    import numpy as np
    import concourse.bacc as bacc
    from concourse.bass_utils import run_bass_kernel_spmd

    nc = bacc.Bacc("TRN2", target_bir_lowering=False, num_devices=1)
    arrays, ins, outs = {}, {}, {}
    for name in _INS:
        x = np.ascontiguousarray(inputs[name])
        arrays[f"in_{name}"] = x
        ins[name] = nc.dram_tensor(f"in_{name}", x.shape, mybir.dt.from_np(x.dtype), kind="ExternalInput").ap()
    depth, samples, past, lru = inputs["state_conv"].shape
    chunk = inputs["w_s"].shape[2]
    gmlp = inputs["g_v"].shape[1]
    prompts = inputs["x_prompt"].shape[0]
    shapes = {
        "y_prompt": inputs["x_prompt"].shape,
        "y_sample": inputs["x_sample"].shape,
        "v_prompt": (depth, prompts, chunk, gmlp),
        "conv_prompt": (depth, prompts, past, lru),
        "lru_prompt": (depth, prompts, lru),
        "v_sample": (depth, samples, 1, gmlp),
        "conv_sample": (depth, samples, past, lru),
        "lru_sample": (depth, samples, lru),
    }
    for name, shape in shapes.items():
        outs[name] = nc.dram_tensor(f"out_{name}", shape, F32, kind="ExternalOutput").ap()
    decode_step(nc, ins, outs)
    r = run_bass_kernel_spmd(nc, [arrays], core_ids=[0])
    return tuple(r.results[0][f"out_{name}"] for name in shapes)
```

```python
from contextlib import ExitStack

import concourse.bass as bass
from concourse import mybir

ALU = mybir.AluOpType
ACT = mybir.ActivationFunctionType
AX = mybir.AxisListType
F32 = mybir.dt.float32
BF16 = mybir.dt.bfloat16
I32 = mybir.dt.int32

P = 128

VECTOR_ROWS = {"g_mix": (0, 8), "g_ffn": (8, 8), "g_ple": (16, 8), "conv_w": (24, 16), "conv_b": (40, 4),
               "lam": (44, 4), "b_a": (48, 4), "b_x": (52, 4), "g_oa": (56, 4), "g_ob": (60, 4)}
N_VECTOR_ROWS = 64


def decode_step(nc, a, out):
    SEQ, D = a["x_prompt"].shape[1:]
    NS = a["x_sample"].shape[0]
    DL = a["state_lru"].shape[2]
    NE, FF2 = a["w1"].shape[1], a["w1"].shape[3]
    FF = FF2 // 2
    PLE = a["w_pp"].shape[1]
    TAPS = a["conv_w"].shape[1]
    HEADS, HD = a["w_a"].shape[1], a["w_a"].shape[2]
    GROUPS = a["w_s"].shape[1]
    EPS = 1e-6
    LRU_C = 8.0
    LIMIT, ALPHA = 7.0, 1.702
    TOP_K = 4
    T = SEQ + NS
    TILES = [(t, P) for t in range(SEQ // P)] + [(SEQ // P, NS)]
    NT = len(TILES)
    KD = D // P
    NB = DL // P
    HALF = 512
    assert D == 2 * HALF and FF == D and SEQ == 2 * P and GROUPS == NB and HD * 2 == P

    CAP = 64
    MAX_ROUNDS = -(-T // CAP)
    STEPS = NE * MAX_ROUNDS
    W1_SLOTS, W2_SLOTS = KD, FF // P // 2
    SLOTS = W1_SLOTS + W2_SLOTS
    MIX_ORDER, MIX_BANKS = (0, 2, 1), (0, 2, 4)
    GATE_BANKS = (0, 2, 4)
    TURN_BANKS = ((0, 4, 5, 6, 7, 2, 3, 1), (5, 6, 7, 0, 1, 4, 2, 3))
    ACT_CHUNKS, DVE_CHUNKS = ((1, 3, 5, 7), (4, 5, 7)), ((0, 2, 4, 6), (0, 1, 2, 3, 6))
    EARLY = 3
    WARM_UP = 22
    EMBED_BANKS = ((4, 0), (6, 7), (1, 1))
    HN_COUNT = {0: 3, 2: 4, 1: 5}
    PARTS = 3

    with ExitStack() as ctx:
        def sb(name, shape, dt=F32, stack=ctx):
            return stack.enter_context(nc.sbuf_tensor(name, shape, dt))

        def sem(name):
            return ctx.enter_context(nc.semaphore(name))

        bank = [ctx.enter_context(nc.psum_tensor(f"bank{i}", [P, HALF], F32)) for i in range(8)]

        ring = sb("ring", [P, SLOTS, FF2])
        h = sb("h", [P, NT, D])
        hn = sb("hn", [P, NT, D])
        nT = sb("nT", [P, KD, T])
        b1_parts = sb("b1_parts", [P, FF2], BF16)
        ident = sb("ident", [P, P])
        head_sum = sb("head_sum", [P, 32])
        group_sum = sb("group_sum", [P, 32])
        ones_b = sb("ones_b", [P, P], BF16)
        before_b = sb("before_b", [P, P], BF16)
        slot_no = sb("slot_no", [P, 2 * CAP])
        expert_pick = sb("expert_pick", [P, STEPS + 1], BF16)
        vecT = sb("vecT", [P, N_VECTOR_ROWS])
        pos = sb("pos", [P, NT, STEPS + 1])
        share = sb("share", [P, NT, STEPS + 1])
        eps_col = sb("eps_col", [P, 1])
        sumsq = sb("sumsq", [P, NT])
        squares = sb("squares", [P, 2, 2])
        table_junk = sb("table_junk", [1, 1])
        rms = sb("rms", [P, NT])
        rstd = sb("rstd", [P, NT])
        n_steps = sb("n_steps", [P, 2], I32)
        y = sb("y", [P, HALF])

        early = ExitStack()
        xpad = sb("xpad", [P, NB, 3 + SEQ + 4 * NS], stack=early)
        conv = sb("conv", [P, NB, SEQ + 4 * NS], stack=early)
        early.close()
        mix = ExitStack()
        NL = NE + TOP_K
        router_words = NT * (2 * NL + 4 * NE + NE // 2 + 8 + 2) + 8 + T + NE + NT * PLE + PLE // P * T + 160 + 64
        lg = sb("lg", [P, NT, NL], stack=mix)
        top = sb("top", [P, NT, 8], stack=mix)
        left = sb("left", [P, NT, NL], stack=mix)
        picked = sb("picked", [P, NT, NE], stack=mix)
        picked_b = sb("picked_b", [P, NT, NE], BF16, stack=mix)
        ex = sb("ex", [P, NT, NE], stack=mix)
        negmax = sb("negmax", [P, NT], stack=mix)
        exsum = sb("exsum", [P, NT], stack=mix)
        cw = sb("cw", [P, NT, NE], stack=mix)
        partial = sb("partial", [P, T], stack=mix)
        fold = sb("fold", [P, NE], stack=mix)
        slot1 = sb("slot1", [P, NT, NE], stack=mix)
        rounds = sb("rounds", [P, 8], stack=mix)
        p_rows = sb("p_rows", [P, NT, PLE], stack=mix)
        pT = sb("pT", [P, PLE // P, T], stack=mix)
        sb("rest_of_early", [P, 160], stack=mix)
        yb = sb("yb", [P, NB, T], stack=mix)
        ya = sb("ya", [P, NB, T], stack=mix)
        xc = sb("xc", [P, NB, T], stack=mix)
        ug = sb("ug", [P, NB, T], stack=mix)
        rg = sb("rg", [P, NB, T], stack=mix)
        ig = sb("ig", [P, NB, T], stack=mix)
        decay = sb("decay", [P, NB, T], stack=mix)
        th = sb("th", [P, NB, T], stack=mix)
        vt = sb("vt", [P, NT, DL], stack=mix)
        vss = sb("vss", [P, NT, GROUPS], stack=mix)
        ws_both = sb("ws_both", [P, 2, GROUPS, P], stack=mix)
        ws, wsT = ws_both[:, 0], ws_both[:, 1]
        w00 = sb("w00", [P, GROUPS], stack=mix)
        w00_diag = sb("w00_diag", [P, GROUPS, NS], stack=mix)
        bs_wide = sb("bs_wide", [P, GROUPS, P], stack=mix)
        sums = sb("sums", [P, T], stack=mix)
        head_back = sb("head_back", [P, P], stack=mix)
        past = sb("past", [32, DL], stack=mix)
        pastT = sb("pastT", [P, NB, 32], stack=mix)
        wab = sb("wab", [P, NB, P], stack=mix)
        wxb = sb("wxb", [P, NB, P], stack=mix)
        gv = sb("gv", [P, DL], stack=mix)
        news = sb("news", [P, NB, 36], stack=mix)
        vrows = sb("vrows", [N_VECTOR_ROWS, P], stack=mix)
        lamt = sb("lamt", [P, 8, NB], stack=mix)
        wr = sb("wr", [P, KD, NE], stack=mix)
        br_row = sb("br_row", [P, NE], stack=mix)
        mix.close()

        moe = ExitStack()
        sb("under_router", [P, router_words], stack=moe)
        split1 = ExitStack()
        rest1 = sb("rest1", [P, D], stack=split1)
        split1.close()
        split2 = ExitStack()
        bpg = sb("bpg", [P, D], stack=split2)
        gfin = sb("gfin", [P, D], stack=split2)
        split2.close()
        gmin = sb("gmin", [P, HALF], stack=moe)
        uclip = sb("uclip", [P, HALF], stack=moe)
        sig = sb("sig", [P, HALF], stack=moe)
        gu = sb("gu", [P, HALF], stack=moe)
        sb("rest_of_ya", [P, 2 * NB * T - 4 * HALF], stack=moe)
        x_parts = sb("x_parts", [P, PARTS, 2, D], BF16, stack=moe)
        xs_parts = sb("xs_parts", [P, D], BF16, stack=moe)
        xs_mid = sb("xs_mid", [NS, D], BF16, stack=moe)
        pick = sb("pick", [P, NT, CAP], BF16, stack=moe)
        wpick = sb("wpick", [P, NT, 2 * CAP], stack=moe)
        wpickT = sb("wpickT", [P, T], stack=moe)
        b1_pick = sb("b1_pick", [P, CAP], BF16, stack=moe)
        xgT = sb("xgT", [P, KD, CAP], stack=moe)
        split0 = ExitStack()
        rest0 = sb("rest0", [P, D], stack=split0)
        split0.close()
        rest = (rest0, rest1)
        act_sb = sb("act_sb", [P, HALF], stack=moe)
        actT = sb("actT", [P, HALF], stack=moe)
        pw = sb("pw", [P, NT, D], stack=moe)
        early_x = sb("early_x", [P, FF2], stack=moe)
        moe.close()
        gate = hn
        y_out = x_parts[:].rearrange("p q t d -> p (q t d)").bitcast(F32).rearrange("p (t d) -> p t d", t=NT)
        early_w1 = [early_x[:], nT[:].rearrange("p k t -> p (k t)")[:, 0:FF2],
                    hn[:, 0:2, :].rearrange("p t d -> p (t d)")]
        b1_rows = hn[0:NE, 0:2, :].rearrange("p t d -> p (t d)")
        b1_mid = hn[0:NE, 2, :].bitcast(BF16)
        news_rows = ws[0:36, :, :].rearrange("p g t -> p (g t)")

        w_in = [ring[:, 2 * g:2 * g + 2, :].rearrange("p s n -> p (s n)").rearrange("p (k n) -> p k n", k=KD)
                for g in range(4)]
        w_out = ring[:, W1_SLOTS:SLOTS, :].rearrange("p s n -> p (s n)").rearrange("p (k n) -> p k n", k=KD)
        w_pg = ring[:, 0:4, :].rearrange("p s n -> p (s n)").rearrange("p (k n) -> p k n", k=KD)
        w_pp = ring[:, W1_SLOTS - 1, :].rearrange("p (k n) -> p k n", k=PLE // P)

        x_in = [sem(f"x_in{t}") for t in range(NT)]
        vec_in = sem("vec_in")
        past_in = sem("past_in")
        ws_in = sem("ws_in")
        bs_in = sem("bs_in")
        gates_in = sem("gates_in")
        gv_in = sem("gv_in")
        b1_in = sem("b1_in")
        b2_in = sem("b2_in")
        router_in = sem("router_in")
        win_in = [[sem("win_in0a"), sem("win_in0b")]] + [[sem(f"win_in{g}")] for g in range(1, 4)]
        wout_in = sem("wout_in")
        slot_in = [sem(f"slot_in{j}") for j in range(SLOTS)]
        early_in = [sem(f"early_in{j}") for j in range(EARLY)]
        p_in = sem("p_in")
        wpg_in = [sem(f"wpg_in{j}") for j in range(4)]
        wpp_in = sem("wpp_in")
        rows_in = sem("rows_in")
        stored = sem("stored")
        consts = sem("consts")
        zeroed = sem("zeroed")
        pool_done = sem("pool_done")
        dve_done = sem("dve_done")
        act_done = sem("act_done")
        turned = sem("turned")
        vecT_ready = sem("vecT_ready")
        pastT_ready = sem("pastT_ready")
        wsT_ready = sem("wsT_ready")
        rstd_ready = sem("rstd_ready")
        hn_act = sem("hn_act")
        square_mid = sem("square_mid")
        rms_ready = sem("rms_ready")
        hn_ready = sem("hn_ready")
        rows_turned = sem("rows_turned")
        nT_dve = sem("nT_dve")
        nT_act = sem("nT_act")
        z_made = sem("z_made")
        z_taken = sem("z_taken")
        xc_ready = sem("xc_ready")
        gates_made = sem("gates_made")
        gates_taken = sem("gates_taken")
        lru_act = sem("lru_act")
        lam_abs_ready = sem("lam_abs_ready")
        lam_exp_ready = sem("lam_exp_ready")
        decay_ready = sem("decay_ready")
        mult2_ready = sem("mult2_ready")
        mult_ready = sem("mult_ready")
        ybsq_ready = sem("ybsq_ready")
        ybss_made = sem("ybss_made")
        ybrms_ready = sem("ybrms_ready")
        ybrstd_ready = sem("ybrstd_ready")
        ybrstd_made = sem("ybrstd_made")
        yb_ready = sem("yb_ready")
        news_ready = sem("news_ready")
        news_turned = sem("news_turned")
        news_taken = sem("news_taken")
        v_turned = sem("v_turned")
        vsq_ready = sem("vsq_ready")
        vss_ready = sem("vss_ready")
        vrms_ready = sem("vrms_ready")
        vt_ready = sem("vt_ready")
        bs_ready = sem("bs_ready")
        s_made = sem("s_made")
        yasq_ready = sem("yasq_ready")
        yass_made = sem("yass_made")
        yarms_ready = sem("yarms_ready")
        yarstd_ready = sem("yarstd_ready")
        yarstd_made = sem("yarstd_made")
        ya_ready = sem("ya_ready")
        b1_ready = sem("b1_ready")
        wout_late = sem("wout_late")
        mixed_made = sem("mixed_made")
        slots_free = sem("slots_free")
        logits_made = sem("logits_made")
        logits_taken = sem("logits_taken")
        negmax_ready = sem("negmax_ready")
        ex_ready = sem("ex_ready")
        picked_ready = sem("picked_ready")
        places_made = sem("places_made")
        steps_ready = sem("steps_ready")
        parts_h = sem("parts_h")
        xs_h = sem("xs_h")
        parts_r = sem("parts_r")
        parts_ready = sem("parts_ready")
        xs_low_ready = sem("xs_low_ready")
        moe_zeroed = sem("moe_zeroed")
        pick_ready = sem("pick_ready")
        wpick_ready = sem("wpick_ready")
        gathered = sem("gathered")
        xgT_ready = sem("xgT_ready")
        b1_pick_ready = sem("b1_pick_ready")
        gate_made = sem("gate_made")
        gmin_ready = sem("gmin_ready")
        uclip_ready = sem("uclip_ready")
        sig_ready = sem("sig_ready")
        gu_ready = sem("gu_ready")
        act_ready = sem("act_ready")
        act_turned = sem("act_turned")
        actT_ready = sem("actT_ready")
        wpick_turned = sem("wpick_turned")
        wpickT_ready = sem("wpickT_ready")
        y_ready = sem("y_ready")
        spread = sem("spread")
        h_added = sem("h_added")
        p_turned = sem("p_turned")
        pT_ready = sem("pT_ready")
        tail_turned = sem("tail_turned")
        tail_nT_dve = sem("tail_nT_dve")
        tail_nT_act = sem("tail_nT_act")
        pw_made = sem("pw_made")
        pw_ready = sem("pw_ready")
        plegate_made = sem("plegate_made")
        plebias_ready = sem("plebias_ready")
        plegate_ready = sem("plegate_ready")
        h_final = sem("h_final")
        squares_ready = sem("squares_ready")
        sumsq_ready = sem("sumsq_ready")
        y_final = sem("y_final")
        sample_bias = sem("sample_bias")
        sample_gate = sem("sample_gate")
        sample_h = sem("sample_h")
        sample_rms = sem("sample_rms")
        sample_final = sem("sample_final")

        def vcol(name, k):
            return vecT[:, VECTOR_ROWS[name][0] + k:VECTOR_ROWS[name][0] + k + 1]

        def halves(n):
            return slice(n * HALF, (n + 1) * HALF)

        block = ctx.enter_context(nc.Block())

        @block.sync
        def _(sp):
            def load(dst, src, s, single_elements=False):
                sp.dma_start(dst, src, allow_slow_non_contiguous=single_elements).then_inc(s, 16)

            def load_w_in(g, k0, k1, s):
                c = (2, 1, 3, 0)[g]
                load(w_in[g][:, k0:k1, :],
                     a["w_in"][0].rearrange("(k p) n -> p k n", p=P)[:, k0:k1, c * DL:(c + 1) * DL], s)

            for t in range(2):
                load(h[:, t, :], a["x_prompt"][0][t * P:(t + 1) * P, :], x_in[t])
            load(h[0:NS, 2, :], a["x_sample"].rearrange("b s d -> (b s) d"), x_in[2])
            load_w_in(0, 0, KD // 2, win_in[0][0])
            for name, (r0, n) in VECTOR_ROWS.items():
                src = a[name][0]
                if name in ("b_a", "b_x"):
                    src = src.rearrange("(r q) j -> r (q j)", q=2)
                elif name == "conv_w":
                    src = src.rearrange("k (r j) -> (k r) j", j=P)
                else:
                    src = src.rearrange("(r j) -> r j", j=P)
                load(vrows[r0:r0 + n, :], src, vec_in)
            load_w_in(0, KD // 2, KD, win_in[0][1])
            load(past[0:3 * NS, :], a["state_conv"][0].rearrange("b k d -> (b k) d"), past_in)
            load(past[3 * NS:3 * NS + NS, :], a["state_lru"][0], past_in)
            sp.wait_ge(zeroed, 4)
            for dst, name in ((wab, "w_a"), (wxb, "w_x")):
                src = a[name][0].rearrange("(b q) i j -> q i b j", q=2)
                for q in range(2):
                    load(dst[HD * q:HD * (q + 1), :, HD * q:HD * (q + 1)], src[q], gates_in)
            load_w_in(1, 0, KD, win_in[1][0])
            load(ws[:], a["w_s"][0].rearrange("g t s -> t g s"), ws_in)
            load(gv[:], a["g_v"][0].partition_broadcast(P), gv_in)
            load_w_in(2, 0, KD, win_in[2][0])
            load(bs_wide[:].rearrange("p g t -> p (g t)"),
                 a["b_s"][0].rearrange("g t -> (g t)").partition_broadcast(P), bs_in)
            load(w00[0:NS, :], a["w_s"][0][:, 0, 0].partition_broadcast(NS), bs_in, True)
            load_w_in(3, 0, KD, win_in[3][0])
            sp.wait_ge(rows_turned, KD)
            load(b1_rows, a["b1"][0], b1_in)
            load(wr[:], a["w_r"][0].rearrange("(k p) e -> p k e", p=P), router_in)
            load(br_row[:], a["b_r"][0].partition_broadcast(P), router_in)
            sp.wait_ge(y_ready, 1)
            for m in range(2):
                load(y[CAP * m:CAP * m + NE, :], a["b2"][0][:, halves(m)], b2_in)
            load(w_out, a["w_out"][0].rearrange("(k p) n -> p k n", p=P), wout_in)

            def load_slot(j, e):
                if j < W1_SLOTS:
                    src = a["w1"][0][bass.ds(e, 1)][:, j * P:(j + 1) * P, :].rearrange("e p n -> p (e n)")
                    sp.dma_start(ring[:, j, :], src).then_inc(slot_in[j], 16)
                else:
                    m = j - W1_SLOTS
                    src = a["w2"][0][bass.ds(e, 1)][:, 2 * m * P:(2 * m + 2) * P, :].rearrange(
                        "e (q p) n -> p (e q) n", p=P)
                    sp.dma_start(ring[:, j, :].rearrange("p (q n) -> p q n", q=2), src).then_inc(slot_in[j], 16)

            for j in range(W1_SLOTS - 2):
                sp.wait_ge(z_made, NB * (j // 2 + 1))
                load_slot(j, 0)
            sp.wait_ge(vt_ready, NT)
            load(out["v_prompt"].rearrange("l b t d -> (l b t) d"), vt[:, 1, :], stored)
            load(out["v_sample"].rearrange("l b t d -> (l b t) d"), vt[0:NS, 2, :], stored)
            sp.wait_ge(news_taken, 1)
            lru0 = 3 + 3 * NS
            load(out["conv_prompt"].rearrange("l b k d -> (l b k) d"), news_rows[0:3, :], stored)
            load(out["conv_sample"].rearrange("l b k d -> (l b k) d"), news_rows[3:lru0, :], stored)
            load(out["lru_prompt"].rearrange("l b d -> (l b) d"), news_rows[lru0:lru0 + 1, :], stored)
            load(out["lru_sample"].rearrange("l b d -> (l b) d"), news_rows[lru0 + 1:lru0 + 1 + NS, :], stored)
            load(p_rows[:, 0:2, :], a["p_prompt"][0, 0].rearrange("(t p) d -> p t d", p=P), p_in)
            load(p_rows[0:NS, 2, :], a["p_sample"][0].rearrange("b s d -> (b s) d"), p_in)
            sp.wait_ge(z_made, 4 * NB)
            load(w_pp, a["w_pp"][0].rearrange("(k p) n -> p k n", p=P), wpp_in)
            load_slot(W1_SLOTS - 2, 0)

            def load_early(j, e):
                src = a["w1"][0, e, j * P:(j + 1) * P, :]
                sp.dma_start(early_w1[j], src).then_inc(early_in[j], 16)

            sp.wait_ge(yarstd_made, GROUPS)
            load_early(0, 1)
            sp.wait_ge(wout_late, 1)
            for j in range(SLOTS - 2, SLOTS):
                load_slot(j, 0)
            sp.wait_ge(mixed_made, NT)
            for j in range(W1_SLOTS, SLOTS - 2):
                load_slot(j, 0)
            sp.wait_ge(logits_made, 1)
            load_early(1, 1)
            sp.wait_ge(pw_made, NT)
            load_slot(W1_SLOTS - 1, 0)
            sp.wait_ge(parts_ready, 2)
            sp.wait_ge(xs_low_ready, 2)
            load_early(2, 1)
            for j in range(SLOTS):
                sp.wait_ge(slots_free, j + 1)
                load_slot(j, 2 if j < EARLY else 1)
            for j in range(EARLY, SLOTS):
                sp.wait_ge(slots_free, SLOTS + j + 1)
                load_slot(j, 2)
            with sp.Fori(2, NE - 1) as e:
                for j in range(SLOTS):
                    sp.wait_ge(slots_free, e * SLOTS + j + 1)
                    load_slot(j, e + 1)
            sp.wait_ge(steps_ready, 1)
            more = sp.value_load(n_steps[0:1, 1:2], min_val=0, max_val=STEPS - NE)
            with sp.If(more > 0):
                with sp.Fori(0, more) as i:
                    for j in range(SLOTS):
                        sp.wait_ge(slots_free, (i + (NE - 1)) * SLOTS + j + 1)
                        load_slot(j, i % NE)
            for j in range(4):
                sp.wait_ge(slots_free, (more + (NE - 1)) * SLOTS + j + 1)
                load(w_pg[:, 2 * j:2 * j + 2, :],
                     a["w_pg"][0].rearrange("(k p) n -> p k n", p=P)[:, 2 * j:2 * j + 2, :], wpg_in[j])
            sp.wait_ge(slots_free, (more + (NE - 1)) * SLOTS + SLOTS)
            load(bpg[:], a["b_pg"][0].partition_broadcast(P), rows_in)
            load(gfin[:], a["g_final"].partition_broadcast(P), rows_in)
            for t in (0, 2, 1):
                if t == 2:
                    sp.wait_ge(sample_final, 1)
                    load(out["y_sample"].rearrange("b s d -> (b s) d"), y_out[0:NS, 2, :], stored)
                else:
                    for m in range(2):
                        sp.wait_ge(y_final, 2 * t + m + 1)
                        load(out["y_prompt"][0][t * P:(t + 1) * P, halves(m)], y_out[:, t, halves(m)], stored)
            sp.wait_ge(stored, 16 * 11)

        @block.gpsimd
        def _(pool):
            pool_count = [0]

            def link(ins):
                pool_count[0] += 1
                ins.then_inc(pool_done, 1)
                pool.wait_ge(pool_done, pool_count[0])
            link(pool.memset(ident[:], 0.0))
            pool.affine_select(out=ident[:], in_=ident[:], compare_op=ALU.not_equal, fill=1.0, base=0,
                               pattern=[[-1, P]], channel_multiplier=1).then_inc(consts, 1)
            link(pool.memset(before_b[:], 1.0))
            pool.affine_select(out=before_b[:], in_=before_b[:], compare_op=ALU.is_gt, fill=0.0, base=0,
                               pattern=[[1, P]], channel_multiplier=-1).then_inc(consts, 1)
            pool.iota(slot_no[:], pattern=[[0, 2], [1, CAP]], base=0, channel_multiplier=0,
                      allow_small_or_imprecise_dtypes=True).then_inc(consts, 1)
            pool.wait_ge(ws_in, 16)
            for g in range(GROUPS):
                pool.affine_select(out=ws[:, g, :], in_=ws[:, g, :], compare_op=ALU.is_ge, fill=0.0, base=0,
                                   pattern=[[-1, P]], channel_multiplier=1).then_inc(consts, 1)
            pool.wait_ge(b1_in, 16)
            link(pool.tensor_copy(b1_parts[0:NE, :], b1_rows))
            link(pool.tensor_tensor(b1_rows, b1_rows, b1_parts[0:NE, :], ALU.subtract))
            link(pool.tensor_copy(b1_mid, b1_rows))
            pool.tensor_copy(b1_parts[NE:2 * NE, :], b1_mid)
            pool.tensor_tensor(b1_parts[2 * NE:3 * NE, :], b1_rows, b1_mid, ALU.subtract).then_inc(b1_ready, 1)
            pool.wait_ge(stored, 16 * 6)
            for t in range(2):
                pool.wait_ge(parts_h, 2 * t + 1)
                pool.tensor_tensor(rest[t][:], hn[:, t, :], x_parts[:, 0, t, :], ALU.subtract
                                   ).then_inc(parts_r, 1)
                pool.wait_ge(parts_h, 2 * t + 2)
                pool.tensor_tensor(x_parts[:, 2, t, :], rest[t][:], x_parts[:, 1, t, :], ALU.subtract
                                   ).then_inc(parts_ready, 1)

        @block.scalar
        def _(act):
            count = [0]

            def link(ins):
                count[0] += 1
                ins.then_inc(act_done, 1)
                act.wait_ge(act_done, count[0])

            def square_rows(t, rows, junk):
                link(act.activation(junk[0:rows, :], h[0:rows, t, :], ACT.Square, accum_out=sumsq[0:rows, t:t + 1]))

            def root_means(first=0, last=NT, step=1):
                tiles = slice(first, last, step)
                act.activation(rms[:, tiles], sumsq[:, tiles], ACT.Sqrt, bias=eps_col[:], scale=1.0 / D
                               ).then_inc(rms_ready, 1)

            def take_nT(stage, gain, banks):
                for k in ACT_CHUNKS[stage]:
                    act.wait_ge(rows_turned, stage * KD + k + 1)
                    act.activation(nT[:, k, :], bank[banks[k]][:, 0:T], ACT.Identity,
                                   scale=vcol(gain, k)).then_inc(nT_act, 1)

            junk0 = ug[:].rearrange("p b t -> p (b t)")[:, 0:D]
            junk1 = ws_both[:].rearrange("p q g t -> p (q g t)")
            act.wait_ge(zeroed, 2)
            link(act.activation(table_junk[:], eps_col[0:1, :], ACT.Sqrt))
            for t, rows in (TILES[0], TILES[2]):
                act.wait_ge(x_in[t], 16)
                square_rows(t, rows, junk0)
            act.wait_ge(square_mid, 1)
            root_means()
            act.wait_ge(rstd_ready, 1)
            act.activation(hn[:, 1, :], h[:, 1, :], ACT.Copy, scale=rstd[:, 1:2]).then_inc(hn_act, 1)
            act.wait_ge(vecT_ready, 1)
            take_nT(0, "g_mix", TURN_BANKS[0])

            act.wait_ge(zeroed, 5)
            for blk in range(NB):
                z = bank[blk]
                act.wait_ge(z_made, blk + 1)
                act.activation(xpad[:, blk, 3:3 + SEQ], z[:, 0:SEQ], ACT.Copy).then_inc(z_taken, 1)
                act.activation(xpad[:, blk, 3 + SEQ:].rearrange("p (s k) -> p s k", k=4)[:, :, 3], z[:, SEQ:T],
                               ACT.Copy).then_inc(z_taken, 1)
            act.wait_ge(lam_abs_ready, 1)
            act.activation(lamt[:, 2, :], lamt[:, 1, :], ACT.Exp, scale=-1.0).then_inc(lam_exp_ready, 1)
            act.wait_ge(turned, 3)
            act.activation(wsT[:].rearrange("p g t -> p (g t)"), bank[7][:], ACT.Copy).then_inc(wsT_ready, 1)

            def take_gelu(dst, group, blocks):
                for blk in blocks:
                    act.wait_ge(z_made, group * NB + blk + 1)
                    act.activation(dst[:, blk, :], bank[blk][:, 0:T], ACT.Gelu_apprx_tanh).then_inc(z_taken, 2)

            def take_gate(dst, bias, first):
                for blk in range(NB):
                    act.wait_ge(gates_made, first + blk + 1)
                    act.activation(dst[:, blk, :], bank[4 + blk][:, 0:T], ACT.Sigmoid, bias=vcol(bias, blk)
                                   ).then_inc(gates_taken, 1)

            take_gelu(ya, 1, (0, 1))
            take_gate(rg, "b_a", 0)
            take_gelu(ya, 1, (2, 3))
            take_gate(ig, "b_x", NB)
            act.wait_ge(decay_ready, 1)
            act.wait_ge(gates_taken, 2 * NB)
            for blk in range(NB):
                act.activation(decay[:, blk, :], rg[:, blk, :], ACT.Exp, scale=lamt[:, 7, blk:blk + 1]
                               ).then_inc(lru_act, 1)
            for blk in range(NB):
                act.activation(th[:, blk, :], rg[:, blk, :], ACT.Tanh, scale=lamt[:, 6, blk:blk + 1]
                               ).then_inc(lru_act, 1)
            take_gelu(yb, 2, (0,))
            act.wait_ge(mult2_ready, 1)
            act.activation(th[:], th[:], ACT.Sqrt).then_inc(mult_ready, 1)
            for t, rows in TILES:
                act.wait_ge(v_turned, t + 1)
                act.activation(vt[0:rows, t, :], bank[4 + t][0:rows, :], ACT.Square).then_inc(vsq_ready, 1)
            take_gelu(yb, 2, (1, 2))
            act.wait_ge(vss_ready, NT)
            act.activation(vss[:], vss[:], ACT.Sqrt, bias=eps_col[:], scale=1.0 / P).then_inc(vrms_ready, 1)
            take_gelu(yb, 2, (3,))
            act.wait_ge(news_turned, 1)
            act.activation(news_rows[:], bank[7][0:36, :], ACT.Copy).then_inc(news_taken, 1)
            take_gelu(ug, 3, (0,))
            act.wait_ge(ybss_made, 1)
            act.activation(sums[:], bank[7][:, 0:T], ACT.Sqrt, bias=eps_col[:], scale=1.0 / HD
                           ).then_inc(ybrms_ready, 1)
            take_gelu(ug, 3, (1, 2, 3))
            act.wait_ge(yass_made, 1)
            act.activation(sums[:], bank[4][:, 0:T], ACT.Sqrt, bias=eps_col[:], scale=1.0 / P).then_inc(yarms_ready, 1)

            for k in range(PLE // P):
                act.wait_ge(p_turned, k + 1)
                act.activation(pT[:, k, :], bank[2 + k][:, 0:T], ACT.Copy).then_inc(pT_ready, 1)

            act.wait_ge(stored, 16 * 6)
            for i, t in enumerate(MIX_ORDER[:2]):
                act.wait_ge(h_added, i + 1)
                square_rows(t, TILES[t][1], junk1)
            root_means(0, NT, 2)

            def high_part(t, rows):
                act.wait_ge(hn_ready, HN_COUNT[t])
                act.activation(x_parts[0:rows, 0, t, :] if t < 2 else xs_parts[0:rows, :], hn[0:rows, t, :], ACT.Copy
                               ).then_inc(parts_h if t < 2 else xs_h, 1)

            def middle_part(t):
                act.wait_ge(parts_r, t + 1)
                act.activation(x_parts[:, 1, t, :], rest[t][:], ACT.Copy).then_inc(parts_h, 1)

            def take_embed(t):
                act.wait_ge(pw_made, (2, 3, 1)[t])
                for m in range(2):
                    src = bank[EMBED_BANKS[t][m]][:] if t < 2 else bank[EMBED_BANKS[2][m]][32 * m:32 * m + NS, :]
                    act.activation(pw[0:TILES[t][1], t, halves(m)], src, ACT.Copy).then_inc(pw_ready, 1)

            act.wait_ge(moe_zeroed, 1)
            high_part(0, P)
            high_part(2, NS)
            act.wait_ge(h_added, NT)
            square_rows(1, P, junk1)
            root_means(1, 2)
            take_nT(1, "g_ffn", TURN_BANKS[1])
            middle_part(0)
            high_part(1, P)
            link(act.activation(table_junk[:], eps_col[0:1, :], ACT.Exp))
            act.wait_ge(negmax_ready, 1)
            for t in range(NT):
                act.activation(ex[:, t, :], lg[:, t, 0:NE], ACT.Exp, bias=negmax[:, t:t + 1]).then_inc(ex_ready, 1)
            middle_part(1)
            act.wait_ge(xs_low_ready, 1)
            act.activation(xs_mid[:], hn[0:NS, 2, :], ACT.Copy).then_inc(xs_h, 1)
            act.wait_ge(xs_h, 2)
            act.activation(xs_parts[32:32 + NS, :], xs_mid[:], ACT.Copy).then_inc(xs_h, 1)
            take_embed(2)
            take_embed(0)
            act.wait_ge(wpick_turned, 1)
            act.activation(wpickT[:], bank[5][:, 0:T], ACT.Copy).then_inc(wpickT_ready, 1)
            take_embed(1)

            act.wait_ge(steps_ready, 1)
            n = act.value_load(n_steps[0:1, 0:1], min_val=NE, max_val=STEPS)
            with act.Fori(0, n) as i:
                act.wait_ge(gmin_ready, i + 1)
                act.activation(sig[:], gmin[:], ACT.Sigmoid, scale=ALPHA).then_inc(sig_ready, 1)
                act.wait_ge(act_turned, i + 1)
                act.activation(actT[:], bank[3][:], ACT.Copy).then_inc(actT_ready, 1)
                act.wait_ge(wpick_turned, i + 2)
                act.activation(wpickT[:], bank[0][:, 0:T], ACT.Copy).then_inc(wpickT_ready, 1)
                act.wait_ge(slots_free, (i + 1) * SLOTS)
                act.activation(y[:], bank[2][:], ACT.Copy).then_inc(y_ready, 1)

            for t in range(2):
                act.wait_ge(tail_turned, 2 * t + 2)
                for c in range(4):
                    act.activation(nT[:, 4 + c, t * P:(t + 1) * P], bank[3 + 4 * t][:, c * P:(c + 1) * P],
                                   ACT.Identity, scale=vcol("g_ple", 4 + c)).then_inc(tail_nT_act, 1)
            for t, rows in TILES:
                act.wait_ge(h_added, n * (2 * NT) + NT + 2 * t + 2)
                square_rows(t, rows, y_out[:, t, :])
            root_means()

            def sigmoid_half(t, m):
                act.wait_ge(plebias_ready, 2 * t + m + 1)
                act.activation(gate[:, t, halves(m)], gate[:, t, halves(m)], ACT.Sigmoid).then_inc(plegate_ready, 1)

            def square_half(t, m):
                act.wait_ge(h_final, 2 * t + m + 1)
                act.activation(y_out[:, t, halves(m)], h[:, t, halves(m)], ACT.Square,
                               accum_out=squares[:, t, m:m + 1]).then_inc(squares_ready, 1)

            def load_table(func):
                link(act.activation(table_junk[:], eps_col[0:1, :], func))

            def root_tile(t):
                act.wait_ge(sumsq_ready, t + 1)
                act.activation(rms[:, t:t + 1], sumsq[:, t:t + 1], ACT.Sqrt, bias=eps_col[:], scale=1.0 / D
                               ).then_inc(rms_ready, 1)

            sigmoid_half(0, 0)
            sigmoid_half(0, 1)
            act.wait_ge(sample_bias, 1)
            act.activation(gate[0:NS, 2, :], gate[0:NS, 2, :], ACT.Sigmoid).then_inc(sample_gate, 1)
            load_table(ACT.Sqrt)
            square_half(0, 0)
            square_half(0, 1)
            root_tile(0)
            act.wait_ge(sample_h, 1)
            link(act.activation(y_out[0:NS, 2, :], h[0:NS, 2, :], ACT.Square, accum_out=sumsq[0:NS, 2:3]))
            act.activation(rms[0:NS, 2:3], sumsq[0:NS, 2:3], ACT.Sqrt, bias=eps_col[0:NS, :], scale=1.0 / D
                           ).then_inc(sample_rms, 1)
            load_table(ACT.Sigmoid)
            sigmoid_half(1, 0)
            square_half(1, 0)
            sigmoid_half(1, 1)
            load_table(ACT.Sqrt)
            square_half(1, 1)
            root_tile(1)

        @block.vector
        def _(dve):
            count = [0]

            def link(ins):
                count[0] += 1
                ins.then_inc(dve_done, 1)
                dve.wait_ge(dve_done, count[0])

            dve.memset(eps_col[:], EPS).then_inc(zeroed, 1)
            dve.memset(sumsq[:], 1.0).then_inc(zeroed, 1)
            dve.memset(wab[:], 0.0).then_inc(zeroed, 1)
            dve.memset(wxb[:], 0.0).then_inc(zeroed, 1)
            dve.memset(xpad[:], 0.0).then_inc(zeroed, 1)
            dve.wait_ge(zeroed, 2)
            dve.wait_ge(x_in[1], 16)
            junk = rg[:].rearrange("p b t -> p (b t)")[:, 0:D]
            dve.scalar_tensor_tensor(out=junk, in0=h[:, 1, :], scalar=1.0, in1=h[:, 1, :], op0=ALU.mult,
                                     op1=ALU.mult, accum_out=sumsq[:, 1:2]).then_inc(square_mid, 1)
            def norm_rows(tiles):
                for t in tiles:
                    rows = TILES[t][1]
                    dve.tensor_scalar(hn[0:rows, t, :], h[0:rows, t, :], rstd[0:rows, t:t + 1], None, ALU.mult
                                      ).then_inc(hn_ready, 1)

            def take_nT(stage, gain, banks):
                for k in DVE_CHUNKS[stage]:
                    dve.wait_ge(rows_turned, stage * KD + k + 1)
                    dve.tensor_scalar(nT[:, k, :], bank[banks[k]][:, 0:T], vcol(gain, k), None, ALU.mult
                                      ).then_inc(nT_dve, 1)

            dve.wait_ge(rms_ready, 1)
            dve.reciprocal(rstd[:], rms[:]).then_inc(rstd_ready, 1)
            dve.wait_ge(rstd_ready, 1)
            norm_rows((0, 2))
            dve.wait_ge(turned, 1)
            dve.tensor_copy(vecT[:], bank[1][:, 0:N_VECTOR_ROWS]).then_inc(vecT_ready, 1)
            dve.wait_ge(vecT_ready, 1)
            take_nT(0, "g_mix", TURN_BANKS[0])

            dve.wait_ge(turned, 2)
            dve.tensor_copy(pastT[:].rearrange("p b r -> p (b r)"), bank[4][:, 0:NB * 32]).then_inc(pastT_ready, 1)
            dve.wait_ge(pastT_ready, 1)
            sam = xpad[:, :, 3 + SEQ:].rearrange("p b (s k) -> p b s k", k=4)
            for blk in range(NB):
                link(dve.tensor_copy(sam[:, blk, :, 0:3],
                                     pastT[:, blk, 0:3 * NS].rearrange("p (s k) -> p s k", k=3)))

            dve.memset(vss[:], 1.0)
            dve.memset(ones_b[:], 1.0)
            dve.memset(y[:], 0.0).then_inc(y_ready, 1)
            dve.memset(head_sum[:], 0.0)
            link(dve.memset(group_sum[:], 0.0))
            dve.memset(group_sum[:, 0:1], 1.0)
            for q in range(2):
                dve.memset(head_sum[HD * q:HD * (q + 1), q:q + 1], 1.0)
            dve.memset(pos[:], -1.0)
            link(dve.memset(share[:], 0.0)) 

            L = [lamt[:, j, :] for j in range(8)]
            lam = vecT[:, VECTOR_ROWS["lam"][0]:VECTOR_ROWS["lam"][0] + NB]
            link(dve.tensor_scalar(L[0], lam, -1.0, None, ALU.mult))
            link(dve.tensor_tensor(L[1], lam, L[0], ALU.max))
            dve.tensor_scalar(L[0], L[0], 0.0, None, ALU.max).then_inc(lam_abs_ready, 1)
            for blk in range(NB):
                dve.wait_ge(z_taken, 2 * (blk + 1))
                width = SEQ + 4 * NS
                link(dve.tensor_scalar(conv[:, blk, :], xpad[:, blk, 0:width], vcol("conv_w", blk),
                                       vcol("conv_b", blk), ALU.mult, ALU.add))
                for k in range(1, TAPS - 1):
                    link(dve.scalar_tensor_tensor(out=conv[:, blk, :], in0=xpad[:, blk, k:k + width],
                                                  scalar=vcol("conv_w", k * NB + blk), in1=conv[:, blk, :],
                                                  op0=ALU.mult, op1=ALU.add))
                k = TAPS - 1
                dve.scalar_tensor_tensor(out=xc[:, blk, 0:SEQ], in0=xpad[:, blk, k:k + SEQ],
                                         scalar=vcol("conv_w", k * NB + blk), in1=conv[:, blk, 0:SEQ],
                                         op0=ALU.mult, op1=ALU.add)
                dve.scalar_tensor_tensor(out=xc[:, blk, SEQ:T], in0=sam[:, blk, :, k],
                                         scalar=vcol("conv_w", k * NB + blk),
                                         in1=conv[:, blk, SEQ:width].rearrange("p (s k) -> p s k", k=4)[:, :, k],
                                         op0=ALU.mult, op1=ALU.add).then_inc(xc_ready, 1)

            dve.wait_ge(lam_exp_ready, 1)
            link(dve.tensor_scalar(L[3], L[2], 2.0, None, ALU.add))
            link(dve.reciprocal(L[3], L[3]))
            link(dve.tensor_tensor(L[2], L[2], L[3], ALU.mult))
            link(dve.tensor_tensor(L[3], L[2], L[2], ALU.mult))
            link(dve.memset(L[4], 1.0 / 17))
            for odd in range(15, 0, -2):
                link(dve.tensor_tensor(L[4], L[4], L[3], ALU.mult))
                link(dve.tensor_scalar(L[4], L[4], 1.0 / odd, None, ALU.add))
            link(dve.tensor_tensor(L[4], L[4], L[2], ALU.mult))
            link(dve.scalar_tensor_tensor(out=L[5], in0=L[4], scalar=2.0, in1=L[0], op0=ALU.mult, op1=ALU.add))
            link(dve.tensor_scalar(L[6], L[5], LRU_C, None, ALU.mult))
            dve.tensor_scalar(L[7], L[5], -LRU_C, None, ALU.mult).then_inc(decay_ready, 1)
            dve.wait_ge(bs_in, 32)
            dve.wait_ge(consts, 1)
            for g in range(GROUPS):
                ins = dve.tensor_scalar(w00_diag[0:NS, g, :], ident[0:NS, 0:NS], w00[0:NS, g:g + 1], None, ALU.mult)
            ins.then_inc(bs_ready, 1)
            for blk in range(NB):
                dve.tensor_copy(head_back[32 * blk:32 * (blk + 1), :].rearrange("p (j d) -> p j d", j=2),
                                ident[0:32, 0:2].unsqueeze(2).to_broadcast([32, 2, HD]))
            for r in range(MAX_ROUNDS):
                for q in range(PARTS):
                    dve.tensor_copy(expert_pick[NE * q:NE * (q + 1), r * NE:(r + 1) * NE], ident[0:NE, 0:NE])
            link(dve.memset(expert_pick[0:PARTS * NE, STEPS:STEPS + 1], 0.0))

            dve.wait_ge(gates_taken, 2 * NB)
            dve.tensor_tensor(ig[:], ig[:], xc[:], ALU.mult)
            dve.wait_ge(lru_act, NB)
            a2 = conv[:, :, 0:T]
            link(dve.tensor_tensor(a2, decay[:], decay[:], ALU.mult))
            dve.wait_ge(lru_act, 2 * NB)
            dve.scalar_tensor_tensor(out=th[:], in0=a2, scalar=1.0, in1=th[:], op0=ALU.add,
                                     op1=ALU.mult).then_inc(mult2_ready, 1)
            dve.wait_ge(mult_ready, 1)
            link(dve.memset(th[:, :, 0:1], 1.0))
            link(dve.tensor_tensor(ig[:], ig[:], th[:], ALU.mult))
            for blk in range(NB):
                dve.tensor_tensor_scan(rg[:, blk, 0:SEQ], decay[:, blk, 0:SEQ], ig[:, blk, 0:SEQ], 0.0,
                                       ALU.mult, ALU.add)
            link(dve.tensor_tensor(rg[:, :, SEQ:T], decay[:, :, SEQ:T], pastT[:, :, 3 * NS:4 * NS], ALU.mult))
            link(dve.tensor_tensor(rg[:, :, SEQ:T], rg[:, :, SEQ:T], ig[:, :, SEQ:T], ALU.add))

            for t, rows in TILES:
                dve.wait_ge(vsq_ready, t + 1)
                dve.tensor_reduce(vss[0:rows, t, :], vt[0:rows, t, :].rearrange("p (g d) -> p g d", g=GROUPS),
                                  AX.X, ALU.add).then_inc(vss_ready, 1)
            dve.tensor_copy(news[:, :, 0:3], xpad[:, :, SEQ:SEQ + 3])
            for blk in range(NB):
                dve.tensor_copy(news[:, blk, 3:3 + 3 * NS].rearrange("p (s k) -> p s k", k=3), sam[:, blk, :, 1:4])
            dve.tensor_copy(news[:, :, 3 + 3 * NS:4 + 4 * NS], rg[:, :, SEQ - 1:T]).then_inc(news_ready, 1)
            dve.wait_ge(vrms_ready, 1)
            dve.wait_ge(gv_in, 16)
            link(dve.reciprocal(vss[:], vss[:]))
            for t, rows in TILES:
                for g in range(GROUPS):
                    cols = slice(g * P, (g + 1) * P)
                    ins = dve.scalar_tensor_tensor(out=vt[0:rows, t, cols], in0=bank[4 + t][0:rows, cols],
                                                   scalar=vss[0:rows, t, g:g + 1], in1=gv[0:rows, cols],
                                                   op0=ALU.mult, op1=ALU.mult)
                ins.then_inc(vt_ready, 1)

            dve.wait_ge(z_taken, 2 * 3 * NB)
            link(dve.tensor_tensor(yb[:], rg[:], yb[:], ALU.mult))
            dve.tensor_tensor(ig[:], yb[:], yb[:], ALU.mult).then_inc(ybsq_ready, 1)
            dve.wait_ge(ybrms_ready, 1)
            dve.reciprocal(sums[:], sums[:]).then_inc(ybrstd_ready, 1)
            for blk in range(NB):
                dve.wait_ge(ybrstd_made, blk + 1)
                dve.scalar_tensor_tensor(out=yb[:, blk, :], in0=yb[:, blk, :], scalar=vcol("g_ob", blk),
                                         in1=bank[4 + blk][:, 0:T], op0=ALU.mult, op1=ALU.mult).then_inc(yb_ready, 1)

            for g in range(GROUPS):
                dve.wait_ge(s_made, g + 1)
                dve.wait_ge(z_taken, 2 * (3 * NB + g + 1))
                dve.scalar_tensor_tensor(out=ya[:, g, SEQ:T], in0=bank[4 + g][:, SEQ:T], scalar=bs_wide[:, g, 0:1],
                                         in1=ug[:, g, SEQ:T], op0=ALU.add, op1=ALU.mult)
                link(dve.tensor_tensor(ya[:, g, 0:SEQ].rearrange("p (c t) -> p c t", c=2),
                                       bank[4 + g][:, 0:SEQ].rearrange("p (c t) -> p c t", c=2),
                                       bs_wide[:, g, :].unsqueeze(1).to_broadcast([P, 2, P]), ALU.add))
                link(dve.tensor_tensor(ya[:, g, 0:SEQ], ya[:, g, 0:SEQ], ug[:, g, 0:SEQ], ALU.mult))
                dve.tensor_tensor(xc[:, g, :], ya[:, g, :], ya[:, g, :], ALU.mult).then_inc(yasq_ready, 1)
            for q in range(P // NE):
                dve.tensor_copy(fold[NE * q:NE * (q + 1), :], ident[0:NE, 0:NE])
            link(dve.memset(lg[:], 0.0))
            link(dve.memset(lg[:, :, NE:NL], 3.0e38))
            dve.wait_ge(yarms_ready, 1)
            dve.reciprocal(sums[:], sums[:]).then_inc(yarstd_ready, 1)
            for g in range(GROUPS):
                dve.wait_ge(yarstd_made, g + 1)
                dve.scalar_tensor_tensor(out=ya[:, g, :], in0=ya[:, g, :], scalar=vcol("g_oa", g),
                                         in1=bank[4 + g][:, 0:T], op0=ALU.mult, op1=ALU.mult).then_inc(ya_ready, 1)

            dve.memset(xs_parts[:], 0.0).then_inc(moe_zeroed, 1)
            dve.memset(wpick[:], 0.0)

            for i, t in enumerate(MIX_ORDER):
                if i == 2:
                    dve.wait_ge(rms_ready, 2)
                    link(dve.reciprocal(rstd[:, 0:NT:2], rms[:, 0:NT:2]))
                    dve.wait_ge(b1_ready, 1)
                    norm_rows((0, 2))
                dve.wait_ge(mixed_made, i + 1)
                if t < 2:
                    for m in range(2):
                        ins = dve.tensor_tensor(h[:, t, halves(m)], bank[MIX_BANKS[t] + m][:], h[:, t, halves(m)],
                                                ALU.add)
                else:
                    for q in range(2):
                        for m in range(2):
                            r0 = 32 * (2 * q + m)
                            ins = dve.tensor_tensor(h[0:NS, 2, halves(m)], bank[MIX_BANKS[t]][r0:r0 + NS, :],
                                                    h[0:NS, 2, halves(m)], ALU.add)
                            if q == 0:
                                link(ins)
                ins.then_inc(h_added, 1)

            take_nT(1, "g_ffn", TURN_BANKS[1])
            dve.wait_ge(rms_ready, 3)
            link(dve.reciprocal(rstd[:, 1:2], rms[:, 1:2]))
            norm_rows((1,))
            dve.wait_ge(logits_made, 1)
            dve.tensor_copy(partial[:], bank[5][:, 0:T]).then_inc(logits_taken, 1)
            dve.wait_ge(xs_h, 1)
            dve.tensor_tensor(hn[0:NS, 2, :], hn[0:NS, 2, :], xs_parts[0:NS, :], ALU.subtract
                              ).then_inc(xs_low_ready, 1)
            dve.wait_ge(logits_made, 2)
            dve.wait_ge(router_in, 32)
            for t, rows in TILES:
                ins = dve.scalar_tensor_tensor(out=lg[0:rows, t, 0:NE], in0=bank[6][0:rows, t * NE:(t + 1) * NE],
                                               scalar=rstd[0:rows, t:t + 1], in1=br_row[0:rows, :], op0=ALU.mult,
                                               op1=ALU.add)
            link(ins)
            for t in range(NT):
                link(dve.max(top[:, t, :], lg[:, t, :]))
            dve.tensor_scalar(negmax[:], top[:, :, TOP_K], -1.0, None, ALU.mult).then_inc(negmax_ready, 1)
            for t in range(NT):
                link(dve.match_replace(left[:, t, :], top[:, t, :], lg[:, t, :], -3.0e38))
            link(dve.tensor_tensor(picked[:], left[:, :, 0:NE], lg[:, :, 0:NE], ALU.is_lt))
            dve.tensor_copy(picked_b[:], picked[:]).then_inc(picked_ready, 1)
            dve.wait_ge(ex_ready, NT)
            link(dve.tensor_tensor(cw[:], ex[:], picked[:], ALU.mult))
            link(dve.tensor_reduce(exsum[:], cw[:], AX.X, ALU.add))
            link(dve.reciprocal(exsum[:], exsum[:]))
            for t in range(NT):
                ins = dve.tensor_scalar(cw[:, t, :], cw[:, t, :], exsum[:, t:t + 1], None, ALU.mult)
            link(ins)
            dve.wait_ge(places_made, 1)
            dve.tensor_copy(slot1[:, 0:2, :], bank[2][:, 0:2 * NE].rearrange("p (t e) -> p t e", t=2))
            link(dve.tensor_copy(slot1[0:NS, 2, :], bank[2][0:NS, 2 * NE:3 * NE]))
            for rows, tt in ((P, slice(0, 2)), (NS, slice(2, 3))):
                link(dve.scalar_tensor_tensor(out=slot1[0:rows, tt, :], in0=slot1[0:rows, tt, :], scalar=1.0,
                                              in1=picked[0:rows, tt, :], op0=ALU.add, op1=ALU.mult))

            def make_places(r):
                cols = slice(r * NE, (r + 1) * NE)
                shift = -1.0 - CAP * r
                for q in range(PARTS):
                    dve.tensor_scalar(pos[32 * q:32 * q + NS, 2, cols], slot1[0:NS, 2, :], shift, None, ALU.add)
                dve.tensor_copy(share[:, 0:2, cols], cw[:, 0:2, :])
                dve.tensor_copy(share[0:NS, 2, cols], cw[0:NS, 2, :])
                link(dve.tensor_scalar(pos[:, 0:2, cols], slot1[:, 0:2, :], shift, None, ALU.add))

            def make_pick(step):
                for t, rows in ((0, P), (1, P), (2, PARTS * 32)):
                    ins = dve.tensor_scalar(pick[0:rows, t, :], slot_no[0:rows, 0:CAP],
                                            pos[0:rows, t, bass.ds(step, 1)], None, ALU.is_equal)
                ins.then_inc(pick_ready, 1)

            def make_b1_pick(step):
                dve.tensor_scalar(b1_pick[0:PARTS * NE, :], ones_b[0:PARTS * NE, 0:CAP],
                                  expert_pick[0:PARTS * NE, bass.ds(step, 1)], None, ALU.mult
                                  ).then_inc(b1_pick_ready, 1)

            def make_xgT(step):
                dve.wait_ge(gathered, step + 1)
                dve.tensor_tensor(xgT[:], bank[3][:].rearrange("p (k s) -> p k s", k=KD),
                                  g_ffn_wide, ALU.mult).then_inc(xgT_ready, 1)

            g0 = VECTOR_ROWS["g_ffn"][0]
            g_ffn_wide = vecT[:, g0:g0 + KD].unsqueeze(2).to_broadcast([P, KD, CAP])
            make_places(0)
            dve.wait_ge(consts, 3)
            make_pick(0)
            make_b1_pick(0)
            dve.wait_ge(xs_h, 3)
            dve.wait_ge(xs_low_ready, 1)
            dve.tensor_tensor(xs_parts[64:64 + NS, :], hn[0:NS, 2, :], xs_mid[:], ALU.subtract
                              ).then_inc(xs_low_ready, 1)
            for m in range(2):
                ins = dve.tensor_copy(wpick[:, :, CAP * m:CAP * m + NE], cw[:])
            ins.then_inc(wpick_ready, 1)
            link(dve.tensor_reduce(rounds[:, 0:1], bank[2][:, 3 * NE:4 * NE], AX.X, ALU.max))
            for r in range(1, MAX_ROUNDS):
                dve.memset(rounds[:, r:r + 1], float(CAP * r))
            link(dve.memset(rounds[:, 6:7], 0.0))
            link(dve.tensor_scalar(rounds[:, 1:MAX_ROUNDS], rounds[:, 1:MAX_ROUNDS], rounds[:, 0:1], None, ALU.is_lt))
            link(dve.tensor_reduce(rounds[:, 6:7], rounds[:, 1:MAX_ROUNDS], AX.X, ALU.add))
            dve.tensor_scalar(n_steps[:, 0:1], rounds[:, 6:7], float(NE), float(NE), ALU.mult, ALU.add)
            dve.tensor_scalar(n_steps[:, 1:2], rounds[:, 6:7], float(NE), None, ALU.mult).then_inc(steps_ready, 1)
            make_xgT(0)
            for r in range(1, MAX_ROUNDS):
                make_places(r)

            def add_tile(t, rows, first_bank, products, added):
                dve.wait_ge(spread, products)
                dve.wait_ge(h_added, added)
                for m in range(2):
                    src = bank[first_bank + m]
                    dve.tensor_tensor(h[0:rows, t, halves(m)], src[0:rows, :], h[0:rows, t, halves(m)], ALU.add
                                      ).then_inc(h_added, 1)

            def add_samples(first_bank, products, added):
                dve.wait_ge(spread, products)
                dve.wait_ge(h_added, added)
                for m in range(2):
                    dve.tensor_tensor(h[0:NS, 2, halves(m)], bank[first_bank][32 * m:32 * m + NS, :],
                                      h[0:NS, 2, halves(m)], ALU.add).then_inc(h_added, 1)

            def turned_to_nT(stage):
                g1 = VECTOR_ROWS["g_ple"][0]
                if stage == 0:
                    dve.wait_ge(tail_turned, 1)
                    dve.tensor_tensor(nT[:, 0:4, 0:P], bank[2][:].rearrange("p (k t) -> p k t", k=4),
                                      vecT[:, g1:g1 + 4].unsqueeze(2).to_broadcast([P, 4, P]), ALU.mult
                                      ).then_inc(tail_nT_dve, 1)
                else:
                    dve.wait_ge(tail_turned, 3)
                    dve.tensor_tensor(nT[:, 0:4, P:2 * P], bank[6][:].rearrange("p (k t) -> p k t", k=4),
                                      vecT[:, g1:g1 + 4].unsqueeze(2).to_broadcast([P, 4, P]), ALU.mult
                                      ).then_inc(tail_nT_dve, 1)
                    dve.wait_ge(tail_turned, 5)
                    dve.tensor_tensor(nT[:, :, SEQ:T], bank[5][:, 0:KD * NS].rearrange("p (k t) -> p k t", k=KD),
                                      vecT[:, g1:g1 + KD].unsqueeze(2).to_broadcast([P, KD, NS]), ALU.mult
                                      ).then_inc(tail_nT_dve, 1)

            dve.wait_ge(steps_ready, 1)
            n = dve.value_load(n_steps[0:1, 0:1], min_val=NE, max_val=STEPS)
            with dve.Fori(0, n) as i:
                dve.wait_ge(gathered, i + 1)
                make_pick(i + 1)
                dve.wait_ge(slots_free, i * SLOTS + 1)
                for t, rows in TILES:
                    ins = dve.tensor_scalar(wpick[0:rows, t, :], slot_no[0:rows, :],
                                            pos[0:rows, t, bass.ds(i, 1)], share[0:rows, t, bass.ds(i, 1)],
                                            ALU.is_equal, ALU.mult)
                ins.then_inc(wpick_ready, 1)
                dve.wait_ge(gate_made, i + 1)
                dve.tensor_scalar(gmin[:], bank[0][:], LIMIT, None, ALU.min).then_inc(gmin_ready, 1)
                dve.wait_ge(slots_free, i * SLOTS + W1_SLOTS)
                dve.tensor_scalar(uclip[:], bank[1][:], LIMIT, -LIMIT, ALU.min, ALU.max).then_inc(uclip_ready, 1)
                dve.wait_ge(gmin_ready, i + 1)
                dve.wait_ge(uclip_ready, i + 1)
                dve.scalar_tensor_tensor(out=gu[:], in0=uclip[:], scalar=1.0, in1=gmin[:], op0=ALU.add,
                                         op1=ALU.mult).then_inc(gu_ready, 1)
                dve.wait_ge(sig_ready, i + 1)
                dve.wait_ge(gu_ready, i + 1)
                dve.tensor_tensor(act_sb[:], gu[:], sig[:], ALU.mult).then_inc(act_ready, 1)
                add_tile(0, P, 4, i * NT + 1, i * 2 * NT + NT)
                add_tile(1, P, 6, i * NT + 2, i * 2 * NT + NT + 2)
                make_xgT(i + 1)
                add_samples(4, i * NT + 3, i * 2 * NT + NT + 4)
                make_b1_pick(i + 1)
            add_tile(0, P, 4, n * NT + 1, n * 2 * NT + NT)
            turned_to_nT(0)
            add_tile(1, P, 6, n * NT + 2, n * 2 * NT + NT + 2)
            add_samples(4, n * NT + 3, n * 2 * NT + NT + 4)
            turned_to_nT(1)

            dve.wait_ge(rms_ready, 4)
            link(dve.reciprocal(rstd[:], rms[:]))
            dve.wait_ge(rows_in, 32)
            dve.wait_ge(pw_ready, 2 * NT)

            def bias_half(t, m, made):
                dve.wait_ge(plegate_made, made)
                dve.scalar_tensor_tensor(out=gate[:, t, halves(m)], in0=bank[GATE_BANKS[t] + m][:],
                                         scalar=rstd[:, t:t + 1], in1=bpg[:, halves(m)], op0=ALU.mult, op1=ALU.add
                                         ).then_inc(plebias_ready, 1)

            def add_half(t, m):
                dve.wait_ge(plegate_ready, 2 * t + m + 1)
                link(dve.tensor_tensor(gate[:, t, halves(m)], gate[:, t, halves(m)], pw[:, t, halves(m)], ALU.mult))
                dve.tensor_tensor(h[:, t, halves(m)], gate[:, t, halves(m)], h[:, t, halves(m)], ALU.add
                                  ).then_inc(h_final, 1)

            def finish_tile(t):
                dve.wait_ge(squares_ready, 2 * t + 2)
                dve.tensor_tensor(sumsq[:, t:t + 1], squares[:, t, 0:1], squares[:, t, 1:2], ALU.add
                                  ).then_inc(sumsq_ready, 1)
                dve.wait_ge(rms_ready, 4 + t + 1)
                link(dve.reciprocal(rstd[:, t:t + 1], rms[:, t:t + 1]))
                for m in range(2):
                    dve.scalar_tensor_tensor(out=y_out[:, t, halves(m)], in0=h[:, t, halves(m)],
                                             scalar=rstd[:, t:t + 1], in1=gfin[:, halves(m)], op0=ALU.mult,
                                             op1=ALU.mult).then_inc(y_final, 1)

            bias_half(0, 0, 1)
            bias_half(0, 1, 2)
            add_half(0, 0)
            add_half(0, 1)
            dve.wait_ge(plegate_made, 3)
            for m in range(2):
                link(dve.scalar_tensor_tensor(out=gate[0:NS, 2, halves(m)],
                                              in0=bank[GATE_BANKS[2]][32 * m:32 * m + NS, :],
                                              scalar=rstd[0:NS, 2:3], in1=bpg[0:NS, halves(m)], op0=ALU.mult,
                                              op1=ALU.add))
            for m in range(2):
                ins = dve.scalar_tensor_tensor(out=gate[0:NS, 2, halves(m)],
                                               in0=bank[GATE_BANKS[2]][64 + 32 * m:64 + 32 * m + NS, :],
                                               scalar=rstd[0:NS, 2:3], in1=gate[0:NS, 2, halves(m)], op0=ALU.mult,
                                               op1=ALU.add)
            ins.then_inc(sample_bias, 1)
            dve.wait_ge(sample_gate, 1)
            link(dve.tensor_tensor(gate[0:NS, 2, :], gate[0:NS, 2, :], pw[0:NS, 2, :], ALU.mult))
            dve.tensor_tensor(h[0:NS, 2, :], gate[0:NS, 2, :], h[0:NS, 2, :], ALU.add).then_inc(sample_h, 1)
            finish_tile(0)
            bias_half(1, 0, 4)
            dve.wait_ge(sample_rms, 1)
            link(dve.reciprocal(rstd[0:NS, 2:3], rms[0:NS, 2:3]))
            dve.scalar_tensor_tensor(out=y_out[0:NS, 2, :], in0=h[0:NS, 2, :], scalar=rstd[0:NS, 2:3],
                                     in1=gfin[0:NS, :], op0=ALU.mult, op1=ALU.mult).then_inc(sample_final, 1)
            add_half(1, 0)
            bias_half(1, 1, 5)
            add_half(1, 1)
            finish_tile(1)

        @block.tensor
        def _(pe):
            def turn(src, stage, k, tiles):
                for t in tiles:
                    rows = TILES[t][1]
                    ins = pe.transpose(bank[TURN_BANKS[stage][k]][:, t * P:t * P + rows],
                                       src[0:rows, t, k * P:(k + 1) * P], ident[0:rows, 0:rows])
                return ins

            def wait_nT(stage, k):
                if k in ACT_CHUNKS[stage]:
                    pe.wait_ge(nT_act, len(ACT_CHUNKS[0]) * stage + ACT_CHUNKS[stage].index(k) + 1)
                else:
                    pe.wait_ge(nT_dve, len(DVE_CHUNKS[0]) * stage + DVE_CHUNKS[stage].index(k) + 1)

            pe.wait_ge(consts, 1)
            for _ in range(WARM_UP):
                pe.matmul(bank[1][:, 0:P], ident[:], ident[:], start=True, stop=True)
            pe.wait_ge(hn_ready, 2)
            for k in range(4):
                turn(hn, 0, k, (0, 2))
            pe.wait_ge(vec_in, 16 * len(VECTOR_ROWS))
            pe.transpose(bank[1][:, 0:N_VECTOR_ROWS], vrows[:], ident[0:N_VECTOR_ROWS, 0:N_VECTOR_ROWS]
                         ).then_inc(turned, 1)
            pe.wait_ge(hn_act, 1)
            for k in range(KD):
                if TURN_BANKS[0][k] == 1:
                    pe.wait_ge(vecT_ready, 1)
                turn(hn, 0, k, (1,) if k < 4 else range(NT)).then_inc(rows_turned, 1)
            def project(b):
                g, blk = b // NB, b % NB
                if b >= 4:
                    pe.wait_ge(z_taken, 2 * (b - 3))
                if b < 4:
                    wait_nT(0, TURN_BANKS[0].index(b))
                for k in range(KD):
                    if blk == 0 and k % (KD // 2) == 0 and k // (KD // 2) < len(win_in[g]):
                        pe.wait_ge(win_in[g][k // (KD // 2)], 16)
                    wait_nT(0, k)
                    ins = pe.matmul(bank[b % 4][:, 0:T], w_in[g][:, k, blk * P:(blk + 1) * P], nT[:, k, :],
                                    start=(k == 0), stop=(k == KD - 1))
                ins.then_inc(z_made, 1)

            def gates(w, first):
                if first == 0:
                    pe.wait_ge(pastT_ready, 1)
                for blk in range(NB):
                    pe.wait_ge(xc_ready, blk + 1)
                    if first:
                        pe.wait_ge(gates_taken, blk + 1)
                    elif blk == NB - 1:
                        pe.wait_ge(wsT_ready, 1)
                    pe.matmul(bank[4 + blk][:, 0:T], w[:, blk, :], xc[:, blk, :], start=True, stop=True
                              ).then_inc(gates_made, 1)

            project(0)
            pe.wait_ge(past_in, 32)
            wait_nT(0, TURN_BANKS[0].index(4))
            for blk in range(NB):
                ins = pe.transpose(bank[4][:, blk * 32:(blk + 1) * 32], past[:, blk * P:(blk + 1) * P],
                                   ident[0:32, 0:32])
            ins.then_inc(turned, 1)
            for b in range(1, NB):
                project(b)
            pe.wait_ge(consts, 3 + GROUPS)
            for g in range(GROUPS):
                ins = pe.transpose(bank[7][:, g * P:(g + 1) * P], ws[:, g, :], ident[:])
            ins.then_inc(turned, 1)
            project(NB)
            project(NB + 1)
            pe.wait_ge(gates_in, 64)
            gates(wab, 0)
            project(NB + 2)
            project(NB + 3)
            gates(wxb, NB)
            project(2 * NB)
            pe.wait_ge(z_taken, 2 * 2 * NB)
            pe.wait_ge(gates_taken, 2 * NB)
            for t, rows in TILES:
                for g in range(GROUPS):
                    ins = pe.transpose(bank[4 + t][0:rows, g * P:(g + 1) * P], ya[:, g, t * P:t * P + rows], ident[:])
                ins.then_inc(v_turned, 1)
            project(2 * NB + 1)
            project(2 * NB + 2)
            project(2 * NB + 3)
            pe.wait_ge(news_ready, 1)
            for blk in range(NB):
                ins = pe.transpose(bank[7][0:36, blk * P:(blk + 1) * P], news[:, blk, :], ident[:])
            ins.then_inc(news_turned, 1)
            project(3 * NB)
            project(3 * NB + 1)
            pe.wait_ge(ybsq_ready, 1)
            pe.wait_ge(news_taken, 1)
            for blk in range(NB):
                ins = pe.matmul(bank[7][32 * blk:32 * (blk + 1), 0:T], head_sum[:], ig[:, blk, :], start=True,
                                stop=True, skip_group_check=True)
            ins.then_inc(ybss_made, 1)
            project(3 * NB + 2)
            pe.wait_ge(ybrstd_ready, 1)
            pe.wait_ge(vt_ready, NT)
            for blk in range(NB):
                r = slice(32 * blk, 32 * (blk + 1))
                pe.matmul(bank[4 + blk][:, 0:T], head_back[r, :], sums[r, :], start=True,
                          stop=True).then_inc(ybrstd_made, 1)
            project(3 * NB + 3)
            pe.wait_ge(bs_ready, 1)
            for g in range(GROUPS):
                cols = slice(g * P, (g + 1) * P)
                s = bank[4 + g]
                pe.wait_ge(yb_ready, g + 1)
                for t in range(2):
                    pe.matmul(s[:, t * P:(t + 1) * P], vt[:, t, cols], wsT[:, g, :], start=True, stop=True,
                              skip_group_check=True)
                pe.matmul(s[:, SEQ:T], vt[0:NS, 2, cols], w00_diag[0:NS, g, :], start=True, stop=True,
                          skip_group_check=True).then_inc(s_made, 1)

            def mixed(t, k, first, last):
                src = ya[:, k, :] if k < NB else yb[:, k - NB, :]
                for m in range(2):
                    ins = pe.matmul(bank[MIX_BANKS[t] + m][:], src[:, t * P:(t + 1) * P], w_out[:, k, halves(m)],
                                    start=first, stop=last)
                return ins

            def small_tile(dst, lhs, w, chunks, start=True, stop=True):
                half = len(chunks) // 2
                for c in range(half):
                    for q in range(2):
                        for m in range(2):
                            k = chunks[q * half + c]
                            r0 = 32 * (2 * q + m)
                            ins = pe.matmul(dst[r0:r0 + NS, :], lhs(k), w[:, k, halves(m)], start=start and c == 0,
                                            stop=stop and c == half - 1, skip_group_check=True)
                return ins

            def mixed_samples(k):
                return (ya[:, k, :] if k < NB else yb[:, k - NB, :])[:, SEQ:T]

            pe.wait_ge(wout_in, 16)
            pe.wait_ge(z_taken, 2 * (3 * NB + 2))
            mixed(0, NB, True, False)
            mixed(0, NB + 1, False, False)
            pe.wait_ge(yasq_ready, GROUPS)
            for g in range(GROUPS):
                ins = pe.matmul(bank[4][32 * g:32 * (g + 1), 0:T], group_sum[:], xc[:, g, :], start=True, stop=True,
                                skip_group_check=True)
            ins.then_inc(yass_made, 1)
            mixed(0, NB + 2, False, False)
            mixed(0, NB + 3, False, False)
            pe.wait_ge(yarstd_ready, 1)
            for g in range(GROUPS):
                r = slice(32 * g, 32 * (g + 1))
                pe.matmul(bank[4 + g][:, 0:T], ident[r, 32 * g:32 * g + 1].to_broadcast([32, P]), sums[r, :],
                          start=True, stop=True).then_inc(yarstd_made, 1)
            pe.wait_ge(z_taken, 8 * NB)
            pe.wait_ge(p_in, 32)
            for k in range(PLE // P):
                for t, rows in TILES:
                    ins = pe.transpose(bank[2 + k][:, t * P:t * P + rows], p_rows[0:rows, t, k * P:(k + 1) * P],
                                       ident[0:rows, 0:rows])
                ins.then_inc(p_turned, 1)
            for g in range(2):
                pe.wait_ge(ya_ready, g + 1)
                mixed(0, g, False, False)
            pe.wait_ge(pT_ready, PLE // P)
            for blk in range(NB):
                mixed(1, NB + blk, blk == 0, False)
            small_tile(bank[MIX_BANKS[2]], mixed_samples, w_out, range(NB, KD), stop=False).then_inc(wout_late, 1)
            for g in range(2, GROUPS):
                pe.wait_ge(ya_ready, g + 1)
                ins = mixed(0, g, False, g == GROUPS - 1)
            ins.then_inc(mixed_made, 1)
            small_tile(bank[MIX_BANKS[2]], mixed_samples, w_out, range(NB), start=False).then_inc(mixed_made, 1)
            for g in range(GROUPS):
                ins = mixed(1, g, False, g == GROUPS - 1)
            ins.then_inc(mixed_made, 1)

            pe.wait_ge(h_added, 2)
            for k in range(6):
                turn(h, 1, k, MIX_ORDER[:2])
            pe.wait_ge(h_added, NT)
            for k in range(KD):
                turn(h, 1, k, MIX_ORDER[2:] if k < 6 else MIX_ORDER).then_inc(rows_turned, 1)
            pe.wait_ge(router_in, 32)
            wait_nT(1, TURN_BANKS[1].index(5))
            for k in range(KD):
                wait_nT(1, k)
                q = k % 4
                ins = pe.matmul(bank[5][NE * q:NE * (q + 1), 0:T], wr[:, k, :], nT[:, k, :], start=(k < 4),
                                stop=(k >= 4), skip_group_check=True)
            ins.then_inc(logits_made, 1)
            pe.wait_ge(wpp_in, 16)
            wait_nT(1, TURN_BANKS[1].index(1))
            for k in range(PLE // P):
                for m in range(2):
                    ins = pe.matmul(bank[EMBED_BANKS[2][m]][32 * m:32 * m + NS, :], pT[:, k, SEQ:T],
                                    w_pp[:, k, halves(m)], start=(k == 0), stop=(k == PLE // P - 1), skip_group_check=True)
            ins.then_inc(pw_made, 1)
            pe.wait_ge(logits_taken, 1)
            wait_nT(1, TURN_BANKS[1].index(6))
            for t, rows in TILES:
                ins = pe.matmul(bank[6][0:rows, t * NE:(t + 1) * NE], partial[:, t * P:t * P + rows], fold[:],
                                start=True, stop=True, skip_group_check=True)
            ins.then_inc(logits_made, 1)

            def embed(t):
                for k in range(PLE // P):
                    for m in range(2):
                        ins = pe.matmul(bank[EMBED_BANKS[t][m]][:], pT[:, k, t * P:(t + 1) * P], w_pp[:, k, halves(m)],
                                        start=(k == 0), stop=(k == PLE // P - 1))
                ins.then_inc(pw_made, 1)

            wait_nT(1, KD - 1)
            wait_nT(1, KD - 2)
            embed(0)
            pe.wait_ge(picked_ready, 1)
            pe.wait_ge(consts, 2)
            for t, rows in TILES:
                for s in range(t + 1):
                    rows_s = TILES[s][1]
                    lhs = before_b if s == t else ones_b
                    pe.matmul(bank[2][0:rows, t * NE:(t + 1) * NE], lhs[0:rows_s, 0:rows], picked_b[0:rows_s, s, :],
                              start=(s == 0), stop=(s == t), skip_group_check=True)
            for s, rows_s in TILES:
                ins = pe.matmul(bank[2][:, 3 * NE:4 * NE], ones_b[0:rows_s, :], picked_b[0:rows_s, s, :],
                                start=(s == 0), stop=(s == NT - 1), skip_group_check=True)
            ins.then_inc(places_made, 1)
            embed(1)

            def gather(step, added=None):
                pe.wait_ge(pick_ready, step + 1)
                for k in range(KD):
                    cols = slice(k * P, (k + 1) * P)
                    dst = bank[3][:, k * CAP:(k + 1) * CAP]
                    for t in range(2):
                        for q in range(PARTS):
                            pe.matmul(dst, x_parts[:, q, t, cols], pick[:, t, :], start=(t == 0 and q == 0),
                                      stop=False, skip_group_check=True)
                    if k == KD - 1 and added is not None:
                        pe.wait_ge(h_added, added)
                    ins = pe.matmul(dst, xs_parts[0:32 * PARTS, cols], pick[0:32 * PARTS, 2, :], start=False,
                                    stop=True, skip_group_check=True)
                ins.then_inc(gathered, 1)

            def scatter(t, rows, first_bank):
                for m in range(2):
                    r = slice(CAP * m, CAP * (m + 1))
                    ins = pe.matmul(bank[first_bank + m][0:rows, :], wpickT[r, t * P:t * P + rows], y[r, :],
                                    start=True, stop=True)
                ins.then_inc(spread, 1)

            def scatter_samples(first_bank):
                for m in range(2):
                    r = slice(CAP * m, CAP * (m + 1))
                    ins = pe.matmul(bank[first_bank][32 * m:32 * m + NS, :], wpickT[r, SEQ:T], y[r, :],
                                    start=True, stop=True)
                ins.then_inc(spread, 1)

            pe.wait_ge(parts_ready, 2)
            pe.wait_ge(parts_h, 4)
            pe.wait_ge(xs_h, 3)
            pe.wait_ge(xs_low_ready, 2)
            gather(0)
            pe.wait_ge(wpick_ready, 1)
            for t, rows in TILES:
                ins = pe.transpose(bank[5][:, t * P:t * P + rows], wpick[0:rows, t, :], ident[0:rows, 0:rows])
            ins.then_inc(wpick_turned, 1)
            pe.wait_ge(steps_ready, 1)
            n = pe.value_load(n_steps[0:1, 0:1], min_val=NE, max_val=STEPS)
            pe.wait_ge(pw_ready, 2 * 2)
            pe.wait_ge(b2_in, 32)
            def step(i, early=0, skipped=0):
                pe.wait_ge(b1_pick_ready, i + 1)
                pe.wait_ge(wpickT_ready, i + 1)
                for part in range(2):
                    for m in range(2):
                        r = slice(CAP * m, CAP * (m + 1))
                        c = part * FF + m * HALF
                        pe.matmul(bank[part][r, :], b1_pick[0:PARTS * NE, :], b1_parts[0:PARTS * NE, c:c + HALF],
                                  start=True, stop=False, skip_group_check=True)
                pe.wait_ge(xgT_ready, i + 1)
                for k in range(W1_SLOTS):
                    if k < early:
                        pe.wait_ge(early_in[k], 16)
                        w = early_w1[k]
                    else:
                        pe.wait_ge(slot_in[k], (i + 1 - (skipped if k < EARLY else 0)) * 16)
                        w = ring[:, k, :]
                    for part in range(2):
                        for m in range(2):
                            r = slice(CAP * m, CAP * (m + 1))
                            c = part * FF + m * HALF
                            ins = pe.matmul(bank[part][r, :], xgT[:, k, :], w[:, c:c + HALF],
                                            start=False, stop=(k == W1_SLOTS - 1), skip_group_check=True)
                        if part == 0 and k == W1_SLOTS - 1:
                            ins.then_inc(gate_made, 1)
                    ins.then_inc(slots_free, 1)
                pe.wait_ge(pw_ready, 2 * NT)
                pe.wait_ge(y_ready, i + 1)
                pe.wait_ge(h_added, i * 2 * NT + NT)
                scatter(0, P, 4)
                scatter(1, P, 6)
                gather(i + 1, i * 2 * NT + NT + 2)
                scatter_samples(4)
                pe.wait_ge(act_ready, i + 1)
                pe.wait_ge(xgT_ready, i + 2)
                for c in range(HALF // P):
                    ins = pe.transpose(bank[3][:, c * P:(c + 1) * P], act_sb[:, c * P:(c + 1) * P], ident[:])
                ins.then_inc(act_turned, 1)
                pe.wait_ge(wpick_ready, i + 2)
                pe.wait_ge(gmin_ready, i + 1)
                for t, rows in TILES:
                    ins = pe.transpose(bank[0][:, t * P:t * P + rows], wpick[0:rows, t, :], ident[0:rows, 0:rows])
                ins.then_inc(wpick_turned, 1)
                pe.wait_ge(actT_ready, i + 1)
                for j in range(W2_SLOTS):
                    pe.wait_ge(slot_in[W1_SLOTS + j], (i + 1) * 16)
                    for q in range(2):
                        f = 2 * j + q
                        half = (f % 4) * P + (f // 4) * CAP
                        for m in range(2):
                            c = q * D + m * HALF
                            ins = pe.matmul(bank[2][CAP * m:CAP * (m + 1), :], actT[:, half:half + CAP],
                                            ring[:, W1_SLOTS + j, c:c + HALF], start=(f == 0),
                                            stop=(f == FF // P - 1), skip_group_check=True)
                    ins.then_inc(slots_free, 1)

            step(0)
            step(1, EARLY)
            with pe.Fori(2, n) as i:
                step(i, 0, 1)
            pe.wait_ge(y_ready, n + 1)
            pe.wait_ge(wpickT_ready, n + 1)
            pe.wait_ge(h_added, n * 2 * NT + NT)
            scatter(0, P, 4)
            scatter(1, P, 6)

            def turn_four(t, half, dst):
                for c in range(4):
                    k = 4 * half + c
                    ins = pe.transpose(dst[:, c * P:(c + 1) * P], h[:, t, k * P:(k + 1) * P], ident[:])
                ins.then_inc(tail_turned, 1)

            pe.wait_ge(h_added, n * 2 * NT + NT + 2)
            turn_four(0, 0, bank[2])
            turn_four(0, 1, bank[3])
            scatter_samples(4)
            pe.wait_ge(tail_nT_dve, 1)
            for k in range(KD):
                pe.wait_ge(wpg_in[k // 2], 16)
                if k == 1:
                    pe.wait_ge(h_added, n * 2 * NT + NT + 4)
                    turn_four(1, 0, bank[6])
                    turn_four(1, 1, bank[7])
                elif k == 3:
                    pe.wait_ge(h_added, (n + 1) * 2 * NT + NT)
                elif k == 4:
                    for c in range(KD):
                        ins = pe.transpose(bank[5][:, c * NS:(c + 1) * NS], h[0:NS, 2, c * P:(c + 1) * P],
                                           ident[0:NS, 0:NS])
                    ins.then_inc(tail_turned, 1)
                    pe.wait_ge(tail_nT_act, 4)
                for m in range(2):
                    ins = pe.matmul(bank[GATE_BANKS[0] + m][:], nT[:, k, 0:P], w_pg[:, k, halves(m)],
                                    start=(k == 0), stop=(k == KD - 1))
                    if k == KD - 1:
                        ins.then_inc(plegate_made, 1)
            pe.wait_ge(tail_nT_dve, 3)
            pe.wait_ge(tail_nT_act, 2 * 4)
            small_tile(bank[GATE_BANKS[2]], lambda k: nT[:, k, SEQ:T], w_pg, range(KD)).then_inc(plegate_made, 1)
            for m in range(2):
                for k in range(KD):
                    ins = pe.matmul(bank[GATE_BANKS[1] + m][:], nT[:, k, P:2 * P], w_pg[:, k, halves(m)],
                                    start=(k == 0), stop=(k == KD - 1))
                ins.then_inc(plegate_made, 1)


_INS = ["x_prompt", "x_sample", "state_conv", "state_lru", "p_prompt", "p_sample", "g_mix", "w_in", "g_v", "w_s",
        "b_s", "conv_w", "conv_b", "w_a", "b_a", "w_x", "b_x", "lam", "g_oa", "g_ob", "w_out", "g_ffn", "w_r",
        "b_r", "w1", "b1", "w2", "b2", "g_ple", "w_pg", "b_pg", "w_pp", "g_final"]


def kernel(**inputs):
    import numpy as np
    import concourse.bacc as bacc
    from concourse.bass_utils import run_bass_kernel_spmd

    nc = bacc.Bacc("TRN2", target_bir_lowering=False, num_devices=1)
    arrays, ins, outs = {}, {}, {}
    for name in _INS:
        x = np.ascontiguousarray(inputs[name])
        arrays[f"in_{name}"] = x
        ins[name] = nc.dram_tensor(f"in_{name}", x.shape, mybir.dt.from_np(x.dtype), kind="ExternalInput").ap()
    depth, samples, past, lru = inputs["state_conv"].shape
    chunk = inputs["w_s"].shape[2]
    gmlp = inputs["g_v"].shape[1]
    prompts = inputs["x_prompt"].shape[0]
    shapes = {
        "y_prompt": inputs["x_prompt"].shape,
        "y_sample": inputs["x_sample"].shape,
        "v_prompt": (depth, prompts, chunk, gmlp),
        "conv_prompt": (depth, prompts, past, lru),
        "lru_prompt": (depth, prompts, lru),
        "v_sample": (depth, samples, 1, gmlp),
        "conv_sample": (depth, samples, past, lru),
        "lru_sample": (depth, samples, lru),
    }
    for name, shape in shapes.items():
        outs[name] = nc.dram_tensor(f"out_{name}", shape, F32, kind="ExternalOutput").ap()
    decode_step(nc, ins, outs)
    r = run_bass_kernel_spmd(nc, [arrays], core_ids=[0])
    return tuple(r.results[0][f"out_{name}"] for name in shapes)
```
